# Optimizing a Trainium2 kernel written in Bass

```python
import math
import jax
import jax.numpy as jnp
from jax import lax
import numpy as np
import jax, jax.numpy as jnp

D_MODEL = 1024
BATCH = 1
SEQ = 512
DEPTH = 2

NORM_EPS = 1e-6
D_FF = 2816
FFN_RES_SCALE = 0.5

A_HEADS = 8
A_HEAD_DIM = 64
A_PATTERNS = ((128, 1), (512, 4), (2048, 16))
A_BLOCK = 128

B_HEADS = 4
B_HEAD_DIM = 128
B_CONV = 4
B_CHUNK = 64

C_D_INNER = 2 * D_MODEL
C_HEAD_DIM = 64
C_HEADS = C_D_INNER // C_HEAD_DIM
C_GROUPS = 4
C_STATE = 128
C_CONV = 4
C_CHUNK = 64

A_WIDTH = A_HEADS * A_HEAD_DIM
B_WIDTH = B_HEADS * B_HEAD_DIM
EVEN_IN = 3 * A_WIDTH + 4 * B_WIDTH + 2 * B_HEADS
C_XBC = C_D_INNER + 2 * C_GROUPS * C_STATE
ODD_IN = C_D_INNER + C_XBC + C_HEADS
N_EVEN = (DEPTH + 1) // 2
N_ODD = DEPTH // 2


def rmsnorm(x, w):
    xf = x.astype(jnp.float32)
    y = xf * lax.rsqrt(jnp.mean(xf * xf, axis=-1, keepdims=True) + NORM_EPS)
    return (y * w.astype(jnp.float32)).astype(x.dtype)

def l2norm(x):
    return x * lax.rsqrt(jnp.sum(x * x, axis=-1, keepdims=True) + NORM_EPS)

def swiglu(x, w_gate, w_up, w_down):
    return (jax.nn.silu(x @ w_gate) * (x @ w_up)) @ w_down

def causal_dwconv(x, w):
    k_len, ch = w.shape
    return lax.conv_general_dilated(x, w[:, None, :].astype(x.dtype), window_strides=(1,),
                                    padding=((k_len - 1, 0),), dimension_numbers=('NWC', 'WIO', 'NWC'),
                                    feature_group_count=ch)

def dilated_window_attention(q, k, v):
    bsz, seq, heads, dh = q.shape
    scale = dh ** -0.5
    nums, maxes, dens = [], [], []
    for window, dil in A_PATTERNS:
        span = window // dil
        length = seq // dil
        blk = math.gcd(length, A_BLOCK)
        nb = length // blk

        def by_residue(t):
            return t.reshape(bsz, length, dil, heads, dh).transpose(0, 2, 1, 3, 4)

        pad = ((0, 0), (0, 0), (span, 0), (0, 0), (0, 0))
        kp = jnp.pad(by_residue(k), pad)
        vp = jnp.pad(by_residue(v), pad)
        idx = jnp.arange(nb)[:, None] * blk + jnp.arange(blk + span)[None, :]
        kb = kp[:, :, idx]
        vb = vp[:, :, idx]
        qb = by_residue(q).reshape(bsz, dil, nb, blk, heads, dh)
        s = jnp.einsum('brnqhd,brnkhd->brnhqk', qb, kb) * scale
        dist = jnp.arange(blk)[:, None] + span - jnp.arange(blk + span)[None, :]
        valid = ((dist >= 0) & (dist <= span))[None] & (idx >= span)[:, None, :]
        s = jnp.where(valid[:, None], s, -jnp.inf)
        m = jnp.max(s, axis=-1, keepdims=True)
        p = jnp.exp(s - m)
        den = jnp.sum(p, axis=-1)
        num = jnp.einsum('brnhqk,brnkhd->brnqhd', p, vb)

        def back(t):
            t = t.reshape(bsz, dil, length, *t.shape[4:])
            return jnp.moveaxis(t, 1, 2).reshape(bsz, seq, *t.shape[3:])

        nums.append(back(num))
        maxes.append(back(jnp.swapaxes(m[..., 0], -1, -2)))
        dens.append(back(jnp.swapaxes(den, -1, -2)))
    mx = jnp.max(jnp.stack(maxes), axis=0)
    wts = [jnp.exp(mi - mx) for mi in maxes]
    num = sum(n * w[..., None] for n, w in zip(nums, wts))
    den = sum(d * w for d, w in zip(dens, wts))
    return num / den[..., None]

def gated_delta_rule(q, k, v, g, beta):
    bsz, seq, heads, dk = q.shape
    dv = v.shape[-1]
    nc = seq // B_CHUNK

    def chunks(t):
        t = t.reshape(bsz, nc, B_CHUNK, heads, *t.shape[3:])
        return jnp.swapaxes(t, 2, 3)

    qc, kc, vc = chunks(q * dk ** -0.5), chunks(k), chunks(v)
    gc = jnp.cumsum(chunks(g), axis=-1)
    bc = chunks(beta)[..., None]
    tri = jnp.tril(jnp.ones((B_CHUNK, B_CHUNK), bool))
    strict = jnp.tril(jnp.ones((B_CHUNK, B_CHUNK), bool), -1)
    decay = jnp.exp(jnp.where(tri, gc[..., :, None] - gc[..., None, :], -jnp.inf))
    k_beta = kc * bc
    a_mat = jnp.where(strict, jnp.einsum('bnhid,bnhjd->bnhij', k_beta, kc) * decay, 0.0)
    t_mat = a_mat + jnp.eye(B_CHUNK, dtype=a_mat.dtype)
    u = lax.linalg.triangular_solve(t_mat, vc * bc, left_side=True, lower=True, unit_diagonal=True)
    w = lax.linalg.triangular_solve(t_mat, k_beta * jnp.exp(gc)[..., None], left_side=True, lower=True,
                                    unit_diagonal=True)
    qk = jnp.where(tri, jnp.einsum('bnhid,bnhjd->bnhij', qc, kc) * decay, 0.0)
    q_dec = qc * jnp.exp(gc)[..., None]
    g_last = gc[..., -1]
    k_dec = kc * jnp.exp(g_last[..., None] - gc)[..., None]

    def step(state, inp):
        u_i, w_i, q_i, qk_i, k_i, gl_i = inp
        v_new = u_i - jnp.einsum('bhck,bhkv->bhcv', w_i, state)
        o_i = jnp.einsum('bhck,bhkv->bhcv', q_i, state) + jnp.einsum('bhij,bhjv->bhiv', qk_i, v_new)
        state = state * jnp.exp(gl_i)[..., None, None] + jnp.einsum('bhck,bhcv->bhkv', k_i, v_new)
        return state, o_i

    xs = tuple(jnp.moveaxis(t, 1, 0) for t in (u, w, q_dec, qk, k_dec, g_last))
    state0 = jnp.zeros((bsz, heads, dk, dv), q.dtype)
    _, o = lax.scan(step, state0, xs)
    return jnp.transpose(o, (1, 0, 3, 2, 4)).reshape(bsz, seq, heads, dv)

def ssd_chunked_scan(x, a, b_in, c_in):
    bsz, seq, heads, p = x.shape
    groups, n = b_in.shape[2:]
    rep = heads // groups
    nc = seq // C_CHUNK
    xc = x.reshape(bsz, nc, C_CHUNK, groups, rep, p)
    acum = jnp.cumsum(a.reshape(bsz, nc, C_CHUNK, groups, rep), axis=2)
    bc = b_in.reshape(bsz, nc, C_CHUNK, groups, n)
    cc = c_in.reshape(bsz, nc, C_CHUNK, groups, n)
    tri = jnp.tril(jnp.ones((C_CHUNK, C_CHUNK), bool))[:, :, None, None]
    seg = jnp.exp(jnp.where(tri, acum[:, :, :, None] - acum[:, :, None, :], -jnp.inf))
    cb = jnp.einsum('bnlgd,bnsgd->bnlsg', cc, bc)
    y_diag = jnp.einsum('bnlsgr,bnsgrp->bnlgrp', cb[..., None] * seg, xc)

    def step(state, inp):
        x_i, a_i, b_i, c_i = inp
        y_off = jnp.einsum('blgd,bgrpd,blgr->blgrp', c_i, state, jnp.exp(a_i))
        a_last = a_i[:, -1]
        state = state * jnp.exp(a_last)[..., None, None] + jnp.einsum(
            'bsgd,bsgr,bsgrp->bgrpd', b_i, jnp.exp(a_last[:, None] - a_i), x_i)
        return state, y_off

    xs = tuple(jnp.moveaxis(t, 1, 0) for t in (xc, acum, bc, cc))
    state0 = jnp.zeros((bsz, groups, rep, p, n), x.dtype)
    _, y_off = lax.scan(step, state0, xs)
    return (y_diag + jnp.moveaxis(y_off, 0, 1)).reshape(bsz, seq, heads, p)

def even_mixer(u, w_in, conv_w, a_log, dt_bias, head_norm_w, w_out):
    bsz, seq, _ = u.shape
    proj = (u @ w_in).astype(jnp.float32)
    cuts = [int(c) for c in np.cumsum([A_WIDTH, A_WIDTH, A_WIDTH, 3 * B_WIDTH, B_WIDTH, B_HEADS])]
    qa, ka, va, qkv_b, z, beta_raw, a_raw = jnp.split(proj, cuts, axis=-1)
    qa, ka, va = (t.reshape(bsz, seq, A_HEADS, A_HEAD_DIM) for t in (qa, ka, va))
    o_a = dilated_window_attention(qa, ka, va)
    qkv_b = jax.nn.silu(causal_dwconv(qkv_b, conv_w))
    qb, kb, vb = (t.reshape(bsz, seq, B_HEADS, B_HEAD_DIM) for t in jnp.split(qkv_b, 3, axis=-1))
    beta = jax.nn.sigmoid(beta_raw)
    g = -jnp.exp(a_log) * jax.nn.softplus(a_raw + dt_bias)
    o_b = gated_delta_rule(l2norm(qb), l2norm(kb), vb, g, beta)
    o_b = rmsnorm(o_b, head_norm_w) * jax.nn.silu(z.reshape(bsz, seq, B_HEADS, B_HEAD_DIM))
    o = jnp.concatenate([o_a.reshape(bsz, seq, A_WIDTH), o_b.reshape(bsz, seq, B_WIDTH)], axis=-1)
    return (o @ w_out).astype(u.dtype)

def odd_mixer(u, w_in, conv_w, conv_b, dt_bias, a_log, d_skip, out_norm_w, w_out):
    bsz, seq, _ = u.shape
    proj = (u @ w_in).astype(jnp.float32)
    z, xbc, dt = jnp.split(proj, [C_D_INNER, C_D_INNER + C_XBC], axis=-1)
    xbc = jax.nn.silu(causal_dwconv(xbc, conv_w) + conv_b)
    xs, b_in, c_in = jnp.split(xbc, [C_D_INNER, C_D_INNER + C_GROUPS * C_STATE], axis=-1)
    xs = xs.reshape(bsz, seq, C_HEADS, C_HEAD_DIM)
    b_in = b_in.reshape(bsz, seq, C_GROUPS, C_STATE)
    c_in = c_in.reshape(bsz, seq, C_GROUPS, C_STATE)
    dt = jax.nn.softplus(dt + dt_bias)
    a = -jnp.exp(a_log) * dt
    y = ssd_chunked_scan(xs * dt[..., None], a, b_in, c_in) + d_skip[:, None] * xs
    y = y.reshape(bsz, seq, C_D_INNER) * jax.nn.silu(z)
    y = rmsnorm(y.reshape(bsz, seq, C_GROUPS, C_D_INNER // C_GROUPS), out_norm_w.reshape(C_GROUPS, -1))
    return (y.reshape(bsz, seq, C_D_INNER) @ w_out).astype(u.dtype)

def _dt_bias(key, shape):
    dt = jnp.exp(jax.random.uniform(key, shape, jnp.float32, math.log(1e-3), math.log(1e-1)))
    return dt + jnp.log(-jnp.expm1(-dt))

def first_inputs(seed: int = 0) -> dict:
    key = jax.random.key(seed)
    ks = iter(jax.random.split(key, 24))

    def nrm(shape, scale):
        return scale * jax.random.normal(next(ks), shape, jnp.float32)

    x = nrm((BATCH, SEQ, D_MODEL), 1.0)
    norm_w = 1.0 + nrm((DEPTH, 6, D_MODEL), 0.05)
    ffn_w_gate = nrm((DEPTH, 2, D_MODEL, D_FF), D_MODEL ** -0.5)
    ffn_w_up = nrm((DEPTH, 2, D_MODEL, D_FF), D_MODEL ** -0.5)
    ffn_w_down = nrm((DEPTH, 2, D_FF, D_MODEL), D_FF ** -0.5)
    even_w_in = nrm((N_EVEN, D_MODEL, EVEN_IN), D_MODEL ** -0.5)
    even_conv_w = nrm((N_EVEN, B_CONV, 3 * B_WIDTH), B_CONV ** -0.5)
    even_a_log = jnp.log(jax.random.uniform(next(ks), (N_EVEN, B_HEADS), jnp.float32, 1.0, 16.0))
    even_dt_bias = _dt_bias(next(ks), (N_EVEN, B_HEADS))
    even_head_norm_w = 1.0 + nrm((N_EVEN, B_HEAD_DIM), 0.05)
    even_w_out = nrm((N_EVEN, A_WIDTH + B_WIDTH, D_MODEL), (A_WIDTH + B_WIDTH) ** -0.5)
    odd_w_in = nrm((N_ODD, D_MODEL, ODD_IN), D_MODEL ** -0.5)
    odd_conv_w = nrm((N_ODD, C_CONV, C_XBC), C_CONV ** -0.5)
    odd_conv_b = nrm((N_ODD, C_XBC), 0.02)
    odd_dt_bias = _dt_bias(next(ks), (N_ODD, C_HEADS))
    odd_a_log = jnp.log(jax.random.uniform(next(ks), (N_ODD, C_HEADS), jnp.float32, 1.0, 16.0))
    odd_d_skip = 1.0 + nrm((N_ODD, C_HEADS), 0.05)
    odd_out_norm_w = 1.0 + nrm((N_ODD, C_D_INNER), 0.05)
    odd_w_out = nrm((N_ODD, C_D_INNER, D_MODEL), C_D_INNER ** -0.5)
    return {'x': x, 'norm_w': norm_w, 'ffn_w_gate': ffn_w_gate, 'ffn_w_up': ffn_w_up,
            'ffn_w_down': ffn_w_down, 'even_w_in': even_w_in, 'even_conv_w': even_conv_w,
            'even_a_log': even_a_log, 'even_dt_bias': even_dt_bias, 'even_head_norm_w': even_head_norm_w,
            'even_w_out': even_w_out, 'odd_w_in': odd_w_in, 'odd_conv_w': odd_conv_w,
            'odd_conv_b': odd_conv_b, 'odd_dt_bias': odd_dt_bias, 'odd_a_log': odd_a_log,
            'odd_d_skip': odd_d_skip, 'odd_out_norm_w': odd_out_norm_w, 'odd_w_out': odd_w_out}

def first_block(x, norm_w, ffn_w_gate, ffn_w_up, ffn_w_down, even_w_in, even_conv_w, even_a_log,
              even_dt_bias, even_head_norm_w, even_w_out, odd_w_in, odd_conv_w, odd_conv_b, odd_dt_bias,
              odd_a_log, odd_d_skip, odd_out_norm_w, odd_w_out):
    h = x
    for layer in range(DEPTH):
        nw = norm_w[layer]
        i = layer // 2
        f = swiglu(rmsnorm(h, nw[0]), ffn_w_gate[layer, 0], ffn_w_up[layer, 0], ffn_w_down[layer, 0])
        h = h + FFN_RES_SCALE * rmsnorm(f, nw[1])
        u = rmsnorm(h, nw[2])
        if layer % 2 == 0:
            m = even_mixer(u, even_w_in[i], even_conv_w[i], even_a_log[i], even_dt_bias[i],
                           even_head_norm_w[i], even_w_out[i])
        else:
            m = odd_mixer(u, odd_w_in[i], odd_conv_w[i], odd_conv_b[i], odd_dt_bias[i], odd_a_log[i],
                          odd_d_skip[i], odd_out_norm_w[i], odd_w_out[i])
        h = h + rmsnorm(m, nw[3])
        f = swiglu(rmsnorm(h, nw[4]), ffn_w_gate[layer, 1], ffn_w_up[layer, 1], ffn_w_down[layer, 1])
        h = h + FFN_RES_SCALE * rmsnorm(f, nw[5])
    return h


HEAD_DIM = 64
FOX_HEADS = 6
DIFF_HEADS = 4
DIFF_QK_DIM = 32
DIFF_V_DIM = 64
DSA_HEADS = 6
DSA_KV_DIM = 64
IDX_HEADS = 4
IDX_DIM = 64
DSA_TOPK = 256
ROPE_THETA = 500000.0
ROPE_FRACTION = 4
Q_BLOCK = 128
FFN_HIDDEN = -(-8 * D_MODEL // (3 * 256)) * 256

MIX_WIDTH = FOX_HEADS * HEAD_DIM + DIFF_HEADS * DIFF_V_DIM + DSA_HEADS * HEAD_DIM

SPLIT_SIZES = (
    FOX_HEADS * HEAD_DIM,
    FOX_HEADS * HEAD_DIM,
    FOX_HEADS * HEAD_DIM,
    FOX_HEADS,
    DIFF_HEADS * 2 * DIFF_QK_DIM,
    DIFF_HEADS * 2 * DIFF_QK_DIM,
    DIFF_HEADS * DIFF_V_DIM,
    DSA_HEADS * HEAD_DIM,
    DSA_KV_DIM,
    DSA_KV_DIM,
    IDX_HEADS * IDX_DIM,
    IDX_DIM,
    IDX_HEADS,
)
IN_WIDTH = sum(SPLIT_SIZES)


def rms_norm(x, g):
    xf = x.astype(jnp.float32)
    y = xf * lax.rsqrt(jnp.mean(xf * xf, axis=-1, keepdims=True) + NORM_EPS)
    return (y * g.astype(jnp.float32)).astype(x.dtype)

def rope_tables(seq_len, head_dim):
    rot = head_dim // ROPE_FRACTION
    inv_freq = 1.0 / (ROPE_THETA ** (jnp.arange(0, rot, 2, dtype=jnp.float32) / rot))
    ang = jnp.arange(seq_len, dtype=jnp.float32)[:, None] * inv_freq[None, :]
    return jnp.cos(ang), jnp.sin(ang)

def partial_rope(x, cos, sin):
    rot = x.shape[-1] // ROPE_FRACTION
    half = rot // 2
    c = cos.astype(x.dtype)
    s = sin.astype(x.dtype)
    x1 = x[..., :half]
    x2 = x[..., half:rot]
    return jnp.concatenate([x1 * c - x2 * s, x2 * c + x1 * s, x[..., rot:]], axis=-1)

def blocks_to_seq(out):
    out = jnp.moveaxis(out, 0, 1)
    return out.reshape((out.shape[0], out.shape[1] * out.shape[2]) + out.shape[3:])

def causal_mask(start, seq_len):
    qpos = start + jnp.arange(Q_BLOCK)
    kpos = jnp.arange(seq_len)
    return kpos[None, :] <= qpos[:, None], qpos

def fox_attention(q, k, v, cum_logf):
    S = q.shape[2]
    scale = q.shape[-1] ** -0.5

    def block(i):
        start = i * Q_BLOCK
        qb = lax.dynamic_slice_in_dim(q, start, Q_BLOCK, axis=2)
        cb = lax.dynamic_slice_in_dim(cum_logf, start, Q_BLOCK, axis=2)
        logits = (jnp.einsum('bhqd,bhkd->bhqk', qb, k).astype(jnp.float32) * scale
                  + cb[..., :, None] - cum_logf[..., None, :])
        mask, _ = causal_mask(start, S)
        p = jax.nn.softmax(jnp.where(mask, logits, -jnp.inf), axis=-1).astype(v.dtype)
        return jnp.einsum('bhqk,bhkd->bqhd', p, v)

    return blocks_to_seq(lax.map(block, jnp.arange(S // Q_BLOCK)))

def diff_attention(q, k, v, lam):
    S = q.shape[3]
    scale = q.shape[-1] ** -0.5

    def block(i):
        start = i * Q_BLOCK
        qb = lax.dynamic_slice_in_dim(q, start, Q_BLOCK, axis=3)
        logits = jnp.einsum('bhmqd,bhmkd->bhmqk', qb, k).astype(jnp.float32) * scale
        mask, _ = causal_mask(start, S)
        p = jax.nn.softmax(jnp.where(mask, logits, -jnp.inf), axis=-1)
        a = (p[:, :, 0] - lam * p[:, :, 1]).astype(v.dtype)
        return jnp.einsum('bhqk,bhkd->bqhd', a, v)

    return blocks_to_seq(lax.map(block, jnp.arange(S // Q_BLOCK)))

def dsa_attention(q, k, v, q_idx, k_idx, w_idx, topk):
    S = q.shape[2]
    scale = q.shape[-1] ** -0.5
    idx_scale = q_idx.shape[-1] ** -0.5
    gather = jax.vmap(lambda table, ix: table[ix])

    def block(i):
        start = i * Q_BLOCK
        qib = lax.dynamic_slice_in_dim(q_idx, start, Q_BLOCK, axis=2)
        wib = lax.dynamic_slice_in_dim(w_idx, start, Q_BLOCK, axis=1).astype(jnp.float32)
        s_idx = jnp.einsum('bhqd,bkd->bhqk', qib, k_idx).astype(jnp.float32) * idx_scale
        score = jnp.einsum('bqh,bhqk->bqk', wib, jax.nn.relu(s_idx))
        mask, qpos = causal_mask(start, S)
        score = jnp.where(mask[None], score, -jnp.inf)
        _, sel = lax.top_k(score, topk)
        valid = sel <= qpos[None, :, None]
        kg = gather(k, sel)
        vg = gather(v, sel)
        qb = lax.dynamic_slice_in_dim(q, start, Q_BLOCK, axis=2)
        logits = jnp.einsum('bhqd,bqjd->bhqj', qb, kg).astype(jnp.float32) * scale
        p = jax.nn.softmax(jnp.where(valid[:, None], logits, -jnp.inf), axis=-1).astype(vg.dtype)
        return jnp.einsum('bhqj,bqjd->bqhd', p, vg)

    return blocks_to_seq(lax.map(block, jnp.arange(S // Q_BLOCK)))

def second_inputs(seed: int = 0) -> dict:
    key = jax.random.key(seed)
    ks = jax.random.split(key, 19)
    f32 = jnp.float32

    def nrm(k, shape, scale):
        return jax.random.normal(k, shape, f32) * scale

    res_scale = 1.0 / math.sqrt(2 * DEPTH)
    return {
        "x": nrm(ks[0], (BATCH, SEQ, D_MODEL), 1.0),
        "attn_norm": 1.0 + nrm(ks[1], (DEPTH, D_MODEL), 0.02),
        "w_in": nrm(ks[2], (DEPTH, D_MODEL, IN_WIDTH), D_MODEL ** -0.5),
        "fox_fb": jax.random.uniform(ks[3], (DEPTH, FOX_HEADS), f32, 1.0, 4.0),
        "fox_qn": 1.0 + nrm(ks[4], (DEPTH, HEAD_DIM), 0.02),
        "fox_kn": 1.0 + nrm(ks[5], (DEPTH, HEAD_DIM), 0.02),
        "diff_qn": 1.0 + nrm(ks[6], (DEPTH, DIFF_QK_DIM), 0.02),
        "diff_kn": 1.0 + nrm(ks[7], (DEPTH, DIFF_QK_DIM), 0.02),
        "diff_lq1": nrm(ks[8], (DEPTH, DIFF_QK_DIM), 0.1),
        "diff_lk1": nrm(ks[9], (DEPTH, DIFF_QK_DIM), 0.1),
        "diff_lq2": nrm(ks[10], (DEPTH, DIFF_QK_DIM), 0.1),
        "diff_lk2": nrm(ks[11], (DEPTH, DIFF_QK_DIM), 0.1),
        "diff_subln": 1.0 + nrm(ks[12], (DEPTH, DIFF_V_DIM), 0.02),
        "dsa_qn": 1.0 + nrm(ks[13], (DEPTH, HEAD_DIM), 0.02),
        "dsa_kn": 1.0 + nrm(ks[14], (DEPTH, DSA_KV_DIM), 0.02),
        "w_out": nrm(ks[15], (DEPTH, MIX_WIDTH, D_MODEL), MIX_WIDTH ** -0.5 * res_scale),
        "ffn_norm": 1.0 + nrm(ks[16], (DEPTH, D_MODEL), 0.02),
        "w_gate_up": nrm(ks[17], (DEPTH, D_MODEL, 2 * FFN_HIDDEN), D_MODEL ** -0.5),
        "w_down": nrm(ks[18], (DEPTH, FFN_HIDDEN, D_MODEL), FFN_HIDDEN ** -0.5 * res_scale),
    }

def second_block(x, attn_norm, w_in, fox_fb, fox_qn, fox_kn, diff_qn, diff_kn,
              diff_lq1, diff_lk1, diff_lq2, diff_lk2, diff_subln, dsa_qn, dsa_kn,
              w_out, ffn_norm, w_gate_up, w_down):
    B, S, _ = x.shape
    topk = min(DSA_TOPK, S // 4)
    cos64, sin64 = rope_tables(S, HEAD_DIM)
    cos32, sin32 = rope_tables(S, DIFF_QK_DIM)
    split_points = [int(v) for v in np.cumsum(SPLIT_SIZES)[:-1]]

    for l in range(DEPTH):
        h = rms_norm(x, attn_norm[l])
        proj = h @ w_in[l]
        (fq, fk, fv, ff, dq, dk, dv, sq, sk, sv, iq, ik, iw) = jnp.split(proj, split_points, axis=-1)

        fq = rms_norm(fq.reshape(B, S, FOX_HEADS, HEAD_DIM), fox_qn[l]).transpose(0, 2, 1, 3)
        fk = rms_norm(fk.reshape(B, S, FOX_HEADS, HEAD_DIM), fox_kn[l]).transpose(0, 2, 1, 3)
        fv = fv.reshape(B, S, FOX_HEADS, HEAD_DIM).transpose(0, 2, 1, 3)
        log_f = jax.nn.log_sigmoid(ff.astype(jnp.float32) + fox_fb[l].astype(jnp.float32))
        cum_logf = jnp.cumsum(log_f, axis=1).transpose(0, 2, 1)
        o_fox = fox_attention(fq, fk, fv, cum_logf).reshape(B, S, FOX_HEADS * HEAD_DIM)

        lam_init = 0.8 - 0.6 * math.exp(-0.3 * l)
        lam = (jnp.exp(jnp.sum(diff_lq1[l].astype(jnp.float32) * diff_lk1[l].astype(jnp.float32)))
               - jnp.exp(jnp.sum(diff_lq2[l].astype(jnp.float32) * diff_lk2[l].astype(jnp.float32)))
               + lam_init)
        dq = rms_norm(dq.reshape(B, S, DIFF_HEADS, 2, DIFF_QK_DIM), diff_qn[l]).transpose(0, 2, 3, 1, 4)
        dk = rms_norm(dk.reshape(B, S, DIFF_HEADS, 2, DIFF_QK_DIM), diff_kn[l]).transpose(0, 2, 3, 1, 4)
        dq = partial_rope(dq, cos32, sin32)
        dk = partial_rope(dk, cos32, sin32)
        dv = dv.reshape(B, S, DIFF_HEADS, DIFF_V_DIM).transpose(0, 2, 1, 3)
        o_diff = diff_attention(dq, dk, dv, lam)
        o_diff = (rms_norm(o_diff, diff_subln[l]) * (1.0 - lam_init)).reshape(B, S, DIFF_HEADS * DIFF_V_DIM)

        sq = partial_rope(rms_norm(sq.reshape(B, S, DSA_HEADS, HEAD_DIM), dsa_qn[l]).transpose(0, 2, 1, 3), cos64, sin64)
        sk = partial_rope(rms_norm(sk, dsa_kn[l]), cos64, sin64)
        iq = partial_rope(iq.reshape(B, S, IDX_HEADS, IDX_DIM).transpose(0, 2, 1, 3), cos64, sin64)
        ik = partial_rope(ik, cos64, sin64)
        iw = iw * (IDX_HEADS ** -0.5)
        o_dsa = dsa_attention(sq, sk, sv, iq, ik, iw, topk).reshape(B, S, DSA_HEADS * HEAD_DIM)

        x = x + jnp.concatenate([o_fox, o_diff, o_dsa], axis=-1) @ w_out[l]

        h = rms_norm(x, ffn_norm[l])
        gate, up = jnp.split(h @ w_gate_up[l], 2, axis=-1)
        x = x + (jax.nn.silu(gate) * up) @ w_down[l]
    return x


def setup_inputs(seed=0):
    out = dict(first_inputs(seed))
    for name, value in second_inputs(seed + 1).items():
        if name != "x":
            out[name + "_2"] = value
    return out


def reference(
    x, norm_w, ffn_w_gate, ffn_w_up, ffn_w_down, even_w_in, even_conv_w, even_a_log,
    even_dt_bias, even_head_norm_w, even_w_out, odd_w_in, odd_conv_w, odd_conv_b, odd_dt_bias,
    odd_a_log, odd_d_skip, odd_out_norm_w, odd_w_out, attn_norm_2, w_in_2, fox_fb_2, fox_qn_2,
    fox_kn_2, diff_qn_2, diff_kn_2, diff_lq1_2, diff_lk1_2, diff_lq2_2, diff_lk2_2,
    diff_subln_2, dsa_qn_2, dsa_kn_2, w_out_2, ffn_norm_2, w_gate_up_2, w_down_2,
):
    x = first_block(
        x, norm_w, ffn_w_gate, ffn_w_up, ffn_w_down, even_w_in, even_conv_w, even_a_log,
        even_dt_bias, even_head_norm_w, even_w_out, odd_w_in, odd_conv_w, odd_conv_b,
        odd_dt_bias, odd_a_log, odd_d_skip, odd_out_norm_w, odd_w_out,
    )
    return second_block(
        x, attn_norm_2, w_in_2, fox_fb_2, fox_qn_2, fox_kn_2, diff_qn_2, diff_kn_2, diff_lq1_2,
        diff_lk1_2, diff_lq2_2, diff_lk2_2, diff_subln_2, dsa_qn_2, dsa_kn_2, w_out_2,
        ffn_norm_2, w_gate_up_2, w_down_2,
    )


_drawn_inputs = setup_inputs


def setup_inputs(seed=0):
    import zlib

    import numpy as np

    out = dict(_drawn_inputs(seed))
    spreads = {}
    factors = {'odd_conv_b': 3.718,
     'attn_norm_2': 8.0,
     'fox_qn_2': 8.0,
     'fox_kn_2': 8.0,
     'diff_qn_2': 8.0,
     'diff_kn_2': 8.0,
     'diff_lq1_2': 4.202,
     'diff_lk1_2': 4.935,
     'diff_lq2_2': 8.0,
     'diff_lk2_2': 8.0,
     'diff_subln_2': 8.0,
     'dsa_qn_2': 8.0,
     'dsa_kn_2': 8.0,
     'ffn_norm_2': 8.0}
    for name, (base, spread) in spreads.items():
        noise = np.random.default_rng([zlib.crc32(name.encode()), seed]).standard_normal(out[name].shape)
        drawn = base * np.exp(spread * noise) if base else spread * noise
        out[name] = jnp.asarray(drawn.astype(out[name].dtype))
    for name, factor in factors.items():
        out[name] = (out[name] * factor).astype(out[name].dtype)
    return out
```

```python
import numpy as np
from contextlib import ExitStack

import concourse.bass as bass
from concourse import mybir
from concourse.alu_op_type import AluOpType as ALU

ACT = mybir.ActivationFunctionType
F32 = mybir.dt.float32
AX = mybir.AxisListType.X

P = 128
S = 512
D = 1024
FF = 2816
NJ = FF // P
EPS = 1e-6
BIG = 1e30
LOW = -3e38
RING = 6

C_PRE, C_ECONV, C_OCONV, C_OBIAS, C_ONORM, C_HNORM, C_N = 0, 80, 128, 224, 248, 264, 265
R_EA, R_EDT, R_OA, R_ODT, R_DSK, R_L = 0, 4, 8, 40, 72, 104
L_FB, L_FQ, L_FK, L_DQ, L_DK, L_SUB, L_SQ, L_SK, L_LQ1, L_LK1, L_LQ2, L_LK2, L_N = (
    0, 6, 70, 134, 166, 198, 262, 326, 390, 422, 454, 486, 518)
R_N = R_L + 2 * L_N
K_ID, K_TRI, K_ONE, K_LOW, K_M1, K_LV, K_CAUS, K_CM, K_R64, K_R32, K_N = (
    0, 128, 256, 384, 512, 640, 1408, 1920, 2432, 2496, 2528)
Q_FQ, Q_FK, Q_FV, Q_FF, Q_DQ, Q_DK, Q_DV, Q_SQ, Q_SK, Q_SV, Q_IQ, Q_IK, Q_IW, Q_N = (
    0, 384, 768, 1152, 1158, 1414, 1670, 1926, 2310, 2374, 2438, 2694, 2758, 2762)


class Queue:

    def __init__(self, sem, engine):
        self.sem, self.n, self.engine, self.seen = sem, 0, engine, {}

    def wait(self, *toks):
        need = {}
        for sem, v in toks:
            if v > self.seen.get(id(sem), 0) and v > need.get(id(sem), (sem, 0))[1]:
                need[id(sem)] = (sem, v)
        for sem, v in need.values():
            self.seen[id(sem)] = v
            if self.engine is not None:
                self.engine.wait_ge(sem, v)

    def quiet(self, fn, *toks):
        self.wait(*toks)
        if self.engine is not None:
            fn(self.engine)

    def __call__(self, fn, *toks):
        self.wait(*toks)
        self.n += 1
        if self.engine is not None:
            fn(self.engine).then_inc(self.sem, 1)
        return (self.sem, self.n)

    def now(self):
        return (self.sem, self.n)


class Slots:

    def __init__(self, items):
        self.free = [(x, ()) for x in items]

    def take(self):
        return self.free.pop(0)

    def give(self, item, *toks):
        self.free.append((item, toks))


def build(nc, a, out, upto=99):
    ctx = ExitStack()
    with ctx:
        def sb(name, n):
            return ctx.enter_context(nc.sbuf_tensor(name, [P, n], F32))

        def sem(name):
            return ctx.enter_context(nc.semaphore(name))

        Ht = sb("H", 4 * D)
        XTt = sb("XT", 8 * S)
        Wt = sb("W", RING * 2048)
        CPt = sb("CP", C_N)
        RPt = sb("RP", R_N)
        KCt = sb("KC", K_N)
        WRt = sb("WR", 2 * D)
        SMt = sb("SM", 1600)
        AR = sb("AR", 20480)
        SC = sb("SC", 4608)
        banks = [ctx.enter_context(nc.psum_tensor(f"ps{i}", [P, 512], F32)) for i in range(8)]
        wsem = [sem(f"ws{i}") for i in range(RING)]
        rsem = [sem("wr0"), sem("wr1")]
        s_in = sem("s_in")
        s_out = sem("s_out")
        sems = [sem(n) for n in ("s_pe", "s_dv", "s_ac", "s_pl", "s_sp")]
        mem = (Ht, XTt, Wt, CPt, RPt, KCt, WRt, SMt, AR, SC, banks, wsem, rsem, s_in, s_out, sems)
        block = ctx.enter_context(nc.Block())

        @block.sync
        def _(e):
            schedule(a, out, mem, 4, e, upto)

        @block.tensor
        def _(e):
            schedule(a, out, mem, 0, e, upto)

        @block.vector
        def _(e):
            schedule(a, out, mem, 1, e, upto)

        @block.scalar
        def _(e):
            schedule(a, out, mem, 2, e, upto)

        @block.gpsimd
        def _(e):
            schedule(a, out, mem, 3, e, upto)


def schedule(a, out, mem, turn_of, engine, upto):
    Ht, XTt, Wt, CPt, RPt, KCt, WRt, SMt, AR, SC, banks, wsem, rsem, s_in, s_out, sems = mem
    H = Ht[:, :].rearrange("p (m d) -> p m d", m=4)
    XT = XTt[:, :].rearrange("p (f s) -> p f s", s=S)
    psum = Slots(range(8))
    ring = Slots(range(RING))
    wcnt = [0] * RING
    rcnt = [0, 0]
    rows = Slots(range(2))
    PE, DV, AC, PL, SP = (Queue(x, engine if k == turn_of else None) for k, x in enumerate(sems))

    def cp(c, n=1):
        return CPt[:, c:c + n]

    def rp(c, n):
        return RPt[:, c:c + n]

    def kc(c, n=128):
        return KCt[:, c:c + n]

    IDN = kc(K_ID)
    TRI = kc(K_TRI)
    ONE = kc(K_ONE)

    def arena(off, n):
        return AR[:, off:off + n]

    small = [0]

    def sm(n):
        o = small[0]
        small[0] += n
        assert small[0] <= 1600
        return SMt[:, o:o + n]

    def fence():
        t = [q.now() for q in (PE, DV, AC, PL)]
        for q in (PE, DV, AC, PL):
            q.wait(*t)

    flip = [0]

    def evac(dst, src, *toks, scale=None):
        flip[0] ^= 1
        if flip[0]:
            if scale is None:
                return AC(lambda e: e.copy(dst, src), *toks)
            return AC(lambda e: e.mul(dst, src, scale), *toks)
        if scale is None:
            return DV(lambda e: e.tensor_copy(dst, src), *toks)
        return DV(lambda e: e.tensor_scalar(dst, src, scale, None, ALU.mult), *toks)

    def act(dst, src, f, *toks, **kw):
        return AC(lambda e: e.activation(dst, src, f, **kw), *toks)

    def tt(q, dst, x, y, op, *toks):
        return q(lambda e: e.tensor_tensor(dst, x, y, op), *toks)

    def ts(dst, x, s1, op0, s2, op1, *toks, q=None):
        q = q or DV
        if s2 is None:
            return q(lambda e: e.tensor_scalar(dst, x, s1, None, op0), *toks)
        return q(lambda e: e.tensor_scalar(dst, x, s1, s2, op0, op1), *toks)

    def stt(dst, x, s, y, op0, op1, *toks):
        return DV(lambda e: e.scalar_tensor_tensor(dst, x, s, y, op0, op1), *toks)

    def load(src, nk, n):
        i, fr = ring.take()
        dst = Wt[:, i * 2048:i * 2048 + nk * n].rearrange("p (k n) -> p k n", n=n)
        wcnt[i] += 16
        SP.quiet(lambda e: e.dma_start(dst, src.rearrange("(k p) n -> p k n", p=P)).then_inc(wsem[i], 16), *fr)
        return dst, i, (wsem[i], wcnt[i])

    def load_row(src):
        i, fr = rows.take()
        dst = WRt[:, i * D:(i + 1) * D]
        rcnt[i] += 16
        SP.quiet(lambda e: e.dma_start(dst, src.partition_broadcast(P)).then_inc(rsem[i], 16), *fr)
        return dst, i, (rsem[i], rcnt[i])

    T_IN = (s_in, 64)
    for dst, src in ((H, a["x"].rearrange("b (m p) d -> p (b m) d", p=P)), (KCt[:, :], a["consts"]),
                     (CPt[:, :], a["colp"])):
        SP.quiet(lambda e, dst=dst, src=src: e.dma_start(dst, src).then_inc(s_in, 16))
    SP.quiet(lambda e: e.dma_start(RPt[:, :], a["rowp"].partition_broadcast(P)).then_inc(s_in, 16))
    for q in (PE, DV, AC, PL):
        q.wait(T_IN)

    def gemm_t(x, nk, w, c0, n, use, *toks):
        def matmuls(j, wt, i, c, tk, last):
            b, fr = psum.take()
            for k in range(nk):
                f = (lambda e, k=k: e.matmul(banks[b][:, :], wt[:, k, c:c + P], x(k), start=(k == 0),
                                             stop=(k == nk - 1)))
                if k < nk - 1:
                    PE.quiet(f, tk, *fr, *(toks if not k else ()))
            t = PE(f)
            if last:
                ring.give(i, t)
            return b, t
        for c in range(0, n, 256):
            wt, i, tk = load(w[:, c0 + c:c0 + c + 256], nk, 256)
            for cc in (0, 128):
                b, t = matmuls((c + cc) // P, wt, i, cc, tk, cc == 128)
                use((c + cc) // P, b, t)

    def gemm(x, nk, w, c0, n, use, toks=()):
        bs, fr = zip(*[psum.take() for _ in range(4)])
        for k0 in range(0, nk, 4):
            kk = min(4, nk - k0)
            wt, i, tk = load(w[k0 * P:(k0 + kk) * P, c0:c0 + n], kk, n)
            for k in range(k0, k0 + kk):
                for m in range(4):
                    f = (lambda e, k=k, m=m, wt=wt, k0=k0: e.matmul(
                        banks[bs[m]][:, 0:n], x(k, m), wt[:, k - k0, :], start=(k == 0), stop=(k == nk - 1)))
                    ws = [tk, *toks] + (list(fr[m]) if k == 0 else [])
                    if k == nk - 1 or (k == k0 + kk - 1 and m == 3):
                        t = PE(f, *ws)
                        if k == nk - 1:
                            use(m, bs[m], t)
                    else:
                        PE.quiet(f, *ws)
            ring.give(i, t)

    def turn(src, nf, dst, toks, scale=None, wait=()):
        done = []
        for f0 in range(0, nf, 8):
            fs = range(f0, min(nf, f0 + 8))
            bs = {f: psum.take() for f in fs}
            last = {}
            for m in range(4):
                for f in fs:
                    b, fr = bs[f]
                    last[f] = PE(lambda e, b=b, m=m, f=f: e.transpose(banks[b][:, m * P:(m + 1) * P], src(m, f), IDN),
                                 *toks[m], *fr)
            for f in fs:
                t = evac(dst(f), banks[bs[f][0]][:, :], last[f], *wait, scale=scale(f) if scale else None)
                psum.give(bs[f][0], t)
                done.append(t)
        return done

    ss8, ss4, rst = sm(8), sm(4), sm(8)
    scr = [SC[:, i * 512:(i + 1) * 512] for i in range(9)]

    def inv_root(dst, src, mul, *toks, factor=None):
        t = ts(dst, src, mul, ALU.mult, EPS, ALU.add, *toks)
        t = act(dst, dst, ACT.Sqrt, t)
        t = DV(lambda e: e.reciprocal(dst, dst), t)
        if factor is not None:
            t = ts(dst, dst, factor, ALU.mult, None, None, t)
        return t

    def prenorm(col, *toks):
        xn = SC[:, 0:4096].rearrange("p (m d) -> p m d", m=4)
        ready = []
        for m in range(4):
            t = AC(lambda e, m=m: e.activation(xn[:, m, :], H[:, m, :], ACT.Square, accum_out=ss4[:, m:m + 1]), *toks)
        t = inv_root(rst[:, 0:4], ss4, 1.0 / D, t)
        for m in range(4):
            ready.append([ts(xn[:, m, :], H[:, m, :], rst[:, m:m + 1], ALU.mult, None, None, t)])
        return turn(lambda m, f: xn[:, m, f * P:(f + 1) * P], 8, lambda f: XT[:, f, :], ready,
                    lambda f: cp(C_PRE + col * 8 + f))

    def finish(parts, row, factor):
        res = []
        if row is None:
            for (m, h), (b, t) in sorted(parts.items()):
                hv = H[:, m, h * 512:(h + 1) * 512]
                t = tt(DV, hv, banks[b][:, :], hv, ALU.add, t)
                psum.give(b, t)
                res.append(t)
            return res
        w, i, tw = load_row(row)
        sq = Slots([(0), (1)])
        for (m, h), (b, t) in sorted(parts.items(), key=lambda x: (x[0][1], x[0][0])):
            n, fr = sq.take()
            t = AC(lambda e, b=b, n=n, k=2 * m + h: e.activation(scr[n], banks[b][:, :], ACT.Square,
                                                               accum_out=ss8[:, k:k + 1]), t, *fr)
            sq.give(n, t)
        s2 = ss8.rearrange("p (m h) -> p m h", h=2)
        t = tt(DV, ss4, s2[:, :, 0], s2[:, :, 1], ALU.add, t)
        t = inv_root(rst[:, 4:8], ss4, 1.0 / D, t, factor=factor)
        tmp = Slots([2, 3, 4, 5])
        for (m, h), (b, _) in sorted(parts.items()):
            n, fr = tmp.take()
            hv = H[:, m, h * 512:(h + 1) * 512]
            tb = stt(scr[n], banks[b][:, :], rst[:, 4 + m:5 + m], w[:, h * 512:(h + 1) * 512], ALU.mult, ALU.mult,
                     t, tw, *fr)
            psum.give(b, tb)
            t2 = tt(PL, hv, hv, scr[n], ALU.add, tb)
            tmp.give(n, t2)
            res.append(t2)
        rows.give(i, tb)
        return res

    def product_out(x, nk, w, row, factor, toks=()):
        parts = {}
        for h in range(2):
            gemm(x, nk, w, h * 512, 512, lambda m, b, t, h=h: parts.__setitem__((m, h), (b, t)), toks)
        return finish(parts, row, factor)

    def ffn(col, wg, wu, wd, row, factor, toks):
        G = arena(0, NJ * S).rearrange("p (j s) -> p j s", s=S)
        tx = prenorm(col, *toks)
        got = {}
        ready = {}

        def use(kind, j, b, t):
            got[kind, j] = (b, t)
            if ("g", j) in got and ("u", j) in got:
                (bg, tg), (bu, tu) = got["g", j], got["u", j]
                t = act(G[:, j, :], banks[bg][:, :], ACT.Silu, tg)
                psum.give(bg, t)
                t = tt(DV, G[:, j, :], banks[bu][:, :], G[:, j, :], ALU.mult, t, tu)
                psum.give(bu, t)
                ready[j] = t

        for j in range(0, NJ, 2):
            for kind, w in (("g", wg), ("u", wu)):
                gemm_t(lambda k: XT[:, k, :], 8, w, j * P, 256,
                       lambda i, b, t, kind=kind, j=j: use(kind, j + i, b, t), *tx)
        return product_out(lambda k, m: G[:, k, m * P:(m + 1) * P], NJ, wd, row, factor, (ready[NJ - 1],))

    st_nm, st_l, st_r = sm(24), sm(24), sm(24)

    def attention(units):
        sbuf = Slots([0, 1, 2])
        pbuf = Slots([3, 4, 5])
        tbuf = Slots([6, 7, 8])
        stat = Slots([0, 1, 2])
        n = len(units)
        obank = [None]

        def scores(u):
            W = (u["i"] + 1) * P
            if u["slot"] == 0:
                u["o"], u["ofr"] = psum.take()
                u["st"], u["sfr"] = stat.take()
                obank[0] = u
            g = u["g"] = obank[0]
            b, fr = psum.take()
            t = PE(lambda e: e.matmul(banks[b][:, 0:W], u["q"], u["k"], start=True, stop=True), *fr)
            col = g["st"] * 8 + u["slot"]
            s, fs = sbuf.take()
            nm, l = st_nm[:, col:col + 1], st_l[:, col:col + 1]
            mask, tm = u["mask"]() if callable(u["mask"]) else (u["mask"], ())
            sv = scr[s][:, 0:W]
            bv = banks[b][:, 0:W]
            if len(mask.shape) == 3:
                sv = sv.rearrange("p (a b) -> p a b", b=P)
                bv = bv.rearrange("p (a b) -> p a b", b=P)
            t = DV(lambda e: e.tensor_tensor_reduce(sv, bv, mask, -1.0, 3e38, ALU.add,
                                                    ALU.min, nm), t, *fs, *g["sfr"], *tm)
            u["maskdone"] = t
            if u.get("free"):
                u["free"](t)
            psum.give(b, t)
            p, fp = pbuf.take()
            u["p"] = p
            t = AC(lambda e: e.activation(scr[p][:, 0:W], scr[s][:, 0:W], ACT.Exp, bias=nm, scale=-1.0,
                                          accum_out=l), t, *fp, *g["sfr"])
            sbuf.give(s, t)
            if u["times"] is not None:
                t = DV(lambda e: e.tensor_tensor_reduce(scr[p][:, 0:W], scr[p][:, 0:W], u["times"], 1.0, 0.0,
                                                        ALU.mult, ALU.add, l), t)
            u["t"] = t

        def turned(u):
            nb = u["i"] + 1
            b, fr = psum.take()
            for kb in range(nb):
                t = PE(lambda e, kb=kb: e.transpose(banks[b][:, kb * P:(kb + 1) * P],
                                                    scr[u["p"]][:, kb * P:(kb + 1) * P], IDN), u["t"], *fr)
            pbuf.give(u["p"], t)
            x, fx = tbuf.take()
            u["x"] = x
            t = evac(scr[x][:, 0:nb * P], banks[b][:, 0:nb * P], t, *fx)
            psum.give(b, t)
            u["t"] = t

        def values(u):
            nb = u["i"] + 1
            g = u["g"]
            for kb in range(nb):
                t = PE(lambda e, kb=kb: e.matmul(banks[g["o"]][:, u["slot"] * 64:u["slot"] * 64 + 64],
                                                 scr[u["x"]][:, kb * P:(kb + 1) * P], u["values"](kb),
                                                 start=(kb == 0), stop=(kb == nb - 1)), u["t"], *g["ofr"])
            tbuf.give(u["x"], t)
            if u["done"] is not None:
                c = g["st"] * 8
                w = u["slot"] + 1
                tr = DV(lambda e: e.reciprocal(st_r[:, c:c + w], st_l[:, c:c + w]), u["t"], *g["sfr"])
                ts_ = u["done"](banks[g["o"]], st_r[:, c:c + w], t, tr)
                psum.give(g["o"], ts_)
                stat.give(g["st"], ts_)

        for x in range(n + 3):
            if x < n:
                scores(units[x])
            if 0 <= x - 2 < n:
                turned(units[x - 2])
            if 0 <= x - 3 < n:
                values(units[x - 3])

    def scale_heads(dst, bank, r, nh, c0, *toks):
        return tt(DV, dst, bank[:, c0 * 64:(c0 + nh) * 64].rearrange("p (h d) -> p h d", d=64),
                  r[:, c0:c0 + nh].unsqueeze(2).broadcast_to((P, nh, 64)), ALU.mult, *toks)

    def softplus(x, t1, t2, t3, *toks):
        t = ts(t1, x, -1.0, ALU.mult, None, None, *toks)
        t = tt(DV, t1, t1, x, ALU.min, t)
        t = act(t1, t1, ACT.Exp, t)
        t = ts(t2, t1, 2.0, ALU.add, None, None, t)
        t = DV(lambda e: e.reciprocal(t2, t2), t)
        t = tt(DV, t1, t1, t2, ALU.mult, t)
        t = tt(DV, t2, t1, t1, ALU.mult, t)
        t = ts(t3, t2, 2.0 / 19, ALU.mult, None, None, t)
        for k in range(8, 0, -1):
            t = stt(t3, t3, 2.0 / (2 * k + 1), t2, ALU.add, ALU.mult, t)
        t = stt(t3, t3, 2.0, t1, ALU.add, ALU.mult, t)
        return stt(x, x, 0.0, t3, ALU.max, ALU.add, t)

    cbuf = Slots([0, 1, 2, 3])

    def conv(b, t, taps, bias):
        n, fr = cbuf.take()
        acc = scr[n]
        x = banks[b]
        t = AC(lambda e: e.mul(acc, x[:, :], cp(taps + 3)), t, *fr)
        for k in (2, 1, 0):
            s = 3 - k
            t = stt(acc[:, s:S], x[:, 0:S - s], cp(taps + k), acc[:, s:S], ALU.mult, ALU.add, t)
        psum.give(b, t)
        if bias is None:
            t = act(acc, acc, ACT.Silu, t)
        else:
            t = act(acc, acc, ACT.Silu, t, bias=cp(bias))
        return n, t

    class Later:

        def __init__(self, lag):
            self.lag, self.fns = lag, []

        def add(self, fn):
            self.fns.append(fn)
            if len(self.fns) > self.lag:
                self.fns.pop(0)()

        def flush(self):
            while self.fns:
                self.fns.pop(0)()

    def turn_block(n, t, dst):
        b, fr = psum.take()
        for c in range(4):
            tp = PE(lambda e, c=c: e.transpose(banks[b][:, c * P:(c + 1) * P], scr[n][:, c * P:(c + 1) * P], IDN),
                    t, *fr)
        te = evac(dst, banks[b][:, :].rearrange("p (c f) -> p c f", f=P), tp)
        psum.give(b, te)
        return tp, te

    def even(toks):
        w = a["even_w_in"][0]
        QA = arena(0, 2048).rearrange("p (f s) -> p f s", s=S)
        KA = arena(2048, 2048).rearrange("p (f s) -> p f s", s=S)
        VA = arena(4096, 2048).rearrange("p (m d) -> p m d", m=4)
        ZB = arena(6144, 2048).rearrange("p (m d) -> p m d", m=4)
        QKV = arena(8192, 6144).rearrange("p (c f) -> p c f", c=4)
        O = arena(14336, 4096).rearrange("p (m d) -> p m d", m=4)
        small[0] = SM0
        GT = sm(32).rearrange("p (m d) -> p m d", m=4)
        tx = prenorm(1, *toks)

        def put(dst, scale=None):
            def use(j, b, t):
                psum.give(b, evac(dst(j), banks[b][:, :], t, scale=scale))
            return use

        xk = lambda k: XT[:, k, :]
        xm = lambda k, m: XT[:, k, m * P:(m + 1) * P]
        fence()
        gemm_t(xk, 8, w, 0, 512, put(lambda j: QA[:, j, :], 0.125), *tx)
        gemm_t(xk, 8, w, 512, 512, put(lambda j: KA[:, j, :]), *tx)
        gemm(xm, 8, w, 1024, 512, put(lambda m: VA[:, m, :]))
        later = Later(2)

        def use(j, b, t):
            n, t = conv(b, t, C_ECONV + 4 * j, None)

            def go():
                tp, te = turn_block(n, t, QKV[:, :, j * P:(j + 1) * P])
                cbuf.give(n, tp)
            later.add(go)
        gemm_t(xk, 8, w, 1536, 1536, use, *tx)
        later.flush()

        def use_z(m, b, t):
            t = act(ZB[:, m, :], banks[b][:, :], ACT.Silu, t)
            psum.give(b, t)
        gemm(xm, 8, w, 3072, 512, use_z)

        def use_g(m, b, t):
            t = DV(lambda e: e.tensor_copy(GT[:, m, :], banks[b][:, 0:8]), t)
            psum.give(b, t)
        gemm(xm, 8, w, 3584, 8, use_g)
        fence()
        AM = arena(18432, 512)
        ts(AM, kc(K_CM, 512), 0.0, ALU.is_equal, -BIG, ALU.mult)
        fence()
        units = []
        for i in range(4):
            def done(bank, r, t, tr, i=i):
                return scale_heads(O[:, i, 0:512].rearrange("p (h d) -> p h d", d=64), bank, r, 8, 0, t, tr)
            for h in range(8):
                r0 = 64 * (h % 2)
                W = (i + 1) * P
                units.append(dict(i=i, q=QA[r0:r0 + 64, h // 2, i * P:(i + 1) * P], k=KA[r0:r0 + 64, h // 2, 0:W],
                                  mask=AM[:, 512 - W:512], times=kc(K_CM + 512 - W, W),
                                  values=lambda kb, h=h: VA[:, kb, h * 64:(h + 1) * 64], slot=h,
                                  done=done if h == 7 else None))
        attention(units)
        fence()
        GB = sm(16).rearrange("p (m d) -> p m d", m=4)
        GG = sm(16)
        G3 = GG.rearrange("p (m d) -> p m d", m=4)
        sa, sb_, sc_, ea4 = sm(16), sm(16), sm(16), sm(4)
        t = act(GB, GT[:, :, 0:4], ACT.Exp, scale=-1.0)
        t = ts(GB, GB, 1.0, ALU.add, None, None, t)
        t = DV(lambda e: e.reciprocal(GB, GB), t)
        t = tt(DV, G3, GT[:, :, 4:8], rp(R_EDT, 4).unsqueeze(1).broadcast_to((P, 4, 4)), ALU.add)
        t = softplus(GG, sa, sb_, sc_, t)
        t1 = act(ea4, rp(R_EA, 4), ACT.Exp)
        t = stt(G3, G3, -1.0, ea4.unsqueeze(1).broadcast_to((P, 4, 4)), ALU.mult, ALU.mult, t, t1)
        SQ = arena(0, 1024)
        QS = sm(32)
        tprev = []
        for c in range(4):
            t = act(SQ, QKV[:, c, 0:1024], ACT.Square, *tprev)
            t = DV(lambda e, c=c: e.tensor_reduce(QS[:, c * 8:(c + 1) * 8], SQ.rearrange("p (h d) -> p h d", d=P),
                                                  AX, ALU.add), t)
            tprev = [t]
        t = inv_root(QS, QS, 1.0, t)
        Q3 = QS.rearrange("p (c h) -> p c h", c=4)
        t = ts(Q3[:, :, 0:4], Q3[:, :, 0:4], float(P) ** -0.5, ALU.mult, None, None, t)
        for c in range(4):
            v = QKV[:, c, 0:1024].rearrange("p (h d) -> p h d", d=P)
            tt(DV, v, v, Q3[:, c, :].unsqueeze(2).broadcast_to((P, 8, P)), ALU.mult, t)
        GC, EG, EL, EK, NB = sm(16), sm(16), sm(16), sm(16), sm(16)
        b, fr = psum.take()
        PE(lambda e: e.matmul(banks[b][:, 0:16], TRI, GG, start=True, stop=True), DV.now(), *fr)
        t = PE(lambda e: e.matmul(banks[b][:, 16:32], ONE, GG, start=True, stop=True))
        t1 = DV(lambda e: e.tensor_copy(GC, banks[b][:, 0:16]), t)
        t2 = act(EG, GC, ACT.Exp, t1)
        t3 = act(EL, banks[b][:, 16:32], ACT.Exp, t, t1)
        t4 = tt(DV, EK, banks[b][:, 16:32], GC, ALU.subtract, t1, t3)
        psum.give(b, t4)
        t5 = act(EK, EK, ACT.Exp, t4)
        t6 = stt(NB, GB.rearrange("p m d -> p (m d)"), -1.0, EG, ALU.mult, ALU.mult, t2)
        fence()
        A3 = lambda off: arena(off, 512)
        KD, UB, WB, QD, KT, QT = (A3(512 * i) for i in range(6))
        QDT, Dm, DT, Am, AT, LT = (A3(512 * i) for i in range(6, 12))
        X, XX, Y, QK, WT, VN = (XTt[:, 512 * i:512 * (i + 1)] for i in range(6))
        ST = XTt[:, 3072:3584]
        h3 = lambda x: x.rearrange("p (h d) -> p h d", d=P)
        hd = lambda x, h: x[:, h * P:(h + 1) * P]

        def per_head(fn, b, *toks):
            for h in range(4):
                t = PE(lambda e, h=h: e.matmul(hd(banks[b], h), *fn(h), start=True, stop=True), *toks)
            return t

        def bc(x, c):
            return x[:, 4 * c:4 * c + 4].unsqueeze(2).broadcast_to((P, 4, P))
        QDT, Dm, DT, Am, AT, LT = scr[0], scr[1], scr[2], scr[3], scr[4], scr[5]
        ARG = scr[6]
        AR2 = scr[7]
        GBf = GB.rearrange("p m d -> p (m d)")
        for c in range(4):
            q, k, v = (QKV[:, c, 512 * i:512 * (i + 1)] for i in range(3))
            fence()
            t_qd = tt(DV, h3(QD), h3(q), bc(EG, c), ALU.mult)
            t_kd = tt(PL, h3(KD), h3(k), bc(EK, c), ALU.mult)
            t_wb = tt(PL, h3(WB), h3(k), bc(NB, c), ALU.mult)
            t_ub = tt(PL, h3(UB), h3(v), bc(GBf, c), ALU.mult)
            bq, f1 = psum.take()
            bk, f2 = psum.take()
            bd, f3 = psum.take()
            br, f4 = psum.take()
            for h in range(4):
                tr = PE(lambda e, h=h: e.matmul(hd(banks[br], h), GG[:, 4 * c + h:4 * c + h + 1].broadcast_to((P, P)),
                                                TRI, start=True, stop=True), *f4)
            for h in range(4):
                tk = PE(lambda e, h=h: e.transpose(hd(banks[bk], h), hd(k, h), IDN), *f2)
            for h in range(4):
                tq = PE(lambda e, h=h: e.transpose(hd(banks[bq], h), hd(q, h), IDN), *f1)
            for h in range(4):
                td = PE(lambda e, h=h: e.transpose(hd(banks[bd], h), hd(QD, h), IDN), t_qd, *f3)
            t_kt = AC(lambda e: e.copy(KT, banks[bk][:, :]), tk)
            psum.give(bk, t_kt)
            t_qt = AC(lambda e: e.copy(QT, banks[bq][:, :]), tq)
            psum.give(bq, t_qt)
            for h in range(4):
                g = GC[:, 4 * c + h:4 * c + h + 1]
                ts(hd(ARG, h), hd(banks[br], h), g, ALU.subtract, 0.0, ALU.min, tr)
                t = ts(hd(AR2, h), hd(banks[br], h), g, ALU.subtract, 0.0, ALU.max)
            psum.give(br, t)
            t1 = act(DT, ARG, ACT.Exp, t)
            t2 = act(Dm, AR2, ACT.Exp, t, scale=-1.0)
            t_qdt = AC(lambda e: e.copy(QDT, banks[bd][:, :]), td)
            psum.give(bd, t_qdt)
            t_dt = tt(PL, h3(DT), h3(DT), TRI.unsqueeze(1).broadcast_to((P, 4, P)), ALU.mult, t1)
            t_dm = tt(PL, h3(Dm), h3(Dm), kc(K_LOW).unsqueeze(1).broadcast_to((P, 4, P)), ALU.mult, t2)
            b1, f1 = psum.take()
            t = per_head(lambda h: (hd(KT, h), hd(KT, h)), b1, t_kt, *f1)
            for h in range(4):
                t_a = stt(hd(Am, h), hd(banks[b1], h), GB[:, c, h:h + 1], hd(Dm, h), ALU.mult, ALU.mult, t, t_dm)
            psum.give(b1, t_a)
            b2, f2 = psum.take()
            t = per_head(lambda h: (hd(KT, h), hd(QT, h)), b2, t_kt, t_qt, *f2)
            t_qk = tt(DV, QK, banks[b2][:, :], DT, ALU.mult, t, t_dt)
            psum.give(b2, t_qk)
            b3, f3 = psum.take()
            for h in range(4):
                t = PE(lambda e, h=h: e.transpose(hd(banks[b3], h), hd(Am, h), IDN), t_a, *f3)
            t_at = AC(lambda e: e.copy(AT, banks[b3][:, :]), t)
            psum.give(b3, t_at)
            t = stt(h3(X), h3(Am), -1.0, kc(K_M1).unsqueeze(1).broadcast_to((P, 4, P)), ALU.mult, ALU.mult, t_a)
            t_x = tt(DV, h3(X), h3(X), IDN.unsqueeze(1).broadcast_to((P, 4, P)), ALU.add, t)
            lvl = lambda n: kc(K_LV + (n - 1) * P).unsqueeze(1).broadcast_to((P, 4, P))
            b4, f4 = psum.take()
            for h in range(4):
                t = PE(lambda e, h=h: e.transpose(hd(banks[b4], h), hd(X, h), IDN), t_x, *f4)
            t_xx = AC(lambda e: e.copy(XX, banks[b4][:, :]), t)
            psum.give(b4, t_xx)
            t_use = t_at
            for n in range(1, 7):
                t_lt = tt(PL, h3(LT), h3(AT), lvl(n), ALU.mult, t_at, t_use)
                b1, f1 = psum.take()
                t = t_use = per_head(lambda h: (hd(LT, h), hd(X, h)), b1, t_lt, t_x, *f1)
                t_y = AC(lambda e, b1=b1: e.copy(Y, banks[b1][:, :]), t)
                psum.give(b1, t_y)
                if n < 6:
                    b2, f2 = psum.take()
                    t_m = per_head(lambda h: (hd(XX, h), hd(Y, h)), b2, t_y, t_xx, *f2)
                b3, f3 = psum.take()
                t_n = per_head(lambda h: (hd(Y, h), hd(XX, h)), b3, t_y, t_xx, *f3)
                if n < 6:
                    t_x = tt(DV, X, X, banks[b2][:, :], ALU.subtract, t_m)
                    psum.give(b2, t_x)
                t_xx = tt(DV, XX, XX, banks[b3][:, :], ALU.subtract, t_n)
                psum.give(b3, t_xx)
            bw, f1 = psum.take()
            t = per_head(lambda h: (hd(WB, h), hd(XX, h)), bw, t_xx, t_wb, *f1)
            t_wt = AC(lambda e: e.copy(WT, banks[bw][:, :]), t)
            psum.give(bw, t_wt)
            bv, f2 = psum.take()
            for h in range(4):
                t = PE(lambda e, h=h: e.matmul(hd(banks[bv], h), hd(XX, h), hd(UB, h), start=True, stop=(c == 0)),
                       t_xx, t_ub, *f2)
                if c:
                    t = PE(lambda e, h=h: e.matmul(hd(banks[bv], h), hd(WT, h), hd(ST, h), start=False, stop=True),
                           t_wt)
            t_vn = DV(lambda e: e.tensor_copy(VN, banks[bv][:, :]), t)
            psum.give(bv, t_vn)
            bo, f3 = psum.take()
            for h in range(4):
                t = PE(lambda e, h=h: e.matmul(hd(banks[bo], h), hd(QK, h), hd(VN, h), start=True, stop=(c == 0)),
                       t_vn, t_qk, *f3)
                if c:
                    t = PE(lambda e, h=h: e.matmul(hd(banks[bo], h), hd(QDT, h), hd(ST, h), start=False, stop=True),
                           t_qdt)
            t = AC(lambda e: e.copy(O[:, c, 512:1024], banks[bo][:, :]), t)
            psum.give(bo, t)
            if c < 3:
                bs, f4 = psum.take()
                t = per_head(lambda h: (hd(KD, h), hd(VN, h)), bs, t_vn, t_kd, *f4)
                if c == 0:
                    t = DV(lambda e: e.tensor_copy(ST, banks[bs][:, :]), t)
                else:
                    for h in range(4):
                        t0 = stt(hd(ST, h), hd(ST, h), EL[:, 4 * c + h:4 * c + h + 1], hd(banks[bs], h), ALU.mult,
                                 ALU.add, t)
                    t = t0
                psum.give(bs, t)
        fence()
        OS = sm(16)
        tprev = []
        for c in range(4):
            t = act(scr[0], O[:, c, 512:1024], ACT.Square, *tprev)
            t = DV(lambda e, c=c: e.tensor_reduce(OS[:, c * 4:(c + 1) * 4], h3(scr[0]), AX, ALU.add), t)
            tprev = [t]
        t = inv_root(OS, OS, 1.0 / P, t)
        ready = []
        for c in range(4):
            t1 = tt(DV, h3(O[:, c, 512:1024]), h3(O[:, c, 512:1024]), bc(OS, c), ALU.mult, t)
            ready.append([tt(PL, O[:, c, 512:1024], O[:, c, 512:1024], ZB[:, c, :], ALU.mult, t1)])
        tx = turn(lambda m, f: O[:, m, f * P:(f + 1) * P], 8, lambda f: XT[:, f, :], ready,
                  lambda f: 1.0 if f < 4 else cp(C_HNORM))
        return product_out(xm, 8, a["even_w_out"][0], a["norm_w"][0, 3:4], 1.0, tuple(tx))

    def odd(toks):
        w = a["odd_w_in"][0]
        Z = arena(0, 8192).rearrange("p (c d) -> p c d", c=4)
        XS = arena(8192, 8192).rearrange("p (c d) -> p c d", c=4)
        BT = arena(16384, 2048).rearrange("p (g s) -> p g s", s=S)
        CT = arena(18432, 2048).rearrange("p (g s) -> p g s", s=S)
        BK = SC[:, 2560:4608].rearrange("p (c d) -> p c d", c=4)
        small[0] = SM0
        DT = sm(128)
        AA = sm(128)
        tx = prenorm(4, *toks)
        xk = lambda k: XT[:, k, :]
        xm = lambda k, m: XT[:, k, m * P:(m + 1) * P]
        fence()
        later = Later(2)

        def use(j, b, t):
            n, t = conv(b, t, C_OCONV + 4 * j, C_OBIAS + j)

            def go():
                if j < 16:
                    tp, te = turn_block(n, t, XS[:, :, j * P:(j + 1) * P])
                elif j < 20:
                    tp, te = turn_block(n, t, BK[:, :, (j - 16) * P:(j - 15) * P])
                    tp = PL(lambda e: e.tensor_copy(BT[:, j - 16, :], scr[n]), t, tp)
                else:
                    tp = PL(lambda e: e.tensor_copy(CT[:, j - 20, :], scr[n]), t)
                cbuf.give(n, tp)
            later.add(go)
        gemm_t(xk, 8, w, 2048, 3072, use, *tx)
        later.flush()
        for q in range(4):
            def use_z(m, b, t, q=q):
                t = act(Z[:, m, q * 512:(q + 1) * 512], banks[b][:, :], ACT.Silu, t)
                psum.give(b, t)
            gemm(xm, 8, w, q * 512, 512, use_z)
        D3 = DT.rearrange("p (c h) -> p c h", c=4)
        A3 = AA.rearrange("p (c h) -> p c h", c=4)

        def use_dt(m, b, t):
            t = tt(DV, D3[:, m, :], banks[b][:, 0:32], rp(R_ODT, 32), ALU.add, t)
            psum.give(b, t)
        gemm(xm, 8, w, 5120, 32, use_dt)
        fence()
        s1, s2, s3, e32 = sm(128), sm(128), sm(128), sm(32)
        t = softplus(DT, s1, s2, s3)
        t1 = act(e32, rp(R_OA, 32), ACT.Exp)
        t = stt(A3, D3, -1.0, e32.unsqueeze(1).broadcast_to((P, 4, 32)), ALU.mult, ALU.mult, t, t1)
        AC_, EA, ET, ED = s1, s2, s3, sm(128)
        b, fr = psum.take()
        PE(lambda e: e.matmul(banks[b][:, 0:128], TRI, AA, start=True, stop=True), t, *fr)
        t = PE(lambda e: e.matmul(banks[b][:, 128:256], ONE, AA, start=True, stop=True))
        t1 = DV(lambda e: e.tensor_copy(AC_, banks[b][:, 0:128]), t)
        t2 = act(EA, AC_, ACT.Exp, t1)
        t3 = act(ET, banks[b][:, 128:256], ACT.Exp, t1)
        t4 = tt(DV, ED, banks[b][:, 128:256], AC_, ALU.subtract, t3)
        psum.give(b, t4)
        act(ED, ED, ACT.Exp, t4)
        fence()
        XD = [XTt[:, 0:512], XTt[:, 512:1024]]
        XE = [XTt[:, 1024:1536], XTt[:, 1536:2048]]
        HS = XTt[:, 2048:4096].rearrange("p (g d) -> p g d", g=4)
        xbuf = Slots([0, 1])
        mbuf = Slots([0, 1, 2])
        MT = [scr[0], scr[1], scr[2]]
        YB = [scr[3], scr[4]]
        ybuf = Slots([0, 1])
        cbm = Slots([0, 1])
        CB = sm(256)
        p8 = lambda x: x.rearrange("p (h d) -> p h d", d=64)
        h3 = lambda x: x.rearrange("p (h d) -> p h d", d=P)
        st = {}
        hs_t = {g: () for g in range(4)}

        def first(u):
            c, g = u["c"], u["g"]
            xi, fx = xbuf.take()
            h8 = c * 32 + g * 8
            bc = lambda x: x[:, h8:h8 + 8].unsqueeze(2).broadcast_to((P, 8, 64))
            xs = XS[:, c, g * 512:(g + 1) * 512]
            u["xi"] = xi
            t = u["t_xd"] = tt(PL, p8(XD[xi]), p8(xs), bc(DT), ALU.mult, *fx)
            u["t_xe"] = tt(PL, p8(XE[xi]), p8(XD[xi]), bc(ED), ALU.mult, t)
            ci, fc = cbm.take()
            u["ci"] = ci
            b, fr = psum.take()
            t = PE(lambda e: e.matmul(banks[b][:, 0:P], BT[:, g, c * P:(c + 1) * P], CT[:, g, c * P:(c + 1) * P],
                                      start=True, stop=True), *fr)
            cb = CB[:, ci * P:(ci + 1) * P]
            t_cb = tt(DV, cb, banks[b][:, 0:P], TRI, ALU.mult, t, *fc)
            psum.give(b, t_cb)
            u["mt"] = []
            for hh in range(2):
                b, fr = psum.take()
                for x in range(4):
                    k = h8 + hh * 4 + x
                    t = PE(lambda e, x=x, k=k, b=b: e.matmul(banks[b][:, x * P:(x + 1) * P],
                                                             AA[:, k:k + 1].broadcast_to((P, P)), TRI, start=True,
                                                             stop=True), *fr)
                mi, fm = mbuf.take()
                for x in range(4):
                    k = h8 + hh * 4 + x
                    t1 = ts(MT[mi][:, x * P:(x + 1) * P], banks[b][:, x * P:(x + 1) * P], AC_[:, k:k + 1],
                            ALU.subtract, 0.0, ALU.min, t, *fm)
                psum.give(b, t1)
                t1 = act(MT[mi], MT[mi], ACT.Exp, t1)
                t1 = tt(DV, h3(MT[mi]), h3(MT[mi]), cb.unsqueeze(1).broadcast_to((P, 4, P)), ALU.mult, t1, t_cb)
                u["mt"].append((mi, t1))
                if hh == 0:
                    self_y(u, 0)
            self_y(u, 1)
            cbm.give(ci, u["mt"][1][1])

        def self_y(u, hh):
            if hh == 0:
                u["yb"], u["yfr"] = psum.take()
            xi = u["xi"]
            mi, tm = u["mt"][hh]
            for x in range(4):
                hx = hh * 4 + x
                t = PE(lambda e, x=x, hx=hx: e.matmul(banks[u["yb"]][:, hx * 64:(hx + 1) * 64],
                                                      MT[mi][:, x * P:(x + 1) * P], XD[xi][:, hx * 64:(hx + 1) * 64],
                                                      start=True, stop=True), tm, u["t_xd"], *u["yfr"])
            mbuf.give(mi, t)
            u["t_y"] = t

        def second(u):
            c, g, xi = u["c"], u["g"], u["xi"]
            h8 = c * 32 + g * 8
            bc = lambda x: x[:, h8:h8 + 8].unsqueeze(2).broadcast_to((P, 8, 64))
            yi, fy = ybuf.take()
            y = YB[yi]
            xs = XS[:, c, g * 512:(g + 1) * 512]
            if c:
                b, fr = psum.take()
                t = t_off = PE(lambda e: e.matmul(banks[b][:, :], CT[:, g, c * P:(c + 1) * P], HS[:, g, :], start=True,
                                          stop=True), *fr, *hs_t[g])
                t = tt(DV, p8(y), p8(banks[b][:, :]), bc(EA), ALU.mult, t, *fy)
                psum.give(b, t)
                t = tt(DV, y, banks[u["yb"]][:, :], y, ALU.add, t, u["t_y"])
            else:
                t_off = u["t_y"]
                t = DV(lambda e: e.tensor_copy(y, banks[u["yb"]][:, :]), u["t_y"], *fy)
            psum.give(u["yb"], t)
            t1 = tt(PL, p8(xs), p8(xs), rp(R_DSK + g * 8, 8).unsqueeze(2).broadcast_to((P, 8, 64)), ALU.mult, u["t_xd"])
            t1 = tt(PL, y, y, xs, ALU.add, t, t1)
            zz = Z[:, c, g * 512:(g + 1) * 512]
            t1 = tt(PL, zz, zz, y, ALU.mult, t1)
            ybuf.give(yi, t1)
            tl = u["t_y"]
            if c < 3:
                b, fr = psum.take()
                tl = t = PE(lambda e: e.matmul(banks[b][:, :], BK[:, c, g * P:(g + 1) * P], XE[xi], start=True, stop=True),
                            u["t_xe"], *fr)
                hv = HS[:, g, :]
                if c:
                    t2 = tt(DV, p8(hv), p8(hv), bc(ET), ALU.mult, t_off, *hs_t[g])
                    t2 = tt(DV, hv, banks[b][:, :], hv, ALU.add, t, t2)
                else:
                    t2 = DV(lambda e: e.tensor_copy(hv, banks[b][:, :]), t)
                psum.give(b, t2)
                hs_t[g] = (t2,)
            xbuf.give(xi, tl, u["t_xe"])

        units = [dict(c=c, g=g) for c in range(4) for g in range(4)]
        for x in range(17):
            if x < 16:
                first(units[x])
            if x:
                second(units[x - 1])
        fence()
        YS = sm(16)
        sq = Slots([0, 1])
        for c in range(4):
            for g in range(4):
                n, fr = sq.take()
                t = AC(lambda e, c=c, g=g, n=n: e.activation(scr[n], Z[:, c, g * 512:(g + 1) * 512], ACT.Square,
                                                             accum_out=YS[:, c * 4 + g:c * 4 + g + 1]), *fr)
                sq.give(n, t)
        t = inv_root(YS, YS, 1.0 / 512, t)
        ready = []
        for c in range(4):
            z4 = Z[:, c, :].rearrange("p (g d) -> p g d", g=4)
            ready.append([tt(DV, z4, z4, YS[:, c * 4:c * 4 + 4].unsqueeze(2).broadcast_to((P, 4, 512)), ALU.mult, t)])
        YT = arena(8192, 8192).rearrange("p (f s) -> p f s", s=S)
        tx = turn(lambda m, f: Z[:, m, f * P:(f + 1) * P], 16, lambda f: YT[:, f, :], ready,
                  lambda f: cp(C_ONORM + f))
        return product_out(lambda k, m: YT[:, k, m * P:(m + 1) * P], 16, a["odd_w_out"][0], a["norm_w"][1, 3:4], 1.0,
                           tuple(tx))

    def mixer2(l, toks):
        w = a["w_in_2"][l]
        r0 = R_L + l * L_N
        PJ = arena(0, 4 * Q_N).rearrange("p (c d) -> p c d", c=4)
        QT = arena(4 * Q_N, 8704).rearrange("p (f s) -> p f s", s=S)
        small[0] = SM0
        tx = prenorm(6 + 2 * l, *toks)
        xm = lambda k, m: XT[:, k, m * P:(m + 1) * P]
        fence()
        for c0 in range(0, Q_N, 512):
            n = min(512, Q_N - c0)

            def use(m, b, t, c0=c0, n=n):
                psum.give(b, evac(PJ[:, m, c0:c0 + n], banks[b][:, 0:n], t))
            gemm(xm, 8, w, c0, n, use, tuple(tx))
        fence()
        wr = sm(64 + 64 + 32 + 32 + 64 + 64)
        wo = 0
        wv = {}
        for name, src, n, f in (("fq", L_FQ, 64, 0.125), ("fk", L_FK, 64, 1.0), ("dq", L_DQ, 32, 32.0 ** -0.5),
                                ("dk", L_DK, 32, 1.0), ("sq", L_SQ, 64, 0.125), ("sk", L_SK, 64, 1.0)):
            wv[name] = wr[:, wo:wo + n]
            ts(wv[name], rp(r0 + src, n), f, ALU.mult, None, None)
            wo += n
        lam_init = 0.8 - 0.6 * float(np.exp(-0.3 * l))
        ld, lj = sm(4), sm(32)
        for k, (x, y) in enumerate(((L_LQ1, L_LK1), (L_LQ2, L_LK2))):
            t = DV(lambda e, k=k, x=x, y=y: e.tensor_tensor_reduce(lj, rp(r0 + x, 32), rp(r0 + y, 32), 1.0, 0.0,
                                                                   ALU.mult, ALU.add, ld[:, k:k + 1]), DV.now())
        t = act(ld[:, 0:2], ld[:, 0:2], ACT.Exp, t)
        t = tt(DV, ld[:, 2:3], ld[:, 1:2], ld[:, 0:1], ALU.subtract, t)
        ts(ld[:, 2:3], ld[:, 2:3], -lam_init, ALU.add, None, None, t)
        NS = sm(140).rearrange("p (c h) -> p c h", c=4)
        qbuf = SC[:, 0:3584]
        sq = Slots([0, 1])
        sz = {0: SC[:, 0:768], 1: SC[:, 768:1536]}
        for c in range(4):
            for off, nh, dh, o in ((Q_FQ, 12, 64, 0), (Q_DQ, 16, 32, 12), (Q_SQ, 7, 64, 28)):
                n, fr = sq.take()
                v = sz[n][:, 0:nh * dh]
                t = act(v, PJ[:, c, off:off + nh * dh], ACT.Square, *fr)
                t = DV(lambda e, v=v, c=c, nh=nh, dh=dh, o=o: e.tensor_reduce(
                    NS[:, c, o:o + nh], v.rearrange("p (h d) -> p h d", d=dh), AX, ALU.add), t)
                sq.give(n, t)
        t = ts(NS[:, :, 12:28], NS[:, :, 12:28], 2.0, ALU.mult, None, None, t)
        nsf = NS.rearrange("p c h -> p (c h)")
        t = inv_root(nsf, nsf, 1.0 / 64, t)
        for c in range(4):
            for off, nh, dh, o, ws in ((Q_FQ, 12, 64, 0, (("fq", 6), ("fk", 6))), (Q_DQ, 16, 32, 12, (("dq", 8), ("dk", 8))),
                                       (Q_SQ, 7, 64, 28, (("sq", 6), ("sk", 1)))):
                v = PJ[:, c, off:off + nh * dh].rearrange("p (h d) -> p h d", d=dh)
                t1 = tt(DV, v, v, NS[:, c, o:o + nh].unsqueeze(2).broadcast_to((P, nh, dh)), ALU.mult, t)
                h = 0
                for name, k in ws:
                    vv = v[:, h:h + k, :]
                    tt(PL, vv, vv, wv[name].unsqueeze(1).broadcast_to((P, k, dh)), ALU.mult, t1)
                    h += k
        fence()
        T4 = [SC[:, i * 280:(i + 1) * 280] for i in range(4)]
        for off, nh, dh, kr in ((Q_DQ, 16, 32, K_R32), (Q_SQ, 7, 64, K_R64), (Q_IQ, 5, 64, K_R64)):
            hf = dh // 8
            cs = kc(kr, 4 * hf).rearrange("p (c d) -> p c d", c=4)
            sn = kc(kr + 4 * hf, 4 * hf).rearrange("p (c d) -> p c d", c=4)
            v = [PJ[:, c, off:off + nh * dh].rearrange("p (h d) -> p h d", d=dh) for c in range(4)]
            t0 = DV.now()
            for c in range(4):
                x1, x2 = v[c][:, :, 0:hf], v[c][:, :, hf:2 * hf]
                cc = cs[:, c, :].unsqueeze(1).broadcast_to((P, nh, hf))
                sn_ = sn[:, c, :].unsqueeze(1).broadcast_to((P, nh, hf))
                tv = [x[:, c * nh * hf - c * nh * hf + c * 70:c * 70 + nh * hf].rearrange("p (h d) -> p h d", d=hf) for x in T4] \
                    if nh * hf <= 70 else None
                tt(DV, tv[0], x1, cc, ALU.mult, t0)
                tt(DV, tv[1], x2, sn_, ALU.mult)
                tt(DV, tv[2], x2, cc, ALU.mult)
                t = tt(DV, tv[3], x1, sn_, ALU.mult)
                tt(DV, x1, tv[0], tv[1], ALU.subtract, t)
                t = tt(DV, x2, tv[2], tv[3], ALU.add)
        KD = SC[:, 1120:2144].rearrange("p (c d) -> p c d", c=4)
        for c in range(4):
            for k, off in ((0, Q_SK), (64, Q_SK), (128, Q_IK), (192, Q_IK)):
                DV(lambda e, c=c, k=k, off=off: e.tensor_copy(KD[:, c, k:k + 64], PJ[:, c, off:off + 64]), t)
        FG = sm(24)
        F3 = FG.rearrange("p (c h) -> p c h", c=4)
        IW = sm(16)
        I3 = IW.rearrange("p (c h) -> p c h", c=4)
        s1, s2, s3 = sm(24), sm(24), sm(24)
        t = tt(DV, F3, PJ[:, :, Q_FF:Q_FF + 6], rp(r0 + L_FB, 6).unsqueeze(1).broadcast_to((P, 4, 6)), ALU.add)
        t = ts(FG, FG, -1.0, ALU.mult, None, None, t)
        t = softplus(FG, s1, s2, s3, t)
        t_f = ts(FG, FG, -1.0, ALU.mult, None, None, t)
        ts(I3, PJ[:, :, Q_IW:Q_IW + 4], 0.5, ALU.mult, None, None)
        fence()
        blocks = [lambda m, k=k: PJ[:, m, k:k + P] for k in (Q_FQ, Q_FQ + 128, Q_FQ + 256, Q_FK, Q_FK + 128, Q_FK + 256,
                                                             Q_DQ, Q_DQ + 128, Q_DK, Q_DK + 128, Q_SQ, Q_SQ + 128,
                                                             Q_SQ + 256)]
        blocks += [lambda m: KD[:, m, 0:128], lambda m: PJ[:, m, Q_IQ:Q_IQ + 128],
                   lambda m: PJ[:, m, Q_IQ + 128:Q_IQ + 256], lambda m: KD[:, m, 128:256]]
        turn(lambda m, f: blocks[f](m), 17, lambda f: QT[:, f, :], [(), (), (), ()])
        fence()
        FQ, FK, DQ, DK, SQ, SK, IQ, IK = 0, 3, 6, 8, 10, 13, 14, 16
        CG = sm(24)
        b, fr = psum.take()
        for i in range(4):
            for j in range(i + 1):
                t = PE(lambda e, i=i, j=j: e.matmul(banks[b][:, i * 6:i * 6 + 6], TRI if j == i else ONE,
                                                    F3[:, j, :], start=(j == 0), stop=(j == i)), *fr)
        t = DV(lambda e: e.tensor_copy(CG, banks[b][:, 0:24]), t)
        psum.give(b, t)
        for h in range(6):
            b, fr = psum.take()
            for i in range(4):
                for j in range(i + 1):
                    t = PE(lambda e, i=i, j=j, h=h, b=b: e.matmul(
                        banks[b][:, i * P:(i + 1) * P], F3[:, j, h:h + 1].broadcast_to((P, P)),
                        TRI if j == i else ONE, start=(j == 0), stop=(j == i)), *fr)
            t = AC(lambda e, h=h, b=b: e.mul(PJ[:, :, h * P:(h + 1) * P],
                                             banks[b][:, :].rearrange("p (c s) -> p c s", c=4), -1.0), t)
            psum.give(b, t)
        fence()
        rb = Slots([0, 1, 2])
        b3 = lambda x: x.rearrange("p (c s) -> p c s", s=P)
        sel = {}
        for i in (1, 2, 3):
            W = (i + 1) * P
            acc = sel[i] = PJ[:, 0:i + 1, Q_DQ + (i - 1) * P:Q_DQ + i * P]
            ta = []
            for h in range(4):
                rr = 64 * (h % 2)
                b, fr = psum.take()
                t = PE(lambda e, b=b, h=h, rr=rr, i=i, W=W: e.matmul(
                    banks[b][:, 0:W], QT[rr:rr + 64, IQ + h // 2, i * P:(i + 1) * P], QT[rr:rr + 64, IK, 0:W],
                    start=True, stop=True), *fr)
                n, fn = rb.take()
                t = act(scr[n][:, 0:W], banks[b][:, 0:W], ACT.Relu, t, *fn, scale=0.125)
                psum.give(b, t)
                if h == 0:
                    t = ts(acc, b3(scr[n][:, 0:W]), I3[:, i, 0:1], ALU.mult, None, None, t)
                else:
                    t = stt(acc, b3(scr[n][:, 0:W]), I3[:, i, h:h + 1], acc, ALU.mult, ALU.add, t, *ta)
                ta = [t]
                rb.give(n, t)
            tt(DV, acc, acc, b3(kc(K_CAUS + 512 - W, W)), ALU.add, *ta)
        m8 = sm(24)
        ti = {i: DV.now() for i in (1, 2, 3)}
        for k in range(16):
            for i in (1, 2, 3):
                mv = m8[:, (i - 1) * 8:i * 8]
                ti[i] = DV(lambda e, i=i, mv=mv: e.max(mv, sel[i]), ti[i])
            for i in (1, 2, 3):
                mv = m8[:, (i - 1) * 8:i * 8]
                ti[i] = DV(lambda e, i=i, mv=mv: e.match_replace(sel[i], mv, sel[i], LOW), ti[i])
        for i in (1, 2, 3):
            ti[i] = ts(sel[i], sel[i], -2e38, ALU.is_gt, -BIG, ALU.mult, ti[i])
        fence()
        O = XTt[:, :].rearrange("p (m d) -> p m d", m=4)
        units = []
        mk = Slots([0, 1])
        fmv = [WRt[:, 0:512], WRt[:, 512:1024]]
        dtmp = [PJ[:, k, Q_IQ:Q_IQ + 256].rearrange("p (h d) -> p h d", d=64) for k in range(2)]
        Q3 = lambda f, rr, n, i: QT[rr:rr + n, f, i * P:(i + 1) * P]
        for i in range(4):
            W = (i + 1) * P
            caus = kc(K_CAUS + 512 - W, W)

            def done_f(bank, r, t, tr, i=i):
                return scale_heads(O[:, i, 0:384].rearrange("p (h d) -> p h d", d=64), bank, r, 6, 0, t, tr)

            def done_s(bank, r, t, tr, i=i):
                return scale_heads(O[:, i, 640:1024].rearrange("p (h d) -> p h d", d=64), bank, r, 6, 0, t, tr)

            def done_d(bank, r, t, tr, i=i):
                r2 = r.rearrange("p (h m) -> p h m", m=2)
                x = dtmp[i % 2]
                ov = O[:, i, 384:640].rearrange("p (h d) -> p h d", d=64)
                bv = bank[:, :].rearrange("p (h m d) -> p h m d", m=2, d=64)
                t1 = ts(r2[:, :, 1], r2[:, :, 1], ld[:, 2:3], ALU.mult, None, None, tr)
                t2 = tt(DV, ov, bv[:, :, 0, :], r2[:, :, 0].unsqueeze(2).broadcast_to((P, 4, 64)), ALU.mult, t, tr)
                t1 = tt(DV, x, bv[:, :, 1, :], r2[:, :, 1].unsqueeze(2).broadcast_to((P, 4, 64)), ALU.mult, t1, t)
                return tt(DV, ov, ov, x, ALU.add, t1, t2)

            for h in range(6):
                rr = 64 * (h % 2)

                def mask(h=h, i=i, W=W, caus=caus):
                    n, fr = mk.take()
                    v = fmv[n][:, 0:W].rearrange("p (c s) -> p c s", s=P)
                    t = stt(v, PJ[:, 0:i + 1, h * P:(h + 1) * P], CG[:, i * 6 + h:i * 6 + h + 1],
                            caus.rearrange("p (c s) -> p c s", s=P), ALU.add, ALU.add, *fr)
                    return fmv[n][:, 0:W], (t,)

                def free(t, cnt=[0], i=i, h=h):
                    mk.give((6 * i + h) % 2, t)
                units.append(dict(i=i, q=Q3(FQ + h // 2, rr, 64, i), k=QT[rr:rr + 64, FK + h // 2, 0:W], mask=mask,
                                  free=free, times=None,
                                  values=lambda kb, h=h: PJ[:, kb, Q_FV + h * 64:Q_FV + h * 64 + 64], slot=h,
                                  done=done_f if h == 5 else None))
            for x in range(8):
                rr = 32 * (x % 4)
                units.append(dict(i=i, q=Q3(DQ + x // 4, rr, 32, i), k=QT[rr:rr + 32, DK + x // 4, 0:W], mask=caus,
                                  times=None, values=lambda kb, x=x: PJ[:, kb, Q_DV + (x // 2) * 64:Q_DV + (x // 2) * 64 + 64],
                                  slot=x, done=done_d if x == 7 else None))
            for h in range(6):
                rr = 64 * (h % 2)
                units.append(dict(i=i, q=Q3(SQ + h // 2, rr, 64, i), k=QT[rr:rr + 64, SK, 0:W],
                                  mask=sel[i] if i else caus, times=None,
                                  values=lambda kb: PJ[:, kb, Q_SV:Q_SV + 64], slot=h,
                                  done=done_s if h == 5 else None))
        attention(units)
        fence()
        NO = sm(16)
        tprev = []
        for c in range(4):
            t = act(scr[0][:, 0:256], O[:, c, 384:640], ACT.Square, *tprev)
            t = DV(lambda e, c=c: e.tensor_reduce(NO[:, c * 4:c * 4 + 4], scr[0][:, 0:256].rearrange("p (h d) -> p h d", d=64),
                                                  AX, ALU.add), t)
            tprev = [t]
        t = inv_root(NO, NO, 1.0 / 64, t, factor=1.0 - lam_init)
        ready = []
        for c in range(4):
            v = O[:, c, 384:640].rearrange("p (h d) -> p h d", d=64)
            t1 = tt(DV, v, v, NO[:, c * 4:c * 4 + 4].unsqueeze(2).broadcast_to((P, 4, 64)), ALU.mult, t)
            ready.append([tt(PL, v, v, rp(r0 + L_SUB, 64).unsqueeze(1).broadcast_to((P, 4, 64)), ALU.mult, t1)])
        OT = arena(0, 4096).rearrange("p (f s) -> p f s", s=S)
        tx = turn(lambda m, f: O[:, m, f * P:(f + 1) * P], 8, lambda f: OT[:, f, :], ready)
        return product_out(lambda k, m: OT[:, k, m * P:(m + 1) * P], 8, a["w_out_2"][l], None, None, tuple(tx))

    SM0 = small[0]
    steps = []
    nw = a["norm_w"]
    for l in range(2):
        fw = [[a[n][l, s] for n in ("ffn_w_gate", "ffn_w_up", "ffn_w_down")] for s in range(2)]
        steps.append(lambda t, l=l, fw=fw: ffn(3 * l, *fw[0], nw[l, 1:2], 0.5, t))
        steps.append(even if l == 0 else odd)
        steps.append(lambda t, l=l, fw=fw: ffn(3 * l + 2, *fw[1], nw[l, 5:6], 0.5, t))
    for l in range(2):
        steps.append(lambda t, l=l: mixer2(l, t))
        gu = a["w_gate_up_2"][l]
        steps.append(lambda t, l=l, gu=gu: ffn(7 + 2 * l, gu[:, 0:FF], gu[:, FF:2 * FF], a["w_down_2"][l], None, None, t))
    toks = [T_IN]
    for n, step in enumerate(steps[:upto]):
        toks = step(toks)
        fence()
    n_out = 1
    SP.quiet(lambda e: e.dma_start(out.rearrange("b (m p) d -> p (b m) d", p=P), H).then_inc(s_out, 16), *toks)
    SP.wait((s_out, 16))


def constants():
    p = np.arange(P)
    c = np.zeros((P, K_N), np.float32)
    c[:, K_ID:K_ID + P] = np.eye(P)
    c[:, K_TRI:K_TRI + P] = p[:, None] <= p[None, :]
    c[:, K_ONE:K_ONE + P] = 1
    c[:, K_LOW:K_LOW + P] = p[None, :] < p[:, None]

    def level(b):
        i, j = p[:, None], p[None, :]
        return ((i // (2 * b) == j // (2 * b)) & ((i // b) % 2 == 1) & ((j // b) % 2 == 0)).astype(np.float32)
    c[:, K_M1:K_M1 + P] = level(1)
    for n in range(1, 7):
        c[:, K_LV + (n - 1) * P:K_LV + n * P] = level(2 ** n).T
    delta = p[:, None] - (np.arange(512)[None, :] - 384)
    c[:, K_CAUS:K_CAUS + 512] = np.where(delta >= 0, 0.0, -BIG)
    times = ((delta >= 0) & (delta <= 128)).astype(np.float32) + ((delta >= 0) & (delta % 4 == 0)) \
        + ((delta >= 0) & (delta % 16 == 0))
    c[:, K_CM:K_CM + 512] = times
    for k0, dh in ((K_R64, 64), (K_R32, 32)):
        rot = dh // 4
        inv = (np.float32(1.0) / np.power(np.float32(500000.0), np.arange(0, rot, 2, dtype=np.float32) / np.float32(rot))
               ).astype(np.float32)
        ang = np.arange(S, dtype=np.float32)[:, None] * inv[None, :]
        for k, f in ((0, np.cos), (1, np.sin)):
            v = f(ang).astype(np.float32).reshape(4, P, rot // 2).transpose(1, 0, 2).reshape(P, -1)
            c[:, k0 + k * v.shape[1]:k0 + (k + 1) * v.shape[1]] = v
    return c


WHOLE = ["x", "norm_w", "ffn_w_gate", "ffn_w_up", "ffn_w_down", "even_w_in", "even_w_out", "odd_w_in", "odd_w_out",
         "w_in_2", "w_out_2", "w_gate_up_2", "w_down_2"]


def pack(inputs):
    v = {k: np.asarray(x) for k, x in inputs.items()}
    arrays = {k: np.ascontiguousarray(v[k]) for k in WHOLE}
    cols = []
    for x in (v["norm_w"][0, 0], v["norm_w"][0, 2], v["norm_w"][0, 4], v["norm_w"][1, 0], v["norm_w"][1, 2],
              v["norm_w"][1, 4], v["attn_norm_2"][0], v["ffn_norm_2"][0], v["attn_norm_2"][1], v["ffn_norm_2"][1]):
        cols.append(x.reshape(8, P).T)
    for x, n in ((v["even_conv_w"][0], 12), (v["odd_conv_w"][0], 24)):
        cols.append(x.reshape(4, n, P).transpose(2, 1, 0).reshape(P, -1))
    cols.append(v["odd_conv_b"][0].reshape(24, P).T)
    cols.append(v["odd_out_norm_w"][0].reshape(16, P).T)
    cols.append(v["even_head_norm_w"][0][:, None])
    arrays["colp"] = np.ascontiguousarray(np.concatenate(cols, axis=1))
    rows = [v["even_a_log"][0], v["even_dt_bias"][0], v["odd_a_log"][0], v["odd_dt_bias"][0], v["odd_d_skip"][0]]
    for l in range(2):
        rows += [v[n + "_2"][l] for n in ("fox_fb", "fox_qn", "fox_kn", "diff_qn", "diff_kn", "diff_subln", "dsa_qn",
                                          "dsa_kn", "diff_lq1", "diff_lk1", "diff_lq2", "diff_lk2")]
    arrays["rowp"] = np.ascontiguousarray(np.concatenate(rows)[None, :])
    arrays["consts"] = constants()
    return arrays


def program(nc, arrays, upto=99):
    a = {k: nc.dram_tensor("in_" + k, list(x.shape), F32, kind="ExternalInput").ap() for k, x in arrays.items()}
    out = nc.dram_tensor("out_y", [1, S, D], F32, kind="ExternalOutput").ap()
    build(nc, a, out, upto)


def kernel(**inputs):
    import concourse.bacc as bacc
    from concourse.bass_utils import run_bass_kernel_spmd

    nc = bacc.Bacc("TRN2", target_bir_lowering=False, num_devices=1)
    arrays = pack(inputs)
    program(nc, arrays)
    r = run_bass_kernel_spmd(nc, [{"in_" + k: x for k, x in arrays.items()}], core_ids=[0])
    return r.results[0]["out_y"]
```

```python
import numpy as np
from contextlib import ExitStack

import concourse.bass as bass
from concourse import mybir
from concourse.alu_op_type import AluOpType as ALU

ACT = mybir.ActivationFunctionType
F32 = mybir.dt.float32
F32R = mybir.dt.float32r
AX = mybir.AxisListType.X

P = 128
S = 512
D = 1024
FF = 2816
NJ = FF // P
EPS = 1e-6
BIG = 1e30
LOW = -3e38
RAW = 4
SPL = 3
SLOT = 1024
AHEAD = 2

C_PRE, C_ECONV, C_OCONV, C_OBIAS, C_ONORM, C_HNORM, C_N = 0, 80, 128, 224, 248, 264, 265
R_EA, R_EDT, R_OA, R_ODT, R_DSK, R_L = 0, 4, 8, 40, 72, 104
L_FB, L_FQ, L_FK, L_DQ, L_DK, L_SUB, L_SQ, L_SK, L_LQ1, L_LK1, L_LQ2, L_LK2, L_N = (
    0, 6, 70, 134, 166, 198, 262, 326, 390, 422, 454, 486, 518)
R_N = R_L + 2 * L_N
K_ID, K_TRI, K_ONE, K_LOW, K_CAUS, K_R64, K_R32, K_N = (0, 128, 256, 384, 512, 1024, 1088, 1120)
E_M1, E_LV, E_CM, E_N = 0, 128, 896, 1408
Q_FQ, Q_FK, Q_FV, Q_FF, Q_DQ, Q_DK, Q_DV, Q_SQ, Q_SK, Q_SV, Q_IQ, Q_IK, Q_IW, Q_N = (
    0, 384, 768, 1152, 1158, 1414, 1670, 1926, 2310, 2374, 2438, 2694, 2758, 2762)


class Queue:

    def __init__(self, sem, engine):
        self.sem, self.n, self.engine, self.seen = sem, 0, engine, {}

    def wait(self, *toks):
        need = {}
        for sem, v in toks:
            if v > self.seen.get(id(sem), 0) and v > need.get(id(sem), (sem, 0))[1]:
                need[id(sem)] = (sem, v)
        for sem, v in need.values():
            self.seen[id(sem)] = v
            if self.engine is not None:
                self.engine.wait_ge(sem, v)

    def quiet(self, fn, *toks):
        self.wait(*toks)
        if self.engine is not None:
            fn(self.engine)

    def __call__(self, fn, *toks):
        self.wait(*toks)
        self.n += 1
        if self.engine is not None:
            fn(self.engine).then_inc(self.sem, 1)
        return (self.sem, self.n)

    def now(self):
        return (self.sem, self.n)


class Slots:

    def __init__(self, items):
        self.free = [(x, ()) for x in items]

    def take(self):
        return self.free.pop(0)

    def give(self, item, *toks):
        self.free.append((item, toks))


def build(nc, a, out, upto=99):
    ctx = ExitStack()
    with ctx:
        def sb(name, n):
            return ctx.enter_context(nc.sbuf_tensor(name, [P, n], F32))

        def sem(name):
            return ctx.enter_context(nc.semaphore(name))

        plan = (("H", 4 * D), ("X", 8192), ("W", RAW * SLOT), ("WS", SPL * 2 * SLOT), ("AR", 25088), ("CP", C_N + 7),
                ("RP", R_N + 4), ("KC", K_N), ("WR", D), ("SM", 1600))
        base = -(-nc.sbuf_base // 32) * 32
        sb("all", sum(n for _, n in plan) + 8)
        at, place = base, {}
        for name, n in plan:
            place[name] = at
            assert n % 8 == 0
            at += 4 * n
        size = dict(plan)

        def put(name, where, dt):
            return nc.alloc_sbuf_tensor_at(name, [P, size[where]], dt, offset=place[where])

        Ht, Xf, Wt, AR, CPt, RPt, KCt, WRt, SMt = (put("f_" + n, n, F32) for n in (
            "H", "X", "W", "AR", "CP", "RP", "KC", "WR", "SM"))
        Xr, WSr, ARr = (put("r_" + n, n, F32R) for n in ("X", "WS", "AR"))
        banks = [ctx.enter_context(nc.psum_tensor(f"ps{i}", [P, 512], F32)) for i in range(8)]
        wsem = [sem(f"ws{i}") for i in range(RAW)]
        rsem = sem("wr0")
        s_in = sem("s_in")
        s_out = sem("s_out")
        sems = [sem(n) for n in ("s_pe", "s_dv", "s_ac", "s_pl", "s_sp")]
        s_ev = sem("s_ev")
        mem = (Ht, Xf, Xr, Wt, WSr, AR, ARr, CPt, RPt, KCt, WRt, SMt, banks, wsem, rsem, s_in, s_ev, s_out, sems)
        order = []
        schedule(a, out, mem, None, None, upto, order, True)
        block = ctx.enter_context(nc.Block())

        @block.sync
        def _(e):
            schedule(a, out, mem, 4, e, upto, order, False)

        @block.tensor
        def _(e):
            schedule(a, out, mem, 0, e, upto, order, False)

        @block.vector
        def _(e):
            schedule(a, out, mem, 1, e, upto, order, False)

        @block.scalar
        def _(e):
            schedule(a, out, mem, 2, e, upto, order, False)

        @block.gpsimd
        def _(e):
            schedule(a, out, mem, 3, e, upto, order, False)


def schedule(a, out, mem, turn_of, engine, upto, order, listing):
    Ht, Xf, Xr, Wt, WSr, AR, ARr, CPt, RPt, KCt, WRt, SMt, banks, wsem, rsem, s_in, s_ev, s_out, sems = mem
    H = Ht[:, :].rearrange("p (m d) -> p m d", m=4)
    XTt = Xf[:, 0:4096]
    SC = AR[:, 20480:25088]
    XH = Xr[:, 0:4096].rearrange("p (f s) -> p f s", s=S)
    XL = Xr[:, 4096:8192].rearrange("p (f s) -> p f s", s=S)
    psum = Slots(range(8))
    raw = Slots(range(RAW))
    split = Slots(range(SPL))
    wcnt = [0] * RAW
    rcnt = [0]
    rows = Slots([0])
    ready_w = []
    asked = [0]
    PE, DV, AC, PL, SP = (Queue(x, engine if k == turn_of else None) for k, x in enumerate(sems))

    def cp(c, n=1):
        return CPt[:, c:c + n]

    def rp(c, n):
        return RPt[:, c:c + n]

    def kc(c, n=128):
        return KCt[:, c:c + n]

    IDN = kc(K_ID)
    TRI = kc(K_TRI)
    ONE = kc(K_ONE)

    def arena(off, n):
        return AR[:, off:off + n]

    small = [0]

    def sm(n):
        o = small[0]
        small[0] += n
        assert small[0] <= 1600
        return SMt[:, o:o + n]

    def fence():
        t = [q.now() for q in (PE, DV, AC, PL)]
        for q in (PE, DV, AC, PL):
            q.wait(*t)

    flip = [0]

    def evac(dst, src, *toks, scale=None):
        flip[0] ^= 1
        if flip[0]:
            if scale is None:
                return AC(lambda e: e.copy(dst, src), *toks)
            return AC(lambda e: e.mul(dst, src, scale), *toks)
        if scale is None:
            return DV(lambda e: e.tensor_copy(dst, src), *toks)
        return DV(lambda e: e.tensor_scalar(dst, src, scale, None, ALU.mult), *toks)

    def act(dst, src, f, *toks, **kw):
        return AC(lambda e: e.activation(dst, src, f, **kw), *toks)

    def tt(q, dst, x, y, op, *toks):
        return q(lambda e: e.tensor_tensor(dst, x, y, op), *toks)

    def ts(dst, x, s1, op0, s2, op1, *toks, q=None):
        q = q or DV
        if s2 is None:
            return q(lambda e: e.tensor_scalar(dst, x, s1, None, op0), *toks)
        return q(lambda e: e.tensor_scalar(dst, x, s1, s2, op0, op1), *toks)

    def stt(dst, x, s, y, op0, op1, *toks):
        return DV(lambda e: e.scalar_tensor_tensor(dst, x, s, y, op0, op1), *toks)

    def hi(dst, src, *toks, scale=None):
        if scale is None:
            return AC(lambda e: e.copy(dst, src), *toks)
        return AC(lambda e: e.mul(dst, src, scale), *toks)

    def lo(dst, src, high, *toks, scale=None):
        if scale is None:
            return DV(lambda e: e.tensor_tensor(dst, src, high.bitcast(F32), ALU.subtract), *toks)
        return DV(lambda e: e.scalar_tensor_tensor(dst, src, scale, high.bitcast(F32), ALU.mult, ALU.subtract), *toks)

    def bring(n):
        src, nk, width = order[n]
        i, fr = raw.take()
        k = nk * width
        src = src.rearrange("(k p) n -> p k n", p=P)
        wcnt[i] += 16
        v = Wt[:, i * SLOT:i * SLOT + k]
        SP.quiet(lambda e: e.dma_start(v.rearrange("p (k n) -> p k n", n=width), src).then_inc(wsem[i], 16), *fr)
        x, fs = split.take()
        h = WSr[:, x * 2 * SLOT:x * 2 * SLOT + k]
        l = WSr[:, x * 2 * SLOT + SLOT:x * 2 * SLOT + SLOT + k]
        t1 = hi(h, v, (wsem[i], wcnt[i]), *fs)
        t2 = lo(l, v, h, t1, *fs)
        raw.give(i, t2)
        ready_w.append((h.rearrange("p (k n) -> p k n", n=width), l.rearrange("p (k n) -> p k n", n=width), x, t2))

    def load(src, nk, n):
        if listing:
            order.append((src, nk, n))
            return None, None, 0, (sems[1], 0)
        asked[0] += 1
        while len(ready_w) < min(asked[0] + AHEAD, len(order)):
            bring(len(ready_w))
        return ready_w[asked[0] - 1]

    def done_with(x, t):
        if not listing:
            split.give(x, t)

    def load_row(src):
        i, fr = rows.take()
        dst = WRt[:, 0:D]
        rcnt[0] += 16
        SP.quiet(lambda e: e.dma_start(dst, src.partition_broadcast(P)).then_inc(rsem, 16), *fr)
        return dst, i, (rsem, rcnt[0])

    T_IN = (s_in, 64)
    for dst, src in ((H, a["x"].rearrange("b (m p) d -> p (b m) d", p=P)), (KCt[:, :], a["consts"]),
                     (CPt[:, 0:C_N], a["colp"])):
        SP.quiet(lambda e, dst=dst, src=src: e.dma_start(dst, src).then_inc(s_in, 16))
    SP.quiet(lambda e: e.dma_start(RPt[:, 0:R_N], a["rowp"].partition_broadcast(P)).then_inc(s_in, 16))
    for q in (PE, DV, AC, PL):
        q.wait(T_IN)

    def gemm_t(x, nk, w, c0, n, use, *toks):
        for c in range(0, n, 256):
            bs = [psum.take() for _ in range(2)]
            for k0 in range(0, nk, 4):
                wh, wl, i, tk = load(w[k0 * P:(k0 + 4) * P, c0 + c:c0 + c + 256], 4, 256)
                for j in range(2):
                    b, fr = bs[j]
                    for k in range(k0, k0 + 4):
                        xh, xl = x(k)
                        PE.quiet(lambda e: e.matmul(banks[b][:, :], wh[:, k - k0, j * P:(j + 1) * P], xh,
                                                    start=(k == 0), stop=False), tk, *fr, *toks)
                        PE.quiet(lambda e: e.matmul(banks[b][:, :], wh[:, k - k0, j * P:(j + 1) * P], xl,
                                                    start=False, stop=False))
                        last = (lambda e: e.matmul(banks[b][:, :], wl[:, k - k0, j * P:(j + 1) * P], xh,
                                                   start=False, stop=(k == nk - 1)))
                        if k == k0 + 3 and (j == 1 or k == nk - 1):
                            t = PE(last)
                            if k == nk - 1:
                                use(c // P + j, b, t)
                        else:
                            PE.quiet(last)
                done_with(i, t)

    def gemm(x, nk, w, c0, n, use, toks=()):
        bs = [psum.take() for _ in range(4)]
        for k0 in range(0, nk, 2):
            wh, wl, i, tk = load(w[k0 * P:(k0 + 2) * P, c0:c0 + n], 2, n)
            for k in range(k0, k0 + 2):
                for m in range(4):
                    b, fr = bs[m]
                    xh, xl = x(k, m)
                    PE.quiet(lambda e: e.matmul(banks[b][:, 0:n], xh, wh[:, k - k0, :], start=(k == 0), stop=False),
                             tk, *toks, *fr)
                    PE.quiet(lambda e: e.matmul(banks[b][:, 0:n], xh, wl[:, k - k0, :], start=False, stop=False))
                    last = (lambda e: e.matmul(banks[b][:, 0:n], xl, wh[:, k - k0, :], start=False,
                                               stop=(k == nk - 1)))
                    if k == nk - 1 or (k == k0 + 1 and m == 3):
                        t = PE(last)
                        if k == nk - 1:
                            use(m, b, t)
                    else:
                        PE.quiet(last)
            done_with(i, t)

    def turn(src, nf, dst, toks, scale=None, wait=()):
        done = []
        for f0 in range(0, nf, 8):
            fs = range(f0, min(nf, f0 + 8))
            bs = {f: psum.take() for f in fs}
            last = {}
            for m in range(4):
                for f in fs:
                    b, fr = bs[f]
                    last[f] = PE(lambda e, b=b, m=m, f=f: e.transpose(banks[b][:, m * P:(m + 1) * P], src(m, f), IDN),
                                 *toks[m], *fr)
            for f in fs:
                d, v, sc = dst(f), banks[bs[f][0]][:, :], scale(f) if scale else None
                if isinstance(d, tuple):
                    t = hi(d[0], v, last[f], *wait, scale=sc)
                    t = lo(d[1], v, d[0], t, scale=sc)
                else:
                    t = evac(d, v, last[f], *wait, scale=sc)
                psum.give(bs[f][0], t)
                done.append(t)
        return done

    ss8, ss4, rst = sm(8), sm(4), sm(8)
    scr = [SC[:, i * 512:(i + 1) * 512] for i in range(9)]

    def inv_root(dst, src, mul, *toks, factor=None):
        t = ts(dst, src, mul, ALU.mult, EPS, ALU.add, *toks)
        t = act(dst, dst, ACT.Sqrt, t)
        t = DV(lambda e: e.reciprocal(dst, dst), t)
        if factor is not None:
            t = ts(dst, dst, factor, ALU.mult, None, None, t)
        return t

    def xs_at(f):
        return XH[:, f, :], XL[:, f, :]

    def x_cols(k, m):
        return XH[:, k, m * P:(m + 1) * P], XL[:, k, m * P:(m + 1) * P]

    def halves(off, nf):
        h, l = (ARr[:, off + y * nf * S:off + (y + 1) * nf * S].rearrange("p (f s) -> p f s", s=S) for y in range(2))
        return (lambda f: (h[:, f, :], l[:, f, :])), (lambda k, m: (h[:, k, m * P:(m + 1) * P], l[:, k, m * P:(m + 1) * P]))

    def prenorm(col, *toks):
        xn = AR[:, 0:4096].rearrange("p (m d) -> p m d", m=4)
        ready = []
        for m in range(4):
            t = AC(lambda e, m=m: e.activation(xn[:, m, :], H[:, m, :], ACT.Square, accum_out=ss4[:, m:m + 1]), *toks)
        t = inv_root(rst[:, 0:4], ss4, 1.0 / D, t)
        for m in range(4):
            ready.append([ts(xn[:, m, :], H[:, m, :], rst[:, m:m + 1], ALU.mult, None, None, t)])
        return turn(lambda m, f: xn[:, m, f * P:(f + 1) * P], 8, xs_at, ready,
                    lambda f: cp(C_PRE + col * 8 + f))

    def finish(parts, row, factor, tmps):
        res = []
        if row is None:
            for (m, h), (b, t) in sorted(parts.items()):
                hv = H[:, m, h * 512:(h + 1) * 512]
                t = tt(DV, hv, banks[b][:, :], hv, ALU.add, t)
                psum.give(b, t)
                res.append(t)
            return res
        w, i, tw = load_row(row)
        sq = Slots(tmps[0:2])
        for (m, h), (b, t) in sorted(parts.items(), key=lambda x: (x[0][1], x[0][0])):
            n, fr = sq.take()
            t = AC(lambda e, b=b, n=n, k=2 * m + h: e.activation(n, banks[b][:, :], ACT.Square,
                                                               accum_out=ss8[:, k:k + 1]), t, *fr)
            sq.give(n, t)
        s2 = ss8.rearrange("p (m h) -> p m h", h=2)
        t = tt(DV, ss4, s2[:, :, 0], s2[:, :, 1], ALU.add, t)
        t = inv_root(rst[:, 4:8], ss4, 1.0 / D, t, factor=factor)
        tmp = Slots(tmps[2:])
        for (m, h), (b, _) in sorted(parts.items()):
            n, fr = tmp.take()
            hv = H[:, m, h * 512:(h + 1) * 512]
            tb = stt(n, banks[b][:, :], rst[:, 4 + m:5 + m], w[:, h * 512:(h + 1) * 512], ALU.mult, ALU.mult,
                     t, tw, *fr)
            psum.give(b, tb)
            t2 = tt(PL, hv, hv, n, ALU.add, tb)
            tmp.give(n, t2)
            res.append(t2)
        rows.give(i, tb)
        return res

    def product_out(x, nk, w, row, factor, toks, tmps):
        parts = {}
        for h in range(2):
            gemm(x, nk, w, h * 512, 512, lambda m, b, t, h=h: parts.__setitem__((m, h), (b, t)), toks)
        return finish(parts, row, factor, tmps)

    x_tmp = [Xf[:, i * 512:(i + 1) * 512] for i in range(6)]

    def ffn(col, wg, wu, wd, row, factor, toks):
        g_at, g_cols = halves(0, NJ)
        tx = prenorm(col, *toks)
        fence()
        got = {}
        ready = {}
        tmp = Slots([scr[5], scr[6], scr[7], scr[8]])

        def use(kind, j, b, t):
            got[kind, j] = (b, t)
            if ("g", j) in got and ("u", j) in got:
                (bg, tg), (bu, tu) = got["g", j], got["u", j]
                v, fr = tmp.take()
                gh, gl = g_at(j)
                t = act(v, banks[bg][:, :], ACT.Silu, tg, *fr)
                psum.give(bg, t)
                t = tt(DV, v, banks[bu][:, :], v, ALU.mult, t, tu)
                psum.give(bu, t)
                t = hi(gh, v, t)
                ready[j] = t = lo(gl, v, gh, t)
                tmp.give(v, t)

        for j in range(0, NJ, 2):
            for kind, w in (("g", wg), ("u", wu)):
                gemm_t(xs_at, 8, w, j * P, 256, lambda i, b, t: use(kind, j + i, b, t), *tx)
        return product_out(g_cols, NJ, wd, row, factor, (ready[NJ - 1],), x_tmp)

    st_nm, st_l, st_r = sm(24), sm(24), sm(24)

    def attention(units):
        sbuf = Slots([0, 1, 2])
        pbuf = Slots([3, 4, 5])
        tbuf = Slots([6, 7, 8])
        stat = Slots([0, 1, 2])
        n = len(units)
        obank = [None]

        def scores(u):
            W = (u["i"] + 1) * P
            if u["slot"] == 0:
                u["o"], u["ofr"] = psum.take()
                u["st"], u["sfr"] = stat.take()
                obank[0] = u
            g = u["g"] = obank[0]
            b, fr = psum.take()
            t = PE(lambda e: e.matmul(banks[b][:, 0:W], u["q"], u["k"], start=True, stop=True), *fr)
            col = g["st"] * 8 + u["slot"]
            s, fs = sbuf.take()
            nm, l = st_nm[:, col:col + 1], st_l[:, col:col + 1]
            mask, tm = u["mask"]() if callable(u["mask"]) else (u["mask"], ())
            sv = scr[s][:, 0:W]
            bv = banks[b][:, 0:W]
            if len(mask.shape) == 3:
                sv = sv.rearrange("p (a b) -> p a b", b=P)
                bv = bv.rearrange("p (a b) -> p a b", b=P)
            t = DV(lambda e: e.tensor_tensor_reduce(sv, bv, mask, -1.0, 3e38, ALU.add,
                                                    ALU.min, nm), t, *fs, *g["sfr"], *tm)
            u["maskdone"] = t
            if u.get("free"):
                u["free"](t)
            psum.give(b, t)
            p, fp = pbuf.take()
            u["p"] = p
            t = AC(lambda e: e.activation(scr[p][:, 0:W], scr[s][:, 0:W], ACT.Exp, bias=nm, scale=-1.0,
                                          accum_out=l), t, *fp, *g["sfr"])
            sbuf.give(s, t)
            if u["times"] is not None:
                t = DV(lambda e: e.tensor_tensor_reduce(scr[p][:, 0:W], scr[p][:, 0:W], u["times"], 1.0, 0.0,
                                                        ALU.mult, ALU.add, l), t)
            u["t"] = t

        def turned(u):
            nb = u["i"] + 1
            b, fr = psum.take()
            for kb in range(nb):
                t = PE(lambda e, kb=kb: e.transpose(banks[b][:, kb * P:(kb + 1) * P],
                                                    scr[u["p"]][:, kb * P:(kb + 1) * P], IDN), u["t"], *fr)
            pbuf.give(u["p"], t)
            x, fx = tbuf.take()
            u["x"] = x
            t = evac(scr[x][:, 0:nb * P], banks[b][:, 0:nb * P], t, *fx)
            psum.give(b, t)
            u["t"] = t

        def values(u):
            nb = u["i"] + 1
            g = u["g"]
            for kb in range(nb):
                t = PE(lambda e, kb=kb: e.matmul(banks[g["o"]][:, u["slot"] * 64:u["slot"] * 64 + 64],
                                                 scr[u["x"]][:, kb * P:(kb + 1) * P], u["values"](kb),
                                                 start=(kb == 0), stop=(kb == nb - 1)), u["t"], *g["ofr"])
            tbuf.give(u["x"], t)
            if u["done"] is not None:
                c = g["st"] * 8
                w = u["slot"] + 1
                tr = DV(lambda e: e.reciprocal(st_r[:, c:c + w], st_l[:, c:c + w]), u["t"], *g["sfr"])
                ts_ = u["done"](banks[g["o"]], st_r[:, c:c + w], t, tr)
                psum.give(g["o"], ts_)
                stat.give(g["st"], ts_)

        for x in range(n + 3):
            if x < n:
                scores(units[x])
            if 0 <= x - 2 < n:
                turned(units[x - 2])
            if 0 <= x - 3 < n:
                values(units[x - 3])

    def scale_heads(dst, bank, r, nh, c0, *toks):
        return tt(DV, dst, bank[:, c0 * 64:(c0 + nh) * 64].rearrange("p (h d) -> p h d", d=64),
                  r[:, c0:c0 + nh].unsqueeze(2).broadcast_to((P, nh, 64)), ALU.mult, *toks)

    def softplus(x, t1, t2, t3, *toks):
        t = ts(t1, x, -1.0, ALU.mult, None, None, *toks)
        t = tt(DV, t1, t1, x, ALU.min, t)
        t = act(t1, t1, ACT.Exp, t)
        t = ts(t2, t1, 2.0, ALU.add, None, None, t)
        t = DV(lambda e: e.reciprocal(t2, t2), t)
        t = tt(DV, t1, t1, t2, ALU.mult, t)
        t = tt(DV, t2, t1, t1, ALU.mult, t)
        t = ts(t3, t2, 2.0 / 19, ALU.mult, None, None, t)
        for k in range(8, 0, -1):
            t = stt(t3, t3, 2.0 / (2 * k + 1), t2, ALU.add, ALU.mult, t)
        t = stt(t3, t3, 2.0, t1, ALU.add, ALU.mult, t)
        return stt(x, x, 0.0, t3, ALU.max, ALU.add, t)

    cbuf = Slots([0, 1, 2, 3])

    def conv(b, t, taps, bias):
        n, fr = cbuf.take()
        acc = scr[n]
        x = banks[b]
        t = AC(lambda e: e.mul(acc, x[:, :], cp(taps + 3)), t, *fr)
        for k in (2, 1, 0):
            s = 3 - k
            t = stt(acc[:, s:S], x[:, 0:S - s], cp(taps + k), acc[:, s:S], ALU.mult, ALU.add, t)
        psum.give(b, t)
        if bias is None:
            t = act(acc, acc, ACT.Silu, t)
        else:
            t = act(acc, acc, ACT.Silu, t, bias=cp(bias))
        return n, t

    class Later:

        def __init__(self, lag):
            self.lag, self.fns = lag, []

        def add(self, fn):
            self.fns.append(fn)
            if len(self.fns) > self.lag:
                self.fns.pop(0)()

        def flush(self):
            while self.fns:
                self.fns.pop(0)()

    def turn_block(n, t, dst):
        b, fr = psum.take()
        for c in range(4):
            tp = PE(lambda e, c=c: e.transpose(banks[b][:, c * P:(c + 1) * P], scr[n][:, c * P:(c + 1) * P], IDN),
                    t, *fr)
        te = evac(dst, banks[b][:, :].rearrange("p (c f) -> p c f", f=P), tp)
        psum.give(b, te)
        return tp, te

    def even(toks):
        w = a["even_w_in"][0]
        KE = arena(18944, E_N)

        def ke(c, n=128):
            return KE[:, c:c + n]
        QA = arena(0, 2048).rearrange("p (f s) -> p f s", s=S)
        KA = arena(2048, 2048).rearrange("p (f s) -> p f s", s=S)
        VA = arena(4096, 2048).rearrange("p (m d) -> p m d", m=4)
        ZB = arena(6144, 2048).rearrange("p (m d) -> p m d", m=4)
        QKV = arena(8192, 6144).rearrange("p (c f) -> p c f", c=4)
        O = arena(14336, 4096).rearrange("p (m d) -> p m d", m=4)
        small[0] = SM0
        GT = sm(32).rearrange("p (m d) -> p m d", m=4)
        tx = prenorm(1, *toks)

        def put(dst, scale=None):
            def use(j, b, t):
                psum.give(b, evac(dst(j), banks[b][:, :], t, scale=scale))
            return use

        xk = xs_at
        xm = x_cols
        fence()
        AC.quiet(lambda e: e.dma_start(KE, a["consts_e"]).then_inc(s_ev, 16))
        gemm_t(xk, 8, w, 0, 512, put(lambda j: QA[:, j, :], 0.125), *tx)
        gemm_t(xk, 8, w, 512, 512, put(lambda j: KA[:, j, :]), *tx)
        gemm(xm, 8, w, 1024, 512, put(lambda m: VA[:, m, :]))
        later = Later(2)

        def use(j, b, t):
            n, t = conv(b, t, C_ECONV + 4 * j, None)

            def go():
                tp, te = turn_block(n, t, QKV[:, :, j * P:(j + 1) * P])
                cbuf.give(n, tp)
            later.add(go)
        gemm_t(xk, 8, w, 1536, 1536, use, *tx)
        later.flush()

        def use_z(m, b, t):
            t = act(ZB[:, m, :], banks[b][:, :], ACT.Silu, t)
            psum.give(b, t)
        gemm(xm, 8, w, 3072, 512, use_z)

        def use_g(m, b, t):
            t = DV(lambda e: e.tensor_copy(GT[:, m, :], banks[b][:, 0:8]), t)
            psum.give(b, t)
        gemm(xm, 8, w, 3584, 8, use_g)
        fence()
        AM = arena(18432, 512)
        ts(AM, ke(E_CM, 512), 0.0, ALU.is_equal, -BIG, ALU.mult, (s_ev, 16))
        fence()
        units = []
        for i in range(4):
            def done(bank, r, t, tr, i=i):
                return scale_heads(O[:, i, 0:512].rearrange("p (h d) -> p h d", d=64), bank, r, 8, 0, t, tr)
            for h in range(8):
                r0 = 64 * (h % 2)
                W = (i + 1) * P
                units.append(dict(i=i, q=QA[r0:r0 + 64, h // 2, i * P:(i + 1) * P], k=KA[r0:r0 + 64, h // 2, 0:W],
                                  mask=AM[:, 512 - W:512], times=ke(E_CM + 512 - W, W),
                                  values=lambda kb, h=h: VA[:, kb, h * 64:(h + 1) * 64], slot=h,
                                  done=done if h == 7 else None))
        attention(units)
        fence()
        PL.wait((s_ev, 16))
        GB = sm(16).rearrange("p (m d) -> p m d", m=4)
        GG = sm(16)
        G3 = GG.rearrange("p (m d) -> p m d", m=4)
        sa, sb_, sc_, ea4 = sm(16), sm(16), sm(16), sm(4)
        t = act(GB, GT[:, :, 0:4], ACT.Exp, scale=-1.0)
        t = ts(GB, GB, 1.0, ALU.add, None, None, t)
        t = DV(lambda e: e.reciprocal(GB, GB), t)
        t = tt(DV, G3, GT[:, :, 4:8], rp(R_EDT, 4).unsqueeze(1).broadcast_to((P, 4, 4)), ALU.add)
        t = softplus(GG, sa, sb_, sc_, t)
        t1 = act(ea4, rp(R_EA, 4), ACT.Exp)
        t = stt(G3, G3, -1.0, ea4.unsqueeze(1).broadcast_to((P, 4, 4)), ALU.mult, ALU.mult, t, t1)
        SQ = arena(0, 1024)
        QS = sm(32)
        tprev = []
        for c in range(4):
            t = act(SQ, QKV[:, c, 0:1024], ACT.Square, *tprev)
            t = DV(lambda e, c=c: e.tensor_reduce(QS[:, c * 8:(c + 1) * 8], SQ.rearrange("p (h d) -> p h d", d=P),
                                                  AX, ALU.add), t)
            tprev = [t]
        t = inv_root(QS, QS, 1.0, t)
        Q3 = QS.rearrange("p (c h) -> p c h", c=4)
        t = ts(Q3[:, :, 0:4], Q3[:, :, 0:4], float(P) ** -0.5, ALU.mult, None, None, t)
        for c in range(4):
            v = QKV[:, c, 0:1024].rearrange("p (h d) -> p h d", d=P)
            tt(DV, v, v, Q3[:, c, :].unsqueeze(2).broadcast_to((P, 8, P)), ALU.mult, t)
        GC, EG, EL, EK, NB = sm(16), sm(16), sm(16), sm(16), sm(16)
        b, fr = psum.take()
        PE(lambda e: e.matmul(banks[b][:, 0:16], TRI, GG, start=True, stop=True), DV.now(), *fr)
        t = PE(lambda e: e.matmul(banks[b][:, 16:32], ONE, GG, start=True, stop=True))
        t1 = DV(lambda e: e.tensor_copy(GC, banks[b][:, 0:16]), t)
        t2 = act(EG, GC, ACT.Exp, t1)
        t3 = act(EL, banks[b][:, 16:32], ACT.Exp, t, t1)
        t4 = tt(DV, EK, banks[b][:, 16:32], GC, ALU.subtract, t1, t3)
        psum.give(b, t4)
        t5 = act(EK, EK, ACT.Exp, t4)
        t6 = stt(NB, GB.rearrange("p m d -> p (m d)"), -1.0, EG, ALU.mult, ALU.mult, t2)
        fence()
        A3 = lambda off: arena(off, 512)
        KD, UB, WB, QD, KT, QT = (A3(512 * i) for i in range(6))
        QDT, Dm, DT, Am, AT, LT = (A3(512 * i) for i in range(6, 12))
        X, XX, Y, QK, WT, VN = (XTt[:, 512 * i:512 * (i + 1)] for i in range(6))
        ST = XTt[:, 3072:3584]
        h3 = lambda x: x.rearrange("p (h d) -> p h d", d=P)
        hd = lambda x, h: x[:, h * P:(h + 1) * P]

        def per_head(fn, b, *toks):
            for h in range(4):
                t = PE(lambda e, h=h: e.matmul(hd(banks[b], h), *fn(h), start=True, stop=True), *toks)
            return t

        def bc(x, c):
            return x[:, 4 * c:4 * c + 4].unsqueeze(2).broadcast_to((P, 4, P))
        QDT, Dm, DT, Am, AT, LT = scr[0], scr[1], scr[2], scr[3], scr[4], scr[5]
        ARG = scr[6]
        AR2 = scr[7]
        GBf = GB.rearrange("p m d -> p (m d)")
        for c in range(4):
            q, k, v = (QKV[:, c, 512 * i:512 * (i + 1)] for i in range(3))
            fence()
            t_qd = tt(DV, h3(QD), h3(q), bc(EG, c), ALU.mult)
            t_kd = tt(PL, h3(KD), h3(k), bc(EK, c), ALU.mult)
            t_wb = tt(PL, h3(WB), h3(k), bc(NB, c), ALU.mult)
            t_ub = tt(PL, h3(UB), h3(v), bc(GBf, c), ALU.mult)
            bq, f1 = psum.take()
            bk, f2 = psum.take()
            bd, f3 = psum.take()
            br, f4 = psum.take()
            for h in range(4):
                tr = PE(lambda e, h=h: e.matmul(hd(banks[br], h), GG[:, 4 * c + h:4 * c + h + 1].broadcast_to((P, P)),
                                                TRI, start=True, stop=True), *f4)
            for h in range(4):
                tk = PE(lambda e, h=h: e.transpose(hd(banks[bk], h), hd(k, h), IDN), *f2)
            for h in range(4):
                tq = PE(lambda e, h=h: e.transpose(hd(banks[bq], h), hd(q, h), IDN), *f1)
            for h in range(4):
                td = PE(lambda e, h=h: e.transpose(hd(banks[bd], h), hd(QD, h), IDN), t_qd, *f3)
            t_kt = AC(lambda e: e.copy(KT, banks[bk][:, :]), tk)
            psum.give(bk, t_kt)
            t_qt = AC(lambda e: e.copy(QT, banks[bq][:, :]), tq)
            psum.give(bq, t_qt)
            for h in range(4):
                g = GC[:, 4 * c + h:4 * c + h + 1]
                ts(hd(ARG, h), hd(banks[br], h), g, ALU.subtract, 0.0, ALU.min, tr)
                t = ts(hd(AR2, h), hd(banks[br], h), g, ALU.subtract, 0.0, ALU.max)
            psum.give(br, t)
            t1 = act(DT, ARG, ACT.Exp, t)
            t2 = act(Dm, AR2, ACT.Exp, t, scale=-1.0)
            t_qdt = AC(lambda e: e.copy(QDT, banks[bd][:, :]), td)
            psum.give(bd, t_qdt)
            t_dt = tt(PL, h3(DT), h3(DT), TRI.unsqueeze(1).broadcast_to((P, 4, P)), ALU.mult, t1)
            t_dm = tt(PL, h3(Dm), h3(Dm), kc(K_LOW).unsqueeze(1).broadcast_to((P, 4, P)), ALU.mult, t2)
            b1, f1 = psum.take()
            t = per_head(lambda h: (hd(KT, h), hd(KT, h)), b1, t_kt, *f1)
            for h in range(4):
                t_a = stt(hd(Am, h), hd(banks[b1], h), GB[:, c, h:h + 1], hd(Dm, h), ALU.mult, ALU.mult, t, t_dm)
            psum.give(b1, t_a)
            b2, f2 = psum.take()
            t = per_head(lambda h: (hd(KT, h), hd(QT, h)), b2, t_kt, t_qt, *f2)
            t_qk = tt(DV, QK, banks[b2][:, :], DT, ALU.mult, t, t_dt)
            psum.give(b2, t_qk)
            b3, f3 = psum.take()
            for h in range(4):
                t = PE(lambda e, h=h: e.transpose(hd(banks[b3], h), hd(Am, h), IDN), t_a, *f3)
            t_at = AC(lambda e: e.copy(AT, banks[b3][:, :]), t)
            psum.give(b3, t_at)
            t = stt(h3(X), h3(Am), -1.0, ke(E_M1).unsqueeze(1).broadcast_to((P, 4, P)), ALU.mult, ALU.mult, t_a)
            t_x = tt(DV, h3(X), h3(X), IDN.unsqueeze(1).broadcast_to((P, 4, P)), ALU.add, t)
            lvl = lambda n: ke(E_LV + (n - 1) * P).unsqueeze(1).broadcast_to((P, 4, P))
            b4, f4 = psum.take()
            for h in range(4):
                t = PE(lambda e, h=h: e.transpose(hd(banks[b4], h), hd(X, h), IDN), t_x, *f4)
            t_xx = AC(lambda e: e.copy(XX, banks[b4][:, :]), t)
            psum.give(b4, t_xx)
            t_use = t_at
            for n in range(1, 7):
                t_lt = tt(PL, h3(LT), h3(AT), lvl(n), ALU.mult, t_at, t_use)
                b1, f1 = psum.take()
                t = t_use = per_head(lambda h: (hd(LT, h), hd(X, h)), b1, t_lt, t_x, *f1)
                t_y = AC(lambda e, b1=b1: e.copy(Y, banks[b1][:, :]), t)
                psum.give(b1, t_y)
                if n < 6:
                    b2, f2 = psum.take()
                    t_m = per_head(lambda h: (hd(XX, h), hd(Y, h)), b2, t_y, t_xx, *f2)
                b3, f3 = psum.take()
                t_n = per_head(lambda h: (hd(Y, h), hd(XX, h)), b3, t_y, t_xx, *f3)
                if n < 6:
                    t_x = tt(DV, X, X, banks[b2][:, :], ALU.subtract, t_m)
                    psum.give(b2, t_x)
                t_xx = tt(DV, XX, XX, banks[b3][:, :], ALU.subtract, t_n)
                psum.give(b3, t_xx)
            bw, f1 = psum.take()
            t = per_head(lambda h: (hd(WB, h), hd(XX, h)), bw, t_xx, t_wb, *f1)
            t_wt = AC(lambda e: e.copy(WT, banks[bw][:, :]), t)
            psum.give(bw, t_wt)
            bv, f2 = psum.take()
            for h in range(4):
                t = PE(lambda e, h=h: e.matmul(hd(banks[bv], h), hd(XX, h), hd(UB, h), start=True, stop=(c == 0)),
                       t_xx, t_ub, *f2)
                if c:
                    t = PE(lambda e, h=h: e.matmul(hd(banks[bv], h), hd(WT, h), hd(ST, h), start=False, stop=True),
                           t_wt)
            t_vn = DV(lambda e: e.tensor_copy(VN, banks[bv][:, :]), t)
            psum.give(bv, t_vn)
            bo, f3 = psum.take()
            for h in range(4):
                t = PE(lambda e, h=h: e.matmul(hd(banks[bo], h), hd(QK, h), hd(VN, h), start=True, stop=(c == 0)),
                       t_vn, t_qk, *f3)
                if c:
                    t = PE(lambda e, h=h: e.matmul(hd(banks[bo], h), hd(QDT, h), hd(ST, h), start=False, stop=True),
                           t_qdt)
            t = AC(lambda e: e.copy(O[:, c, 512:1024], banks[bo][:, :]), t)
            psum.give(bo, t)
            if c < 3:
                bs, f4 = psum.take()
                t = per_head(lambda h: (hd(KD, h), hd(VN, h)), bs, t_vn, t_kd, *f4)
                if c == 0:
                    t = DV(lambda e: e.tensor_copy(ST, banks[bs][:, :]), t)
                else:
                    for h in range(4):
                        t0 = stt(hd(ST, h), hd(ST, h), EL[:, 4 * c + h:4 * c + h + 1], hd(banks[bs], h), ALU.mult,
                                 ALU.add, t)
                    t = t0
                psum.give(bs, t)
        fence()
        OS = sm(16)
        tprev = []
        for c in range(4):
            t = act(scr[0], O[:, c, 512:1024], ACT.Square, *tprev)
            t = DV(lambda e, c=c: e.tensor_reduce(OS[:, c * 4:(c + 1) * 4], h3(scr[0]), AX, ALU.add), t)
            tprev = [t]
        t = inv_root(OS, OS, 1.0 / P, t)
        ready = []
        for c in range(4):
            t1 = tt(DV, h3(O[:, c, 512:1024]), h3(O[:, c, 512:1024]), bc(OS, c), ALU.mult, t)
            ready.append([tt(PL, O[:, c, 512:1024], O[:, c, 512:1024], ZB[:, c, :], ALU.mult, t1)])
        tx = turn(lambda m, f: O[:, m, f * P:(f + 1) * P], 8, xs_at, ready,
                  lambda f: 1.0 if f < 4 else cp(C_HNORM))
        return product_out(xm, 8, a["even_w_out"][0], a["norm_w"][0, 3:4], 1.0, tuple(tx), scr)

    def odd(toks):
        w = a["odd_w_in"][0]
        Z = arena(0, 8192).rearrange("p (c d) -> p c d", c=4)
        XS = arena(8192, 8192).rearrange("p (c d) -> p c d", c=4)
        BT = arena(16384, 2048).rearrange("p (g s) -> p g s", s=S)
        CT = arena(18432, 2048).rearrange("p (g s) -> p g s", s=S)
        BK = SC[:, 2560:4608].rearrange("p (c d) -> p c d", c=4)
        small[0] = SM0
        DT = sm(128)
        AA = sm(128)
        tx = prenorm(4, *toks)
        xk = xs_at
        xm = x_cols
        fence()
        later = Later(2)

        def use(j, b, t):
            n, t = conv(b, t, C_OCONV + 4 * j, C_OBIAS + j)

            def go():
                if j < 16:
                    tp, te = turn_block(n, t, XS[:, :, j * P:(j + 1) * P])
                elif j < 20:
                    tp, te = turn_block(n, t, BK[:, :, (j - 16) * P:(j - 15) * P])
                    tp = PL(lambda e: e.tensor_copy(BT[:, j - 16, :], scr[n]), t, tp)
                else:
                    tp = PL(lambda e: e.tensor_copy(CT[:, j - 20, :], scr[n]), t)
                cbuf.give(n, tp)
            later.add(go)
        gemm_t(xk, 8, w, 2048, 3072, use, *tx)
        later.flush()
        for q in range(4):
            def use_z(m, b, t, q=q):
                t = act(Z[:, m, q * 512:(q + 1) * 512], banks[b][:, :], ACT.Silu, t)
                psum.give(b, t)
            gemm(xm, 8, w, q * 512, 512, use_z)
        D3 = DT.rearrange("p (c h) -> p c h", c=4)
        A3 = AA.rearrange("p (c h) -> p c h", c=4)

        def use_dt(m, b, t):
            t = tt(DV, D3[:, m, :], banks[b][:, 0:32], rp(R_ODT, 32), ALU.add, t)
            psum.give(b, t)
        gemm(xm, 8, w, 5120, 32, use_dt)
        fence()
        s1, s2, s3, e32 = sm(128), sm(128), sm(128), sm(32)
        t = softplus(DT, s1, s2, s3)
        t1 = act(e32, rp(R_OA, 32), ACT.Exp)
        t = stt(A3, D3, -1.0, e32.unsqueeze(1).broadcast_to((P, 4, 32)), ALU.mult, ALU.mult, t, t1)
        AC_, EA, ET, ED = s1, s2, s3, sm(128)
        b, fr = psum.take()
        PE(lambda e: e.matmul(banks[b][:, 0:128], TRI, AA, start=True, stop=True), t, *fr)
        t = PE(lambda e: e.matmul(banks[b][:, 128:256], ONE, AA, start=True, stop=True))
        t1 = DV(lambda e: e.tensor_copy(AC_, banks[b][:, 0:128]), t)
        t2 = act(EA, AC_, ACT.Exp, t1)
        t3 = act(ET, banks[b][:, 128:256], ACT.Exp, t1)
        t4 = tt(DV, ED, banks[b][:, 128:256], AC_, ALU.subtract, t3)
        psum.give(b, t4)
        act(ED, ED, ACT.Exp, t4)
        fence()
        XD = [XTt[:, 0:512], XTt[:, 512:1024]]
        XE = [XTt[:, 1024:1536], XTt[:, 1536:2048]]
        HS = XTt[:, 2048:4096].rearrange("p (g d) -> p g d", g=4)
        xbuf = Slots([0, 1])
        mbuf = Slots([0, 1, 2])
        MT = [scr[0], scr[1], scr[2]]
        YB = [scr[3], scr[4]]
        ybuf = Slots([0, 1])
        cbm = Slots([0, 1])
        CB = sm(256)
        p8 = lambda x: x.rearrange("p (h d) -> p h d", d=64)
        h3 = lambda x: x.rearrange("p (h d) -> p h d", d=P)
        st = {}
        hs_t = {g: () for g in range(4)}

        def first(u):
            c, g = u["c"], u["g"]
            xi, fx = xbuf.take()
            h8 = c * 32 + g * 8
            bc = lambda x: x[:, h8:h8 + 8].unsqueeze(2).broadcast_to((P, 8, 64))
            xs = XS[:, c, g * 512:(g + 1) * 512]
            u["xi"] = xi
            t = u["t_xd"] = tt(PL, p8(XD[xi]), p8(xs), bc(DT), ALU.mult, *fx)
            u["t_xe"] = tt(PL, p8(XE[xi]), p8(XD[xi]), bc(ED), ALU.mult, t)
            ci, fc = cbm.take()
            u["ci"] = ci
            b, fr = psum.take()
            t = PE(lambda e: e.matmul(banks[b][:, 0:P], BT[:, g, c * P:(c + 1) * P], CT[:, g, c * P:(c + 1) * P],
                                      start=True, stop=True), *fr)
            cb = CB[:, ci * P:(ci + 1) * P]
            t_cb = tt(DV, cb, banks[b][:, 0:P], TRI, ALU.mult, t, *fc)
            psum.give(b, t_cb)
            u["mt"] = []
            for hh in range(2):
                b, fr = psum.take()
                for x in range(4):
                    k = h8 + hh * 4 + x
                    t = PE(lambda e, x=x, k=k, b=b: e.matmul(banks[b][:, x * P:(x + 1) * P],
                                                             AA[:, k:k + 1].broadcast_to((P, P)), TRI, start=True,
                                                             stop=True), *fr)
                mi, fm = mbuf.take()
                for x in range(4):
                    k = h8 + hh * 4 + x
                    t1 = ts(MT[mi][:, x * P:(x + 1) * P], banks[b][:, x * P:(x + 1) * P], AC_[:, k:k + 1],
                            ALU.subtract, 0.0, ALU.min, t, *fm)
                psum.give(b, t1)
                t1 = act(MT[mi], MT[mi], ACT.Exp, t1)
                t1 = tt(DV, h3(MT[mi]), h3(MT[mi]), cb.unsqueeze(1).broadcast_to((P, 4, P)), ALU.mult, t1, t_cb)
                u["mt"].append((mi, t1))
                if hh == 0:
                    self_y(u, 0)
            self_y(u, 1)
            cbm.give(ci, u["mt"][1][1])

        def self_y(u, hh):
            if hh == 0:
                u["yb"], u["yfr"] = psum.take()
            xi = u["xi"]
            mi, tm = u["mt"][hh]
            for x in range(4):
                hx = hh * 4 + x
                t = PE(lambda e, x=x, hx=hx: e.matmul(banks[u["yb"]][:, hx * 64:(hx + 1) * 64],
                                                      MT[mi][:, x * P:(x + 1) * P], XD[xi][:, hx * 64:(hx + 1) * 64],
                                                      start=True, stop=True), tm, u["t_xd"], *u["yfr"])
            mbuf.give(mi, t)
            u["t_y"] = t

        def second(u):
            c, g, xi = u["c"], u["g"], u["xi"]
            h8 = c * 32 + g * 8
            bc = lambda x: x[:, h8:h8 + 8].unsqueeze(2).broadcast_to((P, 8, 64))
            yi, fy = ybuf.take()
            y = YB[yi]
            xs = XS[:, c, g * 512:(g + 1) * 512]
            if c:
                b, fr = psum.take()
                t = t_off = PE(lambda e: e.matmul(banks[b][:, :], CT[:, g, c * P:(c + 1) * P], HS[:, g, :], start=True,
                                          stop=True), *fr, *hs_t[g])
                t = tt(DV, p8(y), p8(banks[b][:, :]), bc(EA), ALU.mult, t, *fy)
                psum.give(b, t)
                t = tt(DV, y, banks[u["yb"]][:, :], y, ALU.add, t, u["t_y"])
            else:
                t_off = u["t_y"]
                t = DV(lambda e: e.tensor_copy(y, banks[u["yb"]][:, :]), u["t_y"], *fy)
            psum.give(u["yb"], t)
            t1 = tt(PL, p8(xs), p8(xs), rp(R_DSK + g * 8, 8).unsqueeze(2).broadcast_to((P, 8, 64)), ALU.mult, u["t_xd"])
            t1 = tt(PL, y, y, xs, ALU.add, t, t1)
            zz = Z[:, c, g * 512:(g + 1) * 512]
            t1 = tt(PL, zz, zz, y, ALU.mult, t1)
            ybuf.give(yi, t1)
            tl = u["t_y"]
            if c < 3:
                b, fr = psum.take()
                tl = t = PE(lambda e: e.matmul(banks[b][:, :], BK[:, c, g * P:(g + 1) * P], XE[xi], start=True, stop=True),
                            u["t_xe"], *fr)
                hv = HS[:, g, :]
                if c:
                    t2 = tt(DV, p8(hv), p8(hv), bc(ET), ALU.mult, t_off, *hs_t[g])
                    t2 = tt(DV, hv, banks[b][:, :], hv, ALU.add, t, t2)
                else:
                    t2 = DV(lambda e: e.tensor_copy(hv, banks[b][:, :]), t)
                psum.give(b, t2)
                hs_t[g] = (t2,)
            xbuf.give(xi, tl, u["t_xe"])

        units = [dict(c=c, g=g) for c in range(4) for g in range(4)]
        for x in range(17):
            if x < 16:
                first(units[x])
            if x:
                second(units[x - 1])
        fence()
        YS = sm(16)
        sq = Slots([0, 1])
        for c in range(4):
            for g in range(4):
                n, fr = sq.take()
                t = AC(lambda e, c=c, g=g, n=n: e.activation(scr[n], Z[:, c, g * 512:(g + 1) * 512], ACT.Square,
                                                             accum_out=YS[:, c * 4 + g:c * 4 + g + 1]), *fr)
                sq.give(n, t)
        t = inv_root(YS, YS, 1.0 / 512, t)
        ready = []
        for c in range(4):
            z4 = Z[:, c, :].rearrange("p (g d) -> p g d", g=4)
            ready.append([tt(DV, z4, z4, YS[:, c * 4:c * 4 + 4].unsqueeze(2).broadcast_to((P, 4, 512)), ALU.mult, t)])
        y_at, y_cols = halves(8192, 16)
        tx = turn(lambda m, f: Z[:, m, f * P:(f + 1) * P], 16, y_at, ready,
                  lambda f: cp(C_ONORM + f), (AC.now(),))
        return product_out(y_cols, 16, a["odd_w_out"][0], a["norm_w"][1, 3:4], 1.0,
                           tuple(tx), x_tmp)

    def mixer2(l, toks):
        w = a["w_in_2"][l]
        r0 = R_L + l * L_N
        PJ = arena(0, 4 * Q_N).rearrange("p (c d) -> p c d", c=4)
        QT = arena(4 * Q_N, 8704).rearrange("p (f s) -> p f s", s=S)
        small[0] = SM0
        tx = prenorm(6 + 2 * l, *toks)
        xm = x_cols
        fence()
        for c0 in range(0, Q_N, 512):
            n = min(512, Q_N - c0)

            def use(m, b, t, c0=c0, n=n):
                psum.give(b, evac(PJ[:, m, c0:c0 + n], banks[b][:, 0:n], t))
            gemm(xm, 8, w, c0, n, use, tuple(tx))
        fence()
        wr = sm(64 + 64 + 32 + 32 + 64 + 64)
        wo = 0
        wv = {}
        for name, src, n, f in (("fq", L_FQ, 64, 0.125), ("fk", L_FK, 64, 1.0), ("dq", L_DQ, 32, 32.0 ** -0.5),
                                ("dk", L_DK, 32, 1.0), ("sq", L_SQ, 64, 0.125), ("sk", L_SK, 64, 1.0)):
            wv[name] = wr[:, wo:wo + n]
            ts(wv[name], rp(r0 + src, n), f, ALU.mult, None, None)
            wo += n
        lam_init = 0.8 - 0.6 * float(np.exp(-0.3 * l))
        ld, lj = sm(4), sm(32)
        for k, (x, y) in enumerate(((L_LQ1, L_LK1), (L_LQ2, L_LK2))):
            t = DV(lambda e, k=k, x=x, y=y: e.tensor_tensor_reduce(lj, rp(r0 + x, 32), rp(r0 + y, 32), 1.0, 0.0,
                                                                   ALU.mult, ALU.add, ld[:, k:k + 1]), DV.now())
        t = act(ld[:, 0:2], ld[:, 0:2], ACT.Exp, t)
        t = tt(DV, ld[:, 2:3], ld[:, 1:2], ld[:, 0:1], ALU.subtract, t)
        ts(ld[:, 2:3], ld[:, 2:3], -lam_init, ALU.add, None, None, t)
        NS = sm(140).rearrange("p (c h) -> p c h", c=4)
        qbuf = SC[:, 0:3584]
        sq = Slots([0, 1])
        sz = {0: SC[:, 0:768], 1: SC[:, 768:1536]}
        for c in range(4):
            for off, nh, dh, o in ((Q_FQ, 12, 64, 0), (Q_DQ, 16, 32, 12), (Q_SQ, 7, 64, 28)):
                n, fr = sq.take()
                v = sz[n][:, 0:nh * dh]
                t = act(v, PJ[:, c, off:off + nh * dh], ACT.Square, *fr)
                t = DV(lambda e, v=v, c=c, nh=nh, dh=dh, o=o: e.tensor_reduce(
                    NS[:, c, o:o + nh], v.rearrange("p (h d) -> p h d", d=dh), AX, ALU.add), t)
                sq.give(n, t)
        t = ts(NS[:, :, 12:28], NS[:, :, 12:28], 2.0, ALU.mult, None, None, t)
        nsf = NS.rearrange("p c h -> p (c h)")
        t = inv_root(nsf, nsf, 1.0 / 64, t)
        for c in range(4):
            for off, nh, dh, o, ws in ((Q_FQ, 12, 64, 0, (("fq", 6), ("fk", 6))), (Q_DQ, 16, 32, 12, (("dq", 8), ("dk", 8))),
                                       (Q_SQ, 7, 64, 28, (("sq", 6), ("sk", 1)))):
                v = PJ[:, c, off:off + nh * dh].rearrange("p (h d) -> p h d", d=dh)
                t1 = tt(DV, v, v, NS[:, c, o:o + nh].unsqueeze(2).broadcast_to((P, nh, dh)), ALU.mult, t)
                h = 0
                for name, k in ws:
                    vv = v[:, h:h + k, :]
                    tt(PL, vv, vv, wv[name].unsqueeze(1).broadcast_to((P, k, dh)), ALU.mult, t1)
                    h += k
        fence()
        T4 = [SC[:, i * 280:(i + 1) * 280] for i in range(4)]
        for off, nh, dh, kr in ((Q_DQ, 16, 32, K_R32), (Q_SQ, 7, 64, K_R64), (Q_IQ, 5, 64, K_R64)):
            hf = dh // 8
            cs = kc(kr, 4 * hf).rearrange("p (c d) -> p c d", c=4)
            sn = kc(kr + 4 * hf, 4 * hf).rearrange("p (c d) -> p c d", c=4)
            v = [PJ[:, c, off:off + nh * dh].rearrange("p (h d) -> p h d", d=dh) for c in range(4)]
            t0 = DV.now()
            for c in range(4):
                x1, x2 = v[c][:, :, 0:hf], v[c][:, :, hf:2 * hf]
                cc = cs[:, c, :].unsqueeze(1).broadcast_to((P, nh, hf))
                sn_ = sn[:, c, :].unsqueeze(1).broadcast_to((P, nh, hf))
                tv = [x[:, c * nh * hf - c * nh * hf + c * 70:c * 70 + nh * hf].rearrange("p (h d) -> p h d", d=hf) for x in T4] \
                    if nh * hf <= 70 else None
                tt(DV, tv[0], x1, cc, ALU.mult, t0)
                tt(DV, tv[1], x2, sn_, ALU.mult)
                tt(DV, tv[2], x2, cc, ALU.mult)
                t = tt(DV, tv[3], x1, sn_, ALU.mult)
                tt(DV, x1, tv[0], tv[1], ALU.subtract, t)
                t = tt(DV, x2, tv[2], tv[3], ALU.add)
        KD = SC[:, 1120:2144].rearrange("p (c d) -> p c d", c=4)
        for c in range(4):
            for k, off in ((0, Q_SK), (64, Q_SK), (128, Q_IK), (192, Q_IK)):
                DV(lambda e, c=c, k=k, off=off: e.tensor_copy(KD[:, c, k:k + 64], PJ[:, c, off:off + 64]), t)
        FG = sm(24)
        F3 = FG.rearrange("p (c h) -> p c h", c=4)
        IW = sm(16)
        I3 = IW.rearrange("p (c h) -> p c h", c=4)
        s1, s2, s3 = sm(24), sm(24), sm(24)
        t = tt(DV, F3, PJ[:, :, Q_FF:Q_FF + 6], rp(r0 + L_FB, 6).unsqueeze(1).broadcast_to((P, 4, 6)), ALU.add)
        t = ts(FG, FG, -1.0, ALU.mult, None, None, t)
        t = softplus(FG, s1, s2, s3, t)
        t_f = ts(FG, FG, -1.0, ALU.mult, None, None, t)
        ts(I3, PJ[:, :, Q_IW:Q_IW + 4], 0.5, ALU.mult, None, None)
        fence()
        blocks = [lambda m, k=k: PJ[:, m, k:k + P] for k in (Q_FQ, Q_FQ + 128, Q_FQ + 256, Q_FK, Q_FK + 128, Q_FK + 256,
                                                             Q_DQ, Q_DQ + 128, Q_DK, Q_DK + 128, Q_SQ, Q_SQ + 128,
                                                             Q_SQ + 256)]
        blocks += [lambda m: KD[:, m, 0:128], lambda m: PJ[:, m, Q_IQ:Q_IQ + 128],
                   lambda m: PJ[:, m, Q_IQ + 128:Q_IQ + 256], lambda m: KD[:, m, 128:256]]
        turn(lambda m, f: blocks[f](m), 17, lambda f: QT[:, f, :], [(), (), (), ()])
        fence()
        FQ, FK, DQ, DK, SQ, SK, IQ, IK = 0, 3, 6, 8, 10, 13, 14, 16
        CG = sm(24)
        b, fr = psum.take()
        for i in range(4):
            for j in range(i + 1):
                t = PE(lambda e, i=i, j=j: e.matmul(banks[b][:, i * 6:i * 6 + 6], TRI if j == i else ONE,
                                                    F3[:, j, :], start=(j == 0), stop=(j == i)), *fr)
        t = DV(lambda e: e.tensor_copy(CG, banks[b][:, 0:24]), t)
        psum.give(b, t)
        for h in range(6):
            b, fr = psum.take()
            for i in range(4):
                for j in range(i + 1):
                    t = PE(lambda e, i=i, j=j, h=h, b=b: e.matmul(
                        banks[b][:, i * P:(i + 1) * P], F3[:, j, h:h + 1].broadcast_to((P, P)),
                        TRI if j == i else ONE, start=(j == 0), stop=(j == i)), *fr)
            t = AC(lambda e, h=h, b=b: e.mul(PJ[:, :, h * P:(h + 1) * P],
                                             banks[b][:, :].rearrange("p (c s) -> p c s", c=4), -1.0), t)
            psum.give(b, t)
        fence()
        rb = Slots([0, 1, 2])
        b3 = lambda x: x.rearrange("p (c s) -> p c s", s=P)
        sel = {}
        for i in (1, 2, 3):
            W = (i + 1) * P
            acc = sel[i] = PJ[:, 0:i + 1, Q_DQ + (i - 1) * P:Q_DQ + i * P]
            ta = []
            for h in range(4):
                rr = 64 * (h % 2)
                b, fr = psum.take()
                t = PE(lambda e, b=b, h=h, rr=rr, i=i, W=W: e.matmul(
                    banks[b][:, 0:W], QT[rr:rr + 64, IQ + h // 2, i * P:(i + 1) * P], QT[rr:rr + 64, IK, 0:W],
                    start=True, stop=True), *fr)
                n, fn = rb.take()
                t = act(scr[n][:, 0:W], banks[b][:, 0:W], ACT.Relu, t, *fn, scale=0.125)
                psum.give(b, t)
                if h == 0:
                    t = ts(acc, b3(scr[n][:, 0:W]), I3[:, i, 0:1], ALU.mult, None, None, t)
                else:
                    t = stt(acc, b3(scr[n][:, 0:W]), I3[:, i, h:h + 1], acc, ALU.mult, ALU.add, t, *ta)
                ta = [t]
                rb.give(n, t)
            tt(DV, acc, acc, b3(kc(K_CAUS + 512 - W, W)), ALU.add, *ta)
        m8 = sm(24)
        ti = {i: DV.now() for i in (1, 2, 3)}
        for k in range(16):
            for i in (1, 2, 3):
                mv = m8[:, (i - 1) * 8:i * 8]
                ti[i] = DV(lambda e, i=i, mv=mv: e.max(mv, sel[i]), ti[i])
            for i in (1, 2, 3):
                mv = m8[:, (i - 1) * 8:i * 8]
                ti[i] = DV(lambda e, i=i, mv=mv: e.match_replace(sel[i], mv, sel[i], LOW), ti[i])
        for i in (1, 2, 3):
            ti[i] = ts(sel[i], sel[i], -2e38, ALU.is_gt, -BIG, ALU.mult, ti[i])
        fence()
        O = XTt[:, :].rearrange("p (m d) -> p m d", m=4)
        units = []
        mk = Slots([0, 1])
        fmv = [WRt[:, 0:512], WRt[:, 512:1024]]
        dtmp = [PJ[:, k, Q_IQ:Q_IQ + 256].rearrange("p (h d) -> p h d", d=64) for k in range(2)]
        Q3 = lambda f, rr, n, i: QT[rr:rr + n, f, i * P:(i + 1) * P]
        for i in range(4):
            W = (i + 1) * P
            caus = kc(K_CAUS + 512 - W, W)

            def done_f(bank, r, t, tr, i=i):
                return scale_heads(O[:, i, 0:384].rearrange("p (h d) -> p h d", d=64), bank, r, 6, 0, t, tr)

            def done_s(bank, r, t, tr, i=i):
                return scale_heads(O[:, i, 640:1024].rearrange("p (h d) -> p h d", d=64), bank, r, 6, 0, t, tr)

            def done_d(bank, r, t, tr, i=i):
                r2 = r.rearrange("p (h m) -> p h m", m=2)
                x = dtmp[i % 2]
                ov = O[:, i, 384:640].rearrange("p (h d) -> p h d", d=64)
                bv = bank[:, :].rearrange("p (h m d) -> p h m d", m=2, d=64)
                t1 = ts(r2[:, :, 1], r2[:, :, 1], ld[:, 2:3], ALU.mult, None, None, tr)
                t2 = tt(DV, ov, bv[:, :, 0, :], r2[:, :, 0].unsqueeze(2).broadcast_to((P, 4, 64)), ALU.mult, t, tr)
                t1 = tt(DV, x, bv[:, :, 1, :], r2[:, :, 1].unsqueeze(2).broadcast_to((P, 4, 64)), ALU.mult, t1, t)
                return tt(DV, ov, ov, x, ALU.add, t1, t2)

            for h in range(6):
                rr = 64 * (h % 2)

                def mask(h=h, i=i, W=W, caus=caus):
                    n, fr = mk.take()
                    v = fmv[n][:, 0:W].rearrange("p (c s) -> p c s", s=P)
                    t = stt(v, PJ[:, 0:i + 1, h * P:(h + 1) * P], CG[:, i * 6 + h:i * 6 + h + 1],
                            caus.rearrange("p (c s) -> p c s", s=P), ALU.add, ALU.add, *fr)
                    return fmv[n][:, 0:W], (t,)

                def free(t, cnt=[0], i=i, h=h):
                    mk.give((6 * i + h) % 2, t)
                units.append(dict(i=i, q=Q3(FQ + h // 2, rr, 64, i), k=QT[rr:rr + 64, FK + h // 2, 0:W], mask=mask,
                                  free=free, times=None,
                                  values=lambda kb, h=h: PJ[:, kb, Q_FV + h * 64:Q_FV + h * 64 + 64], slot=h,
                                  done=done_f if h == 5 else None))
            for x in range(8):
                rr = 32 * (x % 4)
                units.append(dict(i=i, q=Q3(DQ + x // 4, rr, 32, i), k=QT[rr:rr + 32, DK + x // 4, 0:W], mask=caus,
                                  times=None, values=lambda kb, x=x: PJ[:, kb, Q_DV + (x // 2) * 64:Q_DV + (x // 2) * 64 + 64],
                                  slot=x, done=done_d if x == 7 else None))
            for h in range(6):
                rr = 64 * (h % 2)
                units.append(dict(i=i, q=Q3(SQ + h // 2, rr, 64, i), k=QT[rr:rr + 64, SK, 0:W],
                                  mask=sel[i] if i else caus, times=None,
                                  values=lambda kb: PJ[:, kb, Q_SV:Q_SV + 64], slot=h,
                                  done=done_s if h == 5 else None))
        attention(units)
        fence()
        NO = sm(16)
        tprev = []
        for c in range(4):
            t = act(scr[0][:, 0:256], O[:, c, 384:640], ACT.Square, *tprev)
            t = DV(lambda e, c=c: e.tensor_reduce(NO[:, c * 4:c * 4 + 4], scr[0][:, 0:256].rearrange("p (h d) -> p h d", d=64),
                                                  AX, ALU.add), t)
            tprev = [t]
        t = inv_root(NO, NO, 1.0 / 64, t, factor=1.0 - lam_init)
        ready = []
        for c in range(4):
            v = O[:, c, 384:640].rearrange("p (h d) -> p h d", d=64)
            t1 = tt(DV, v, v, NO[:, c * 4:c * 4 + 4].unsqueeze(2).broadcast_to((P, 4, 64)), ALU.mult, t)
            ready.append([tt(PL, v, v, rp(r0 + L_SUB, 64).unsqueeze(1).broadcast_to((P, 4, 64)), ALU.mult, t1)])
        o_at, o_cols = halves(0, 8)
        tx = turn(lambda m, f: O[:, m, f * P:(f + 1) * P], 8, o_at, ready)
        return product_out(o_cols, 8, a["w_out_2"][l], None, None, tuple(tx), x_tmp)

    SM0 = small[0]
    steps = []
    nw = a["norm_w"]
    for l in range(2):
        fw = [[a[n][l, s] for n in ("ffn_w_gate", "ffn_w_up", "ffn_w_down")] for s in range(2)]
        steps.append(lambda t, l=l, fw=fw: ffn(3 * l, *fw[0], nw[l, 1:2], 0.5, t))
        steps.append(even if l == 0 else odd)
        steps.append(lambda t, l=l, fw=fw: ffn(3 * l + 2, *fw[1], nw[l, 5:6], 0.5, t))
    for l in range(2):
        steps.append(lambda t, l=l: mixer2(l, t))
        gu = a["w_gate_up_2"][l]
        steps.append(lambda t, l=l, gu=gu: ffn(7 + 2 * l, gu[:, 0:FF], gu[:, FF:2 * FF], a["w_down_2"][l], None, None, t))
    toks = [T_IN]
    for n, step in enumerate(steps[:upto]):
        toks = step(toks)
        fence()
    SP.quiet(lambda e: e.dma_start(out.rearrange("b (m p) d -> p (b m) d", p=P), H).then_inc(s_out, 16), *toks)
    SP.wait((s_out, 16))


def constants():
    p = np.arange(P)
    c = np.zeros((P, K_N), np.float32)
    c[:, K_ID:K_ID + P] = np.eye(P)
    c[:, K_TRI:K_TRI + P] = p[:, None] <= p[None, :]
    c[:, K_ONE:K_ONE + P] = 1
    c[:, K_LOW:K_LOW + P] = p[None, :] < p[:, None]

    def level(b):
        i, j = p[:, None], p[None, :]
        return ((i // (2 * b) == j // (2 * b)) & ((i // b) % 2 == 1) & ((j // b) % 2 == 0)).astype(np.float32)
    ce = np.zeros((P, E_N), np.float32)
    ce[:, E_M1:E_M1 + P] = level(1)
    for n in range(1, 7):
        ce[:, E_LV + (n - 1) * P:E_LV + n * P] = level(2 ** n).T
    delta = p[:, None] - (np.arange(512)[None, :] - 384)
    c[:, K_CAUS:K_CAUS + 512] = np.where(delta >= 0, 0.0, -BIG)
    times = ((delta >= 0) & (delta <= 128)).astype(np.float32) + ((delta >= 0) & (delta % 4 == 0)) \
        + ((delta >= 0) & (delta % 16 == 0))
    ce[:, E_CM:E_CM + 512] = times
    for k0, dh in ((K_R64, 64), (K_R32, 32)):
        rot = dh // 4
        inv = (np.float32(1.0) / np.power(np.float32(500000.0), np.arange(0, rot, 2, dtype=np.float32) / np.float32(rot))
               ).astype(np.float32)
        ang = np.arange(S, dtype=np.float32)[:, None] * inv[None, :]
        for k, f in ((0, np.cos), (1, np.sin)):
            v = f(ang).astype(np.float32).reshape(4, P, rot // 2).transpose(1, 0, 2).reshape(P, -1)
            c[:, k0 + k * v.shape[1]:k0 + (k + 1) * v.shape[1]] = v
    return c, ce


WHOLE = ["x", "norm_w", "ffn_w_gate", "ffn_w_up", "ffn_w_down", "even_w_in", "even_w_out", "odd_w_in", "odd_w_out",
         "w_in_2", "w_out_2", "w_gate_up_2", "w_down_2"]


def pack(inputs):
    v = {k: np.asarray(x) for k, x in inputs.items()}
    arrays = {k: np.ascontiguousarray(v[k]) for k in WHOLE}
    cols = []
    for x in (v["norm_w"][0, 0], v["norm_w"][0, 2], v["norm_w"][0, 4], v["norm_w"][1, 0], v["norm_w"][1, 2],
              v["norm_w"][1, 4], v["attn_norm_2"][0], v["ffn_norm_2"][0], v["attn_norm_2"][1], v["ffn_norm_2"][1]):
        cols.append(x.reshape(8, P).T)
    for x, n in ((v["even_conv_w"][0], 12), (v["odd_conv_w"][0], 24)):
        cols.append(x.reshape(4, n, P).transpose(2, 1, 0).reshape(P, -1))
    cols.append(v["odd_conv_b"][0].reshape(24, P).T)
    cols.append(v["odd_out_norm_w"][0].reshape(16, P).T)
    cols.append(v["even_head_norm_w"][0][:, None])
    arrays["colp"] = np.ascontiguousarray(np.concatenate(cols, axis=1))
    rows = [v["even_a_log"][0], v["even_dt_bias"][0], v["odd_a_log"][0], v["odd_dt_bias"][0], v["odd_d_skip"][0]]
    for l in range(2):
        rows += [v[n + "_2"][l] for n in ("fox_fb", "fox_qn", "fox_kn", "diff_qn", "diff_kn", "diff_subln", "dsa_qn",
                                          "dsa_kn", "diff_lq1", "diff_lk1", "diff_lq2", "diff_lk2")]
    arrays["rowp"] = np.ascontiguousarray(np.concatenate(rows)[None, :])
    arrays["consts"], arrays["consts_e"] = constants()
    return arrays


def program(nc, arrays, upto=99):
    a = {k: nc.dram_tensor("in_" + k, list(x.shape), F32, kind="ExternalInput").ap() for k, x in arrays.items()}
    out = nc.dram_tensor("out_y", [1, S, D], F32, kind="ExternalOutput").ap()
    build(nc, a, out, upto)


def kernel(**inputs):
    import concourse.bacc as bacc
    from concourse.bass_utils import run_bass_kernel_spmd

    nc = bacc.Bacc("TRN2", target_bir_lowering=False, num_devices=1)
    arrays = pack(inputs)
    program(nc, arrays)
    r = run_bass_kernel_spmd(nc, [{"in_" + k: x for k, x in arrays.items()}], core_ids=[0])
    return r.results[0]["out_y"]
```

```python
import numpy as np
from contextlib import ExitStack

import concourse.bass as bass
from concourse import mybir
from concourse.alu_op_type import AluOpType as ALU

ACT = mybir.ActivationFunctionType
F32 = mybir.dt.float32
F32R = mybir.dt.float32r
AX = mybir.AxisListType.X

P = 128
S = 512
D = 1024
FF = 2816
NJ = FF // P
EPS = 1e-6
BIG = 1e30
LOW = -3e38
RAW = 4
PACE = 2
HOLD = 2
LAG = 1
DPACE = 2
SPL = 3
SLOT = 1024
AHEAD = 2

C_PRE, C_ECONV, C_OCONV, C_OBIAS, C_ONORM, C_HNORM, C_N = 0, 80, 128, 224, 248, 264, 265
R_EA, R_EDT, R_OA, R_ODT, R_DSK, R_L = 0, 4, 8, 40, 72, 104
L_FB, L_FQ, L_FK, L_DQ, L_DK, L_SUB, L_SQ, L_SK, L_LQ1, L_LK1, L_LQ2, L_LK2, L_N = (
    0, 6, 70, 134, 166, 198, 262, 326, 390, 422, 454, 486, 518)
R_N = R_L + 2 * L_N
K_ID, K_TRI, K_ONE, K_LOW, K_CAUS, K_R64, K_R32, K_N = (0, 128, 256, 384, 512, 1024, 1088, 1120)
E_M1, E_LV, E_CM, E_N = 0, 128, 896, 1408
Q_FQ, Q_FK, Q_FV, Q_FF, Q_DQ, Q_DK, Q_DV, Q_SQ, Q_SK, Q_SV, Q_IQ, Q_IK, Q_IW, Q_N = (
    0, 384, 768, 1152, 1158, 1414, 1670, 1926, 2310, 2374, 2438, 2694, 2758, 2762)


class Queue:

    def __init__(self, sem, engine):
        self.sem, self.n, self.engine, self.seen = sem, 0, engine, {}

    def wait(self, *toks):
        need = {}
        for sem, v in toks:
            if v > self.seen.get(id(sem), 0) and v > need.get(id(sem), (sem, 0))[1]:
                need[id(sem)] = (sem, v)
        for sem, v in need.values():
            self.seen[id(sem)] = v
            if self.engine is not None:
                self.engine.wait_ge(sem, v)

    def quiet(self, fn, *toks):
        self.wait(*toks)
        if self.engine is not None:
            fn(self.engine)

    def __call__(self, fn, *toks):
        self.wait(*toks)
        self.n += 1
        if self.engine is not None:
            fn(self.engine).then_inc(self.sem, 1)
        return (self.sem, self.n)

    def now(self):
        return (self.sem, self.n)


class Slots:

    def __init__(self, items):
        self.free = [(x, ()) for x in items]

    def take(self):
        return self.free.pop(0)

    def give(self, item, *toks):
        self.free.append((item, toks))


def build(nc, a, out, upto=99):
    ctx = ExitStack()
    with ctx:
        def sb(name, n):
            return ctx.enter_context(nc.sbuf_tensor(name, [P, n], F32))

        def sem(name):
            return ctx.enter_context(nc.semaphore(name))

        plan = (("H", 4 * D), ("X", 8192), ("W", RAW * SLOT), ("WS", SPL * 2 * SLOT), ("AR", 25088), ("CP", C_N + 7),
                ("RP", R_N + 4), ("KC", K_N), ("WR", D), ("SM", 1600))
        base = -(-nc.sbuf_base // 32) * 32
        sb("all", sum(n for _, n in plan) + 8)
        at, place = base, {}
        for name, n in plan:
            place[name] = at
            assert n % 8 == 0
            at += 4 * n
        size = dict(plan)

        def put(name, where, dt):
            return nc.alloc_sbuf_tensor_at(name, [P, size[where]], dt, offset=place[where])

        Ht, Xf, Wt, AR, CPt, RPt, KCt, WRt, SMt = (put("f_" + n, n, F32) for n in (
            "H", "X", "W", "AR", "CP", "RP", "KC", "WR", "SM"))
        Xr, WSr, ARr = (put("r_" + n, n, F32R) for n in ("X", "WS", "AR"))
        banks = [ctx.enter_context(nc.psum_tensor(f"ps{i}", [P, 512], F32)) for i in range(8)]
        wsem = [sem(f"ws{i}") for i in range(RAW)]
        rsem = sem("wr0")
        s_in = sem("s_in")
        s_out = sem("s_out")
        sems = [sem(n) for n in ("s_pe", "s_dv", "s_ac", "s_pl", "s_sp")]
        s_ev = sem("s_ev")
        mem = (Ht, Xf, Xr, Wt, WSr, AR, ARr, CPt, RPt, KCt, WRt, SMt, banks, wsem, rsem, s_in, s_ev, s_out, sems)
        order = []
        schedule(a, out, mem, None, None, upto, order, True)
        block = ctx.enter_context(nc.Block())

        @block.sync
        def _(e):
            schedule(a, out, mem, 4, e, upto, order, False)

        @block.tensor
        def _(e):
            schedule(a, out, mem, 0, e, upto, order, False)

        @block.vector
        def _(e):
            schedule(a, out, mem, 1, e, upto, order, False)

        @block.scalar
        def _(e):
            schedule(a, out, mem, 2, e, upto, order, False)

        @block.gpsimd
        def _(e):
            schedule(a, out, mem, 3, e, upto, order, False)


def schedule(a, out, mem, turn_of, engine, upto, order, listing):
    Ht, Xf, Xr, Wt, WSr, AR, ARr, CPt, RPt, KCt, WRt, SMt, banks, wsem, rsem, s_in, s_ev, s_out, sems = mem
    H = Ht[:, :].rearrange("p (m d) -> p m d", m=4)
    XTt = Xf[:, 0:4096]
    SC = AR[:, 20480:25088]
    XH = Xr[:, 0:4096].rearrange("p (f s) -> p f s", s=S)
    XL = Xr[:, 4096:8192].rearrange("p (f s) -> p f s", s=S)
    psum = Slots(range(8))
    raw = Slots(range(RAW))
    split = Slots(range(SPL))
    wcnt = [0] * RAW
    rcnt = [0]
    rows = Slots([0])
    ready_w = []
    asked = [0]
    pace = [1]
    PE, DV, AC, PL, SP = (Queue(x, engine if k == turn_of else None) for k, x in enumerate(sems))

    def cp(c, n=1):
        return CPt[:, c:c + n]

    def rp(c, n):
        return RPt[:, c:c + n]

    def kc(c, n=128):
        return KCt[:, c:c + n]

    IDN = kc(K_ID)
    TRI = kc(K_TRI)
    ONE = kc(K_ONE)

    def arena(off, n):
        return AR[:, off:off + n]

    small = [0]

    def sm(n):
        o = small[0]
        small[0] += n
        assert small[0] <= 1600
        return SMt[:, o:o + n]

    def fence():
        t = [q.now() for q in (PE, DV, AC, PL)]
        for q in (PE, DV, AC, PL):
            q.wait(*t)

    def settle():
        t = [q.now() for q in (PE, DV, AC, PL)]
        for q in (DV, AC, PL):
            q.wait(*t)

    threads = []

    def advance(k=1):
        for g in list(threads):
            for _ in range(k):
                if next(g, 0) is None:
                    continue
                threads.remove(g)
                break

    def beside(g):
        threads.append(g)
        return g

    def finish(*gs):
        for g in gs or list(threads):
            for _ in g:
                pass
            if g in threads:
                threads.remove(g)

    flip = [0]

    def evac(dst, src, *toks, scale=None):
        flip[0] ^= 1
        if flip[0]:
            if scale is None:
                return AC(lambda e: e.copy(dst, src), *toks)
            return AC(lambda e: e.mul(dst, src, scale), *toks)
        if scale is None:
            return DV(lambda e: e.tensor_copy(dst, src), *toks)
        return DV(lambda e: e.tensor_scalar(dst, src, scale, None, ALU.mult), *toks)

    def act(dst, src, f, *toks, **kw):
        return AC(lambda e: e.activation(dst, src, f, **kw), *toks)

    def tt(q, dst, x, y, op, *toks):
        return q(lambda e: e.tensor_tensor(dst, x, y, op), *toks)

    def ts(dst, x, s1, op0, s2, op1, *toks, q=None):
        q = q or DV
        if s2 is None:
            return q(lambda e: e.tensor_scalar(dst, x, s1, None, op0), *toks)
        return q(lambda e: e.tensor_scalar(dst, x, s1, s2, op0, op1), *toks)

    def stt(dst, x, s, y, op0, op1, *toks):
        return DV(lambda e: e.scalar_tensor_tensor(dst, x, s, y, op0, op1), *toks)

    def hi(dst, src, *toks, scale=None):
        if scale is None:
            return AC(lambda e: e.copy(dst, src), *toks)
        return AC(lambda e: e.mul(dst, src, scale), *toks)

    def lo(dst, src, high, *toks, scale=None):
        if scale is None:
            return DV(lambda e: e.tensor_tensor(dst, src, high.bitcast(F32), ALU.subtract), *toks)
        return DV(lambda e: e.scalar_tensor_tensor(dst, src, scale, high.bitcast(F32), ALU.mult, ALU.subtract), *toks)

    def bring(n):
        src, nk, width = order[n]
        i, fr = raw.take()
        k = nk * width
        src = src.rearrange("(k p) n -> p k n", p=P)
        wcnt[i] += 16
        v = Wt[:, i * SLOT:i * SLOT + k]
        SP.quiet(lambda e: e.dma_start(v.rearrange("p (k n) -> p k n", n=width), src).then_inc(wsem[i], 16), *fr)
        x, fs = split.take()
        h = WSr[:, x * 2 * SLOT:x * 2 * SLOT + k]
        l = WSr[:, x * 2 * SLOT + SLOT:x * 2 * SLOT + SLOT + k]
        t1 = hi(h, v, (wsem[i], wcnt[i]), *fs)
        t2 = lo(l, v, h, t1, *fs)
        raw.give(i, t2)
        ready_w.append((h.rearrange("p (k n) -> p k n", n=width), l.rearrange("p (k n) -> p k n", n=width), x, t2))

    def load(src, nk, n, ahead=AHEAD):
        if listing:
            advance(pace[0])
            order.append((src, nk, n))
            return None, None, 0, (sems[1], 0)
        advance(pace[0])
        asked[0] += 1
        while len(ready_w) < min(asked[0] + ahead, len(order)):
            bring(len(ready_w))
        return ready_w[asked[0] - 1]

    def done_with(x, t):
        if not listing:
            split.give(x, t)

    def load_row(src):
        i, fr = rows.take()
        dst = WRt[:, 0:D]
        rcnt[0] += 16
        SP.quiet(lambda e: e.dma_start(dst, src.partition_broadcast(P)).then_inc(rsem, 16), *fr)
        return dst, i, (rsem, rcnt[0])

    T_IN = (s_in, 64)
    for dst, src in ((H, a["x"].rearrange("b (m p) d -> p (b m) d", p=P)), (KCt[:, :], a["consts"]),
                     (CPt[:, 0:C_N], a["colp"])):
        SP.quiet(lambda e, dst=dst, src=src: e.dma_start(dst, src).then_inc(s_in, 16))
    SP.quiet(lambda e: e.dma_start(RPt[:, 0:R_N], a["rowp"].partition_broadcast(P)).then_inc(s_in, 16))
    for q in (PE, DV, AC, PL):
        q.wait(T_IN)

    def gemm_t(x, nk, w, c0, n, use, tx):
        for c in range(0, n, 256):
            bs = [psum.take() for _ in range(2)]
            for k0 in range(0, nk, 4):
                wh, wl, i, tk = load(w[k0 * P:(k0 + 4) * P, c0 + c:c0 + c + 256], 4, 256)
                for j in range(2):
                    b, fr = bs[j]
                    for k in range(k0, k0 + 4):
                        xh, xl = x(k)
                        PE.quiet(lambda e: e.matmul(banks[b][:, :], wh[:, k - k0, j * P:(j + 1) * P], xh,
                                                    start=(k == 0), stop=False), tk, tx[k], *fr)
                        PE.quiet(lambda e: e.matmul(banks[b][:, :], wh[:, k - k0, j * P:(j + 1) * P], xl,
                                                    start=False, stop=False))
                        last = (lambda e: e.matmul(banks[b][:, :], wl[:, k - k0, j * P:(j + 1) * P], xh,
                                                   start=False, stop=(k == nk - 1)))
                        if k == k0 + 3 and (j == 1 or k == nk - 1):
                            t = PE(last)
                            if k == nk - 1:
                                use(c // P + j, b, t)
                        else:
                            PE.quiet(last)
                done_with(i, t)

    def gemm(x, nk, w, c0, n, use, toks=(), hold=1):
        bs = [psum.take() for _ in range(4)]
        kg = 2 if n > 256 else 4 if n > 128 else 8
        groups = list(range(0, nk, kg))
        for held in [[k0] for k0 in groups[:-hold]] + [groups[-hold:]]:
            parts = [load(w[k0 * P:(k0 + kg) * P, c0:c0 + n], kg, n, AHEAD - y) for y, k0 in enumerate(held)]
            ends = held[-1] + kg == nk
            ks = [(k, part, k - k0) for k0, part in zip(held, parts) for k in range(k0, k0 + kg)]
            steps = [(m, z) for m in range(4) for z in ks] if ends else [(m, z) for z in ks for m in range(4)]
            t_part = {}
            for m, (k, (wh, wl, i, tk), y) in steps:
                b, fr = bs[m]
                xh, xl = x(k, m)
                PE.quiet(lambda e: e.matmul(banks[b][:, 0:n], xh, wh[:, y, :], start=(k == 0), stop=False),
                         tk, *(toks[k:k + 1] if len(toks) > 1 else toks), *fr)
                PE.quiet(lambda e: e.matmul(banks[b][:, 0:n], xh, wl[:, y, :], start=False, stop=False))
                last = (lambda e: e.matmul(banks[b][:, 0:n], xl, wh[:, y, :], start=False, stop=(k == nk - 1)))
                if k == nk - 1 or (y == kg - 1 and m == 3):
                    t = PE(last)
                    t_part[i] = t
                    if k == nk - 1:
                        use(m, b, t)
                else:
                    PE.quiet(last)
            for part in parts:
                done_with(part[2], t_part[part[2]])

    def turn(src, nf, dst, toks, scale=None, wait=()):
        done = []
        for f0 in range(0, nf, 8):
            fs = range(f0, min(nf, f0 + 8))
            bs = {f: psum.take() for f in fs}
            last = {}
            for m in range(4):
                for f in fs:
                    b, fr = bs[f]
                    last[f] = PE(lambda e, b=b, m=m, f=f: e.transpose(banks[b][:, m * P:(m + 1) * P], src(m, f), IDN),
                                 *toks[m], *fr)
            for f in fs:
                d, v, sc = dst(f), banks[bs[f][0]][:, :], scale(f) if scale else None
                if isinstance(d, tuple):
                    t = hi(d[0], v, last[f], *wait, scale=sc)
                    t = lo(d[1], v, d[0], t, scale=sc)
                else:
                    t = evac(d, v, last[f], *wait, scale=sc)
                psum.give(bs[f][0], t)
                done.append(t)
        return done

    ss8, ss4, ss42, rst, wm = sm(8), sm(4), sm(4), sm(8), sm(1)
    scr = [SC[:, i * 512:(i + 1) * 512] for i in range(9)]

    def inv_root(dst, src, mul, *toks, factor=None):
        t = ts(dst, src, mul, ALU.mult, EPS, ALU.add, *toks)
        t = act(dst, dst, ACT.Sqrt, t)
        t = DV(lambda e: e.reciprocal(dst, dst), t)
        if factor is not None:
            t = ts(dst, dst, factor, ALU.mult, None, None, t)
        return t

    def xs_at(f):
        return XH[:, f, :], XL[:, f, :]

    def x_cols(k, m):
        return XH[:, k, m * P:(m + 1) * P], XL[:, k, m * P:(m + 1) * P]

    def halves(off, nf):
        h, l = (ARr[:, off + y * nf * S:off + (y + 1) * nf * S].rearrange("p (f s) -> p f s", s=S) for y in range(2))
        return (lambda f: (h[:, f, :], l[:, f, :])), (lambda k, m: (h[:, k, m * P:(m + 1) * P], l[:, k, m * P:(m + 1) * P]))

    def junction(parts, row, factor, tmps, col, junk=None):
        xn = AR[:, 0:4096].rearrange("p (m d) -> p m d", m=4)
        end = () if parts is None else (parts[3, 1][1],)
        hv = lambda m, h: H[:, m, h * 512:(h + 1) * 512]
        st = [{} for _ in range(4)]
        if row is not None:
            w, wi, tw = load_row(row)
            f2 = factor * factor
        tmp = Slots(tmps[2:])
        used = []
        bs = {}

        def square(m):
            if row is not None:
                t = junk[m % 2] = AC(lambda e: e.activation(tmps[m % 2], banks[parts[m, 1][0]][:, :], ACT.Square,
                                                            accum_out=ss8[:, 2 * m + 1:2 * m + 2]), parts[m, 1][1],
                                     junk[m % 2])
                t = tt(DV, ss4[:, m:m + 1], ss8[:, 2 * m:2 * m + 1], ss8[:, 2 * m + 1:2 * m + 2], ALU.add, t)
                used.append(t)
                st[m]["t"] = ts(ss4[:, m:m + 1], ss4[:, m:m + 1], 1.0 / (D * f2), ALU.mult, EPS / f2, ALU.add, t)

        def root(m):
            if row is not None:
                t = act(ss4[:, m:m + 1], ss4[:, m:m + 1], ACT.Sqrt, st[m]["t"])
                st[m]["t"] = DV(lambda e: e.reciprocal(rst[:, 4 + m:5 + m], ss4[:, m:m + 1]), t)

        def add(m):
            out = []
            for h in range(2):
                if row is not None:
                    b = parts[m, h][0]
                    n, fr = tmp.take()
                    tb = stt(n, banks[b][:, :], rst[:, 4 + m:5 + m], w[:, h * 512:(h + 1) * 512], ALU.mult, ALU.mult,
                             st[m]["t"], tw, *fr)
                    psum.give(b, tb)
                    t2 = tt(PL if h else DV, hv(m, h), hv(m, h), n, ALU.add, tb)
                    tmp.give(n, t2)
                    used.append(t2)
                    out.append(t2)
                    if m == 3 and h == 1:
                        rows.give(wi, tb)
                elif parts is not None:
                    b, t = parts[m, h]
                    t = tt(DV, hv(m, h), banks[b][:, :], hv(m, h), ALU.add, t)
                    psum.give(b, t)
                    out.append(t)
            st[m]["h"] = out

        def square2(m):
            if col is not None:
                t = AC(lambda e: e.activation(xn[:, m, :], H[:, m, :], ACT.Square, accum_out=ss42[:, m:m + 1]),
                       *st[m]["h"], *end)
                st[m]["t"] = ts(ss42[:, m:m + 1], ss42[:, m:m + 1], 1.0 / D, ALU.mult, EPS, ALU.add, t)

        def root2(m):
            if col is not None:
                t = act(ss42[:, m:m + 1], ss42[:, m:m + 1], ACT.Sqrt, st[m]["t"])
                st[m]["t"] = DV(lambda e: e.reciprocal(rst[:, m:m + 1], ss42[:, m:m + 1]), t)

        def scaled(m):
            if col is not None:
                t = st[m]["t"]
                st[m]["t"] = AC(lambda e: e.mul(xn[:, m, 0:512], hv(m, 0), rst[:, m:m + 1]), t)
                st[m]["t1"] = ts(xn[:, m, 512:D], hv(m, 1), rst[:, m:m + 1], ALU.mult, None, None, t)

        def turn_one(m, f):
            b, fr = bs[f]
            return PE(lambda e: e.transpose(banks[b][:, m * P:(m + 1) * P], xn[:, m, f * P:(f + 1) * P], IDN),
                      st[m]["t1" if f > 3 else "t"], *fr)

        def turned(m):
            if col is not None and m < 3:
                for f in range(6):
                    if m == 0:
                        bs[f] = psum.take()
                    turn_one(m, f)

        stages = [square, root, add, square2, root2, scaled, turned]
        for x in range(3 * LAG + len(stages)):
            if x in (3 * LAG - 1, 3 * LAG) and not listing and parts is not None:
                while len(ready_w) < min(asked[0] + x - 3 * LAG + 2, len(order)):
                    bring(len(ready_w))
            for m in range(4):
                if 0 <= x - m * LAG < len(stages):
                    stages[x - m * LAG](m)
        if col is None:
            return [st[m]["h"] for m in range(4)]
        done = []
        last = {}
        for f in range(6):
            last[f] = turn_one(3, f)
        for f in (6, 7):
            bs[f] = psum.take()
            for m in range(4):
                last[f] = turn_one(m, f)
        warm(ACT.Silu)
        for f in range(8):
            v, sc = banks[bs[f][0]][:, :], cp(C_PRE + col * 8 + f)
            xh, xl = xs_at(f)
            t = hi(xh, v, last[f], *used, *end, scale=sc)
            t = lo(xl, v, xh, t, scale=sc)
            psum.give(bs[f][0], t)
            done.append(t)
        return done

    def warm(f):
        return act(wm, rp(0, 1), f)

    def product_out(x, nk, w, row, factor, toks, tmps, col):
        parts = {}

        def use(h):
            def f(m, b, t):
                parts[m, h] = (b, t)
                if h == 0 and row is not None:
                    junk[m % 2] = AC(lambda e: e.activation(tmps[m % 2], banks[b][:, :], ACT.Square,
                                                            accum_out=ss8[:, 2 * m:2 * m + 1]), t, junk[m % 2])
            return f
        junk = [(sems[2], 0), (sems[2], 0)]
        gemm(x, nk, w, 0, 512, use(0), toks)
        warm(ACT.Sqrt)
        gemm(x, nk, w, 512, 512, use(1), hold=HOLD)
        return junction(parts, row, factor, tmps, col, junk)

    x_tmp = [Xf[:, i * 512:(i + 1) * 512] for i in range(6)]

    def ffn(wg, wu, wd, row, factor, tx, col):
        g_at, g_cols = halves(0, NJ)
        got = {}
        ready = {}
        tmp = Slots([scr[5], scr[6], scr[7], scr[8]])

        def use(kind, j, b, t):
            got[kind, j] = (b, t)
            if ("g", j) in got and ("u", j) in got:
                (bg, tg), (bu, tu) = got["g", j], got["u", j]
                v, fr = tmp.take()
                gh, gl = g_at(j)
                t = act(v, banks[bg][:, :], ACT.Silu, tg, *fr)
                psum.give(bg, t)
                t = tt(DV, v, banks[bu][:, :], v, ALU.mult, t, tu)
                psum.give(bu, t)
                t = hi(gh, v, t)
                ready[j] = t = lo(gl, v, gh, t)
                tmp.give(v, t)

        for j in range(0, NJ, 2):
            for kind, w in (("g", wg), ("u", wu)):
                gemm_t(xs_at, 8, w, j * P, 256, lambda i, b, t: use(kind, j + i, b, t), tx)
        return product_out(g_cols, NJ, wd, row, factor, (ready[NJ - 1],), x_tmp, col)

    st_nm, st_l, st_r = sm(24), sm(24), sm(24)

    def attention(units, pieces=1, nb=9):
        sbuf = Slots(range(nb - 4) if nb > 8 else range(4))
        tbuf = Slots(range(nb - 4, nb) if nb > 8 else range(4, nb))
        stat = Slots([0, 1, 2])
        n = len(units)
        obank = [None]

        def scores(u):
            if u.get("start"):
                u["start"]()
            W = (u["i"] + 1) * P
            if u["slot"] == 0:
                u["o"], u["ofr"] = psum.take()
                u["st"], u["sfr"] = stat.take()
                obank[0] = u
            g = u["g"] = obank[0]
            b, fr = psum.take()
            wide = max(W, 256)
            qh, ql = u["q"]
            kh, kl = u["k"](wide)
            bw = banks[b][:, 0:wide]
            if len(kh.shape) != len(bw.shape):
                bw = bw.rearrange("p (a b) -> p a b", b=P)
            PE.quiet(lambda e: e.matmul(bw, qh, kh, start=True, stop=False), *fr)
            PE.quiet(lambda e: e.matmul(bw, ql, kh, start=False, stop=False))
            if len(kl.shape) != len(bw.shape):
                bw = banks[b][:, 0:wide].rearrange("p (a b) -> p a b", b=P)
            t = PE(lambda e: e.matmul(bw, qh, kl, start=False, stop=True))
            col = g["st"] * 8 + u["slot"]
            s, fs = sbuf.take()
            nm, l = st_nm[:, col:col + 1], st_l[:, col:col + 1]
            mask, tm = u["mask"]() if callable(u["mask"]) else (u["mask"], ())
            sv = scr[s][:, 0:W]
            bv = banks[b][:, 0:W]
            if len(mask.shape) == 3:
                sv = sv.rearrange("p (a b) -> p a b", b=P)
                bv = bv.rearrange("p (a b) -> p a b", b=P)
            t = DV(lambda e: e.tensor_tensor_reduce(sv, bv, mask, -1.0, 3e38, ALU.add,
                                                    ALU.min, nm), t, *fs, *g["sfr"], *tm)
            u["maskdone"] = t
            if u.get("free"):
                u["free"](t)
            psum.give(b, t)
            p = u["p"] = s
            t = AC(lambda e: e.activation(scr[p][:, 0:W], scr[p][:, 0:W], ACT.Exp, bias=nm, scale=-1.0,
                                          accum_out=l), t, *g["sfr"])
            if u["times"] is not None:
                t = DV(lambda e: e.tensor_tensor_reduce(scr[p][:, 0:W], scr[p][:, 0:W], u["times"], 1.0, 0.0,
                                                        ALU.mult, ALU.add, l), t)
            u["t"] = t

        def turned(u):
            nb = u["i"] + 1
            b, fr = psum.take()
            for kb in range(nb):
                t = PE(lambda e, kb=kb: e.transpose(banks[b][:, kb * P:(kb + 1) * P],
                                                    scr[u["p"]][:, kb * P:(kb + 1) * P], IDN), u["t"], *fr)
            sbuf.give(u["p"], t)
            x, fx = tbuf.take()
            u["x"] = x
            t = evac(scr[x][:, 0:nb * P], banks[b][:, 0:nb * P], t, *fx)
            psum.give(b, t)
            u["t"] = t

        def values(u):
            nb = u["i"] + 1
            g = u["g"]
            for kb in range(nb):
                t = PE(lambda e, kb=kb: e.matmul(banks[g["o"]][:, u["slot"] * 64:u["slot"] * 64 + 64],
                                                 scr[u["x"]][:, kb * P:(kb + 1) * P], u["values"](kb),
                                                 start=(kb == 0), stop=(kb == nb - 1)), u["t"], *g["ofr"])
            tbuf.give(u["x"], t)
            if u["done"] is not None:
                c = g["st"] * 8
                w = u["slot"] + 1
                tr = DV(lambda e: e.reciprocal(st_r[:, c:c + w], st_l[:, c:c + w]), u["t"], *g["sfr"])
                ts_ = u["done"](banks[g["o"]], st_r[:, c:c + w], t, tr)
                psum.give(g["o"], ts_)
                stat.give(g["st"], ts_)

        for x in range(n + 5):
            if x < n:
                scores(units[x])
            if 0 <= x - 3 < n:
                turned(units[x - 3])
            if 0 <= x - 5 < n:
                values(units[x - 5])
            advance(pieces)

    def scale_heads(dst, bank, r, nh, c0, *toks):
        return tt(DV, dst, bank[:, c0 * 64:(c0 + nh) * 64].rearrange("p (h d) -> p h d", d=64),
                  r[:, c0:c0 + nh].unsqueeze(2).broadcast_to((P, nh, 64)), ALU.mult, *toks)

    def softplus(x, t1, t2, t3, *toks):
        t = ts(t1, x, -1.0, ALU.mult, None, None, *toks)
        t = tt(DV, t1, t1, x, ALU.min, t)
        yield
        t = act(t1, t1, ACT.Exp, t)
        yield
        t = ts(t2, t1, 2.0, ALU.add, None, None, t)
        t = DV(lambda e: e.reciprocal(t2, t2), t)
        t = tt(DV, t1, t1, t2, ALU.mult, t)
        t = tt(DV, t2, t1, t1, ALU.mult, t)
        t = ts(t3, t2, 2.0 / 19, ALU.mult, None, None, t)
        for k in range(8, 0, -1):
            if k % 3 == 0:
                yield
            t = stt(t3, t3, 2.0 / (2 * k + 1), t2, ALU.add, ALU.mult, t)
        t = stt(t3, t3, 2.0, t1, ALU.add, ALU.mult, t)
        sp_t[0] = stt(x, x, 0.0, t3, ALU.max, ALU.add, t)

    sp_t = [None]

    cbuf = Slots([0, 1, 2, 3])

    def conv(b, t, taps, bias):
        n, fr = cbuf.take()
        acc = scr[n]
        x = banks[b]
        t = AC(lambda e: e.mul(acc, x[:, :], cp(taps + 3)), t, *fr)
        for k in (2, 1, 0):
            s = 3 - k
            t = stt(acc[:, s:S], x[:, 0:S - s], cp(taps + k), acc[:, s:S], ALU.mult, ALU.add, t)
        psum.give(b, t)
        if bias is None:
            t = act(acc, acc, ACT.Silu, t)
        else:
            t = act(acc, acc, ACT.Silu, t, bias=cp(bias))
        return n, t

    class Later:

        def __init__(self, lag):
            self.lag, self.fns = lag, []

        def add(self, fn):
            self.fns.append(fn)
            if len(self.fns) > self.lag:
                self.fns.pop(0)()

        def flush(self):
            while self.fns:
                self.fns.pop(0)()

    def turn_block(n, t, dst):
        b, fr = psum.take()
        for c in range(4):
            tp = PE(lambda e, c=c: e.transpose(banks[b][:, c * P:(c + 1) * P], scr[n][:, c * P:(c + 1) * P], IDN),
                    t, *fr)
        te = evac(dst, banks[b][:, :].rearrange("p (c f) -> p c f", f=P), tp)
        psum.give(b, te)
        return tp, te

    def even(tx, col):
        w = a["even_w_in"][0]
        KE = arena(18944, E_N)

        def ke(c, n=128):
            return KE[:, c:c + n]
        QA = [ARr[:, y:y + 2048].rearrange("p (f s) -> p f s", s=S) for y in (0, 14336)]
        KA = [ARr[:, y:y + 2048].rearrange("p (f s) -> p f s", s=S) for y in (2048, 16384)]
        VA = arena(4096, 2048).rearrange("p (m d) -> p m d", m=4)
        ZB = arena(6144, 2048).rearrange("p (m d) -> p m d", m=4)
        QKV = arena(8192, 6144).rearrange("p (c f) -> p c f", c=4)
        OA, OB = (Xf[:, y:y + 2048].rearrange("p (m d) -> p m d", m=4) for y in (6144, 4096))
        small[0] = SM0
        GT = sm(32).rearrange("p (m d) -> p m d", m=4)

        def put(dst, scale=None):
            def use(j, b, t):
                psum.give(b, evac(dst(j), banks[b][:, :], t, scale=scale))
            return use

        def put2(dst, scale=None):
            def use(j, b, t):
                t = hi(dst[0][:, j, :], banks[b][:, :], t, scale=scale)
                psum.give(b, lo(dst[1][:, j, :], banks[b][:, :], dst[0][:, j, :], t, scale=scale))
            return use

        xk = xs_at
        xm = x_cols
        settle()
        AC.quiet(lambda e: e.dma_start(KE, a["consts_e"]).then_inc(s_ev, 16))
        later = Later(2)
        t_qkv, t_gt = [], []

        def use(j, b, t):
            n, t = conv(b, t, C_ECONV + 4 * j, None)

            def go():
                tp, te = turn_block(n, t, QKV[:, :, j * P:(j + 1) * P])
                cbuf.give(n, tp)
                t_qkv.append(te)
            later.add(go)
        gemm_t(xk, 8, w, 1536, 1536, use, tx)
        later.flush()

        for c0 in (0, 260):
            def use_z(m, b, t):
                n = min(260, 512 - c0)
                t = act(ZB[:, m, c0:c0 + n], banks[b][:, 0:n], ACT.Silu, t)
                if c0:
                    t = DV(lambda e: e.tensor_copy(GT[:, m, :], banks[b][:, 252:260]), t)
                    t_gt.append(t)
                psum.give(b, t)
            gemm(xm, 8, w, 3072 + c0, 260, use_z)
        GB = sm(16).rearrange("p (m d) -> p m d", m=4)
        GG = sm(16)
        G3 = GG.rearrange("p (m d) -> p m d", m=4)
        sa, sb_, sc_, ea4 = sm(16), sm(16), sm(16), sm(4)
        SQ = SC[:, 3584:4608]
        QS = sm(32)
        Q3 = QS.rearrange("p (c h) -> p c h", c=4)
        GC, EG, EL, EK, NB = sm(16), sm(16), sm(16), sm(16), sm(16)

        def norms():
            tprev = t_qkv
            for c in range(4):
                t = act(SQ, QKV[:, c, 0:1024], ACT.Square, *tprev)
                yield
                t = DV(lambda e: e.tensor_reduce(QS[:, c * 8:(c + 1) * 8], SQ.rearrange("p (h d) -> p h d", d=P),
                                                 AX, ALU.add), t)
                yield
                tprev = [t]
            t = ts(QS, QS, 1.0, ALU.mult, EPS, ALU.add, t)
            yield
            t = act(QS, QS, ACT.Sqrt, t)
            yield
            t = DV(lambda e: e.reciprocal(QS, QS), t)
            t = ts(Q3[:, :, 0:4], Q3[:, :, 0:4], float(P) ** -0.5, ALU.mult, None, None, t)
            for c in range(4):
                v = QKV[:, c, 0:1024].rearrange("p (h d) -> p h d", d=P)
                tt(DV, v, v, Q3[:, c, :].unsqueeze(2).broadcast_to((P, 8, P)), ALU.mult, t)
                yield

        def gates():
            t = act(GB, GT[:, :, 0:4], ACT.Exp, *t_gt, scale=-1.0)
            t1 = act(ea4, rp(R_EA, 4), ACT.Exp)
            yield
            t = ts(GB, GB, 1.0, ALU.add, None, None, t)
            t = DV(lambda e: e.reciprocal(GB, GB), t)
            t = tt(DV, G3, GT[:, :, 4:8], rp(R_EDT, 4).unsqueeze(1).broadcast_to((P, 4, 4)), ALU.add)
            yield from softplus(GG, sa, sb_, sc_, t)
            t = stt(G3, G3, -1.0, ea4.unsqueeze(1).broadcast_to((P, 4, 4)), ALU.mult, ALU.mult, sp_t[0], t1)
            yield
            b, fr = psum.take()
            PE.quiet(lambda e: e.matmul(banks[b][:, 0:16], TRI, GG, start=True, stop=True), t, *fr)
            t = PE(lambda e: e.matmul(banks[b][:, 16:32], ONE, GG, start=True, stop=True))
            yield
            t1 = DV(lambda e: e.tensor_copy(GC, banks[b][:, 0:16]), t)
            t4 = tt(DV, EK, banks[b][:, 16:32], GC, ALU.subtract, t1)
            yield
            t2 = act(EG, GC, ACT.Exp, t1)
            t3 = act(EL, banks[b][:, 16:32], ACT.Exp, t4)
            psum.give(b, t3)
            t5 = act(EK, EK, ACT.Exp, t4)
            yield
            stt(NB, GB.rearrange("p m d -> p (m d)"), -1.0, EG, ALU.mult, ALU.mult, t2)

        beside(norms())
        beside(gates())
        gemm_t(xk, 8, w, 0, 512, put2(QA, 0.125), tx)
        gemm_t(xk, 8, w, 512, 512, put2(KA), tx)
        gemm(xm, 8, w, 1024, 512, put(lambda m: VA[:, m, :]))
        finish()
        AM = arena(18432, 512)
        ts(AM, ke(E_CM, 512), 0.0, ALU.is_equal, -BIG, ALU.mult, (s_ev, 16))
        PL.wait((s_ev, 16))
        fence()
        h3 = lambda x: x.rearrange("p (h d) -> p h d", d=P)
        hd = lambda x, h: x[:, h * P:(h + 1) * P]
        KD, QDT, Dm, DT, Am, AT, KT, QT = (XTt[:, 512 * i:512 * (i + 1)] for i in range(8))
        X, XX, QK, ST = WRt[:, 0:512], WRt[:, 512:1024], scr[7], scr[8]
        LT, Y, WT, VN = Dm, KT, QT, DT
        wr_i, wr_fr = rows.take()
        DV.wait(*wr_fr)
        GBf = GB.rearrange("p m d -> p (m d)")

        def per_head(fn, b, *toks):
            for h in range(4):
                t = PE(lambda e, h=h: e.matmul(hd(banks[b], h), *fn(h), start=True, stop=True), *toks)
            return t

        def bc(x, c):
            return x[:, 4 * c:4 * c + 4].unsqueeze(2).broadcast_to((P, 4, P))

        def delta():
            end = []
            for c in range(4):
                q, k, v = (QKV[:, c, 512 * i:512 * (i + 1)] for i in range(3))
                t_kd = tt(PL, h3(KD), h3(k), bc(EK, c), ALU.mult, *end)
                t_ub = tt(PL, h3(v), h3(v), bc(GBf, c), ALU.mult)
                bq, f1 = psum.take()
                bk, f2 = psum.take()
                br, f4 = psum.take()
                for h in range(4):
                    tr = PE(lambda e: e.matmul(hd(banks[br], h), GG[:, 4 * c + h:4 * c + h + 1].broadcast_to((P, P)),
                                               TRI, start=True, stop=True), *f4)
                for h in range(4):
                    tk = PE(lambda e: e.transpose(hd(banks[bk], h), hd(k, h), IDN), *f2)
                for h in range(4):
                    tq = PE(lambda e: e.transpose(hd(banks[bq], h), hd(q, h), IDN), *f1)
                yield
                t_kt = AC(lambda e: e.copy(KT, banks[bk][:, :]), tk, *end)
                psum.give(bk, t_kt)
                t_wb = tt(PL, h3(k), h3(k), bc(NB, c), ALU.mult, tk, t_kd)
                for h in range(4):
                    g = GC[:, 4 * c + h:4 * c + h + 1]
                    ts(hd(DT, h), hd(banks[br], h), g, ALU.subtract, 0.0, ALU.min, tr, *end)
                    t = ts(hd(Dm, h), hd(banks[br], h), g, ALU.subtract, 0.0, ALU.max)
                psum.give(br, t)
                t_qd = tt(DV, h3(q), h3(q), bc(EG, c), ALU.mult, tq)
                yield
                b1, f1 = psum.take()
                t_b1 = per_head(lambda h: (hd(KT, h), hd(KT, h)), b1, t_kt, *f1)
                t2 = act(Dm, Dm, ACT.Exp, t, scale=-1.0)
                t1 = act(DT, DT, ACT.Exp, t)
                t_dm = tt(PL, h3(Dm), h3(Dm), kc(K_LOW).unsqueeze(1).broadcast_to((P, 4, P)), ALU.mult, t2)
                t_dt = tt(PL, h3(DT), h3(DT), TRI.unsqueeze(1).broadcast_to((P, 4, P)), ALU.mult, t1)
                t_qt = AC(lambda e: e.copy(QT, banks[bq][:, :]), tq)
                psum.give(bq, t_qt)
                yield
                for h in range(4):
                    t_a = stt(hd(Am, h), hd(banks[b1], h), GB[:, c, h:h + 1], hd(Dm, h), ALU.mult, ALU.mult, t_b1, t_dm)
                psum.give(b1, t_a)
                bd, f3 = psum.take()
                for h in range(4):
                    td = PE(lambda e: e.transpose(hd(banks[bd], h), hd(q, h), IDN), t_qd, *f3)
                b2, f2 = psum.take()
                t_b2 = per_head(lambda h: (hd(KT, h), hd(QT, h)), b2, t_qt, *f2)
                yield
                t = stt(h3(X), h3(Am), -1.0, ke(E_M1).unsqueeze(1).broadcast_to((P, 4, P)), ALU.mult, ALU.mult, t_a)
                t_x = tt(DV, h3(X), h3(X), IDN.unsqueeze(1).broadcast_to((P, 4, P)), ALU.add, t)
                t_qdt = AC(lambda e: e.copy(QDT, banks[bd][:, :]), td)
                psum.give(bd, t_qdt)
                b3, f3 = psum.take()
                for h in range(4):
                    t = PE(lambda e: e.transpose(hd(banks[b3], h), hd(Am, h), IDN), t_a, *f3)
                t_at = AC(lambda e: e.copy(AT, banks[b3][:, :]), t)
                psum.give(b3, t_at)
                yield
                b4, f4 = psum.take()
                for h in range(4):
                    t = PE(lambda e: e.transpose(hd(banks[b4], h), hd(X, h), IDN), t_x, *f4)
                t_qk = tt(DV, QK, banks[b2][:, :], DT, ALU.mult, t_b2, t_dt)
                psum.give(b2, t_qk)
                t_xx = AC(lambda e: e.copy(XX, banks[b4][:, :]), t)
                psum.give(b4, t_xx)
                lvl = lambda n: ke(E_LV + (n - 1) * P).unsqueeze(1).broadcast_to((P, 4, P))
                t_use = t_a
                for n in range(1, 7):
                    t_lt = tt(PL, h3(LT), h3(AT), lvl(n), ALU.mult, t_at, t_use)
                    yield
                    b1, f1 = psum.take()
                    t = t_use = per_head(lambda h: (hd(LT, h), hd(X, h)), b1, t_lt, t_x, *f1)
                    t_y = AC(lambda e: e.copy(Y, banks[b1][:, :]), t)
                    psum.give(b1, t_y)
                    yield
                    b3, f3 = psum.take()
                    if n < 6:
                        b2, f2 = psum.take()
                        t_m = per_head(lambda h: (hd(XX, h), hd(Y, h)), b2, t_y, t_xx, *f2)
                    t_n = per_head(lambda h: (hd(Y, h), hd(XX, h)), b3, t_y, t_xx, *f3)
                    if n < 6:
                        t_x = tt(DV, X, X, banks[b2][:, :], ALU.subtract, t_m)
                        psum.give(b2, t_x)
                    t_xx = tt(DV, XX, XX, banks[b3][:, :], ALU.subtract, t_n)
                    psum.give(b3, t_xx)
                yield
                bw, f1 = psum.take()
                t = per_head(lambda h: (hd(k, h), hd(XX, h)), bw, t_xx, t_wb, *f1)
                t_wt = AC(lambda e: e.copy(WT, banks[bw][:, :]), t)
                psum.give(bw, t_wt)
                bv, f2 = psum.take()
                yield
                for h in range(4):
                    t = PE(lambda e: e.matmul(hd(banks[bv], h), hd(XX, h), hd(v, h), start=True, stop=(c == 0)),
                           t_xx, t_ub, *f2)
                    if c:
                        t = PE(lambda e: e.matmul(hd(banks[bv], h), hd(WT, h), hd(ST, h), start=False, stop=True),
                               t_wt, *end)
                t_vn = DV(lambda e: e.tensor_copy(VN, banks[bv][:, :]), t)
                psum.give(bv, t_vn)
                yield
                if c < 3:
                    bs, f4 = psum.take()
                    t_s = per_head(lambda h: (hd(KD, h), hd(VN, h)), bs, t_vn, t_kd, *f4)
                bo, f3 = psum.take()
                for h in range(4):
                    t_o = PE(lambda e: e.matmul(hd(banks[bo], h), hd(QK, h), hd(VN, h), start=True, stop=(c == 0)),
                             t_vn, t_qk, *f3)
                    if c:
                        t_o = PE(lambda e: e.matmul(hd(banks[bo], h), hd(QDT, h), hd(ST, h), start=False, stop=True),
                                 t_qdt)
                if c == 0:
                    t_s = DV(lambda e: e.tensor_copy(ST, banks[bs][:, :]), t_s)
                elif c < 3:
                    for h in range(4):
                        t = stt(hd(ST, h), hd(ST, h), EL[:, 4 * c + h:4 * c + h + 1], hd(banks[bs], h), ALU.mult,
                                ALU.add, t_s, t_o)
                    t_s = t
                if c < 3:
                    psum.give(bs, t_s)
                t = AC(lambda e: e.copy(OB[:, c, :], banks[bo][:, :]), t_o)
                psum.give(bo, t)
                end = [t, t_s, t_o]
                yield

        beside(delta())
        units = []
        for i in range(4):
            def done(bank, r, t, tr, i=i):
                return scale_heads(OA[:, i, :].rearrange("p (h d) -> p h d", d=64), bank, r, 8, 0, t, tr)
            for h in range(8):
                r0 = 64 * (h % 2)
                W = (i + 1) * P
                units.append(dict(i=i, q=[x[r0:r0 + 64, h // 2, i * P:(i + 1) * P] for x in QA],
                                  k=lambda W, r0=r0, h=h: [x[r0:r0 + 64, h // 2, 0:W] for x in KA],
                                  mask=AM[:, 512 - W:512], times=ke(E_CM + 512 - W, W),
                                  values=lambda kb, h=h: VA[:, kb, h * 64:(h + 1) * 64], slot=h,
                                  done=done if h == 7 else None))
        attention(units, DPACE, 7)
        finish()
        rows.give(wr_i, PE.now(), DV.now())
        fence()
        OS = sm(16)
        tprev = []
        for c in range(4):
            t = act(scr[0], OB[:, c, :], ACT.Square, *tprev)
            t = DV(lambda e, c=c: e.tensor_reduce(OS[:, c * 4:(c + 1) * 4], h3(scr[0]), AX, ALU.add), t)
            tprev = [t]
        t = inv_root(OS, OS, 1.0 / P, t)
        ready = []
        o_at, o_cols = halves(2048, 8)
        for c in range(4):
            t1 = tt(DV, h3(OB[:, c, :]), h3(OB[:, c, :]), bc(OS, c), ALU.mult, t)
            ready.append([tt(PL, OB[:, c, :], OB[:, c, :], ZB[:, c, :], ALU.mult, t1)])
        tx = turn(lambda m, f: (OB if f > 3 else OA)[:, m, f % 4 * P:(f % 4 + 1) * P], 8, o_at, ready,
                  lambda f: 1.0 if f < 4 else cp(C_HNORM))
        return product_out(o_cols, 8, a["even_w_out"][0], a["norm_w"][0, 3:4], 1.0, tuple(tx), scr, col)

    def odd(tx, col):
        w = a["odd_w_in"][0]
        Z = arena(0, 8192).rearrange("p (c d) -> p c d", c=4)
        XS = arena(8192, 8192).rearrange("p (c d) -> p c d", c=4)
        BT = arena(16384, 2048).rearrange("p (g s) -> p g s", s=S)
        CT = arena(18432, 2048).rearrange("p (g s) -> p g s", s=S)
        BK = SC[:, 2560:4608].rearrange("p (c d) -> p c d", c=4)
        small[0] = SM0
        DT = sm(128)
        AA = sm(128)
        xk = xs_at
        xm = x_cols
        fence()
        D3 = DT.rearrange("p (c h) -> p c h", c=4)
        A3 = AA.rearrange("p (c h) -> p c h", c=4)

        t_dt = []

        def use_dt(m, b, t):
            t = tt(DV, D3[:, m, :], banks[b][:, 0:32], rp(R_ODT, 32), ALU.add, t)
            psum.give(b, t)
            t_dt.append(t)
        s1, s2, s3, e32 = sm(128), sm(128), sm(128), sm(32)
        AC_, EA, ET, ED = s1, s2, s3, sm(128)

        def decay_rows():
            yield from softplus(DT, s1, s2, s3, t_dt[3])
            t = sp_t[0]
            t1 = act(e32, rp(R_OA, 32), ACT.Exp)
            yield
            t = stt(A3, D3, -1.0, e32.unsqueeze(1).broadcast_to((P, 4, 32)), ALU.mult, ALU.mult, t, t1)
            yield
            b, fr = psum.take()
            PE.quiet(lambda e: e.matmul(banks[b][:, 0:128], TRI, AA, start=True, stop=True), t, *fr)
            t = PE(lambda e: e.matmul(banks[b][:, 128:256], ONE, AA, start=True, stop=True))
            yield
            t1 = DV(lambda e: e.tensor_copy(AC_, banks[b][:, 0:128]), t)
            t4 = tt(DV, ED, banks[b][:, 128:256], AC_, ALU.subtract, t1)
            yield
            act(EA, AC_, ACT.Exp, t1)
            t3 = act(ET, banks[b][:, 128:256], ACT.Exp, t4)
            act(ED, ED, ACT.Exp, t4)
            psum.give(b, t4, t3)

        later = Later(2)

        def use(j, b, t):
            n, t = conv(b, t, C_OCONV + 4 * j, C_OBIAS + j)

            def go():
                if j < 16:
                    tp, te = turn_block(n, t, XS[:, :, j * P:(j + 1) * P])
                elif j < 20:
                    tp, te = turn_block(n, t, BK[:, :, (j - 16) * P:(j - 15) * P])
                    tp = PL(lambda e: e.tensor_copy(BT[:, j - 16, :], scr[n]), t, tp)
                else:
                    tp = PL(lambda e: e.tensor_copy(CT[:, j - 20, :], scr[n]), t)
                cbuf.give(n, tp)
            later.add(go)
        gemm_t(xk, 8, w, 2048, 3072, use, tx)
        later.flush()
        for q in range(4):
            if q == 1:
                gemm(xm, 8, w, 5120, 32, use_dt)
                beside(decay_rows())
            def use_z(m, b, t, q=q):
                t = act(Z[:, m, q * 512:(q + 1) * 512], banks[b][:, :], ACT.Silu, t)
                psum.give(b, t)
            gemm(xm, 8, w, q * 512, 512, use_z)
        finish()
        fence()
        piece = lambda k: Xf[:, k * 512:(k + 1) * 512]
        HS = Xf[:, 0:2048].rearrange("p (g d) -> p g d", g=4)
        xbuf = Slots([(piece(4), piece(5)), (piece(6), piece(7)), (piece(8), piece(9))])
        ybuf = Slots([piece(10), piece(11), piece(12)])
        mbuf = Slots([scr[0], scr[1], scr[2], scr[3]])
        CB = sm(384)
        cbm = Slots([CB[:, 0:128], CB[:, 128:256], CB[:, 256:384]])
        p8 = lambda x: x.rearrange("p (h d) -> p h d", d=64)
        h3 = lambda x: x.rearrange("p (h d) -> p h d", d=P)
        hs_t = {g: () for g in range(4)}

        def by_head(x, c, g):
            h8 = c * 32 + g * 8
            return x[:, h8:h8 + 8].unsqueeze(2).broadcast_to((P, 8, 64))

        def decays(u):
            c, g = u["c"], u["g"]
            h8 = c * 32 + g * 8
            (xd, xe), fx = u["x"], u["fx"] = xbuf.take()
            xs = XS[:, c, g * 512:(g + 1) * 512]
            u["t_xd"] = tt(PL, p8(xd), p8(xs), by_head(DT, c, g), ALU.mult, *fx)
            u["t_xe"] = tt(PL, p8(xe), p8(xd), by_head(ED, c, g), ALU.mult, u["t_xd"], *fx)
            b, fr = psum.take()
            t = PE(lambda e: e.matmul(banks[b][:, 0:P], BT[:, g, c * P:(c + 1) * P], CT[:, g, c * P:(c + 1) * P],
                                      start=True, stop=True), *fr)
            rb = []
            for hh in range(2):
                br, fr = psum.take()
                for x in range(4):
                    k = h8 + hh * 4 + x
                    tr = PE(lambda e: e.matmul(banks[br][:, x * P:(x + 1) * P], AA[:, k:k + 1].broadcast_to((P, P)), TRI,
                                               start=True, stop=True), *fr)
                rb.append((br, tr))
            cb, fc = cbm.take()
            t_cb = tt(DV, cb, banks[b][:, 0:P], TRI, ALU.mult, t, *fc)
            psum.give(b, t_cb)
            u["mt"] = []
            for hh in (1, 0):
                br, tr = rb[hh]
                mt, fm = mbuf.take()
                for x in range(4):
                    k = h8 + hh * 4 + x
                    dst, src, a_k = mt[:, x * P:(x + 1) * P], banks[br][:, x * P:(x + 1) * P], AC_[:, k:k + 1]
                    if hh:
                        t = act(dst, src, ACT.Relu, tr, *fm, bias=a_k, scale=-1.0)
                    else:
                        t = ts(dst, src, a_k, ALU.subtract, 0.0, ALU.min, tr, *fm)
                psum.give(br, t)
                t = act(mt, mt, ACT.Exp, t, scale=-1.0 if hh else 1.0)
                t = tt(DV, h3(mt), h3(mt), cb.unsqueeze(1).broadcast_to((P, 4, P)), ALU.mult, t, t_cb)
                u["mt"].append((hh, mt, t))
            cbm.give(cb, t)

        def outputs(u):
            c, g, (xd, xe) = u["c"], u["g"], u["x"]
            b0, f0 = psum.take()
            if c:
                b1, f1 = psum.take()
                t_off = PE(lambda e: e.matmul(banks[b1][:, :], CT[:, g, c * P:(c + 1) * P], HS[:, g, :], start=True,
                                              stop=True), *f1, *hs_t[g])
            if c < 3:
                b2, f2 = psum.take()
                t_st = PE(lambda e: e.matmul(banks[b2][:, :], BK[:, c, g * P:(g + 1) * P], xe, start=True, stop=True),
                          u["t_xe"], *f2)
            for hh, mt, tm in u["mt"]:
                for x in range(4):
                    hx = hh * 4 + x
                    t_y = PE(lambda e: e.matmul(banks[b0][:, hx * 64:(hx + 1) * 64], mt[:, x * P:(x + 1) * P],
                                                xd[:, hx * 64:(hx + 1) * 64], start=True, stop=True),
                             tm, u["t_xd"], *f0)
                mbuf.give(mt, t_y)
            xbuf.give(u["x"], t_y)
            y, fy = ybuf.take()
            hv = HS[:, g, :]
            if c < 3:
                if c:
                    t2 = tt(DV, p8(hv), p8(hv), by_head(ET, c, g), ALU.mult, t_off, *hs_t[g])
                    t2 = tt(DV, hv, banks[b2][:, :], hv, ALU.add, t_st, t2)
                else:
                    t2 = DV(lambda e: e.tensor_copy(hv, banks[b2][:, :]), t_st)
                psum.give(b2, t2)
                hs_t[g] = (t2,)
            if c:
                t = tt(DV, p8(y), p8(banks[b1][:, :]), by_head(EA, c, g), ALU.mult, t_off, *fy)
                psum.give(b1, t)
                t = tt(DV, y, banks[b0][:, :], y, ALU.add, t, t_y)
            else:
                t = AC(lambda e: e.copy(y, banks[b0][:, :]), t_y, *fy)
            psum.give(b0, t)
            xs = XS[:, c, g * 512:(g + 1) * 512]
            t1 = tt(PL, p8(xs), p8(xs), rp(R_DSK + g * 8, 8).unsqueeze(2).broadcast_to((P, 8, 64)), ALU.mult, u["t_xd"])
            t1 = tt(PL, y, y, xs, ALU.add, t, t1)
            zz = Z[:, c, g * 512:(g + 1) * 512]
            t1 = tt(PL, zz, zz, y, ALU.mult, t1)
            ybuf.give(y, t1)
            u["t_z"] = t1

        YS = sm(16)
        junk = Slots([piece(13), piece(14)])
        ready = []

        def squares(u):
            c, g = u["c"], u["g"]
            n, fr = junk.take()
            t = AC(lambda e: e.activation(n, Z[:, c, g * 512:(g + 1) * 512], ACT.Square,
                                          accum_out=YS[:, c * 4 + g:c * 4 + g + 1]), u["t_z"], *fr)
            junk.give(n, t)
            return t

        units = [dict(c=c, g=g) for c in range(4) for g in range(4)]
        for x in range(19):
            if x > 2:
                t_sq = squares(units[x - 3])
            if x > 16:
                continue
            if x < 16:
                decays(units[x])
            if x:
                outputs(units[x - 1])
        t = inv_root(YS, YS, 1.0 / 512, t_sq)
        for c in range(4):
            z4 = Z[:, c, :].rearrange("p (g d) -> p g d", g=4)
            ready.append([tt(DV, z4, z4, YS[:, c * 4:c * 4 + 4].unsqueeze(2).broadcast_to((P, 4, 512)), ALU.mult, t)])
        y_at, y_cols = halves(8192, 16)
        tx = turn(lambda m, f: Z[:, m, f * P:(f + 1) * P], 16, y_at, ready,
                  lambda f: cp(C_ONORM + f), (AC.now(),))
        return product_out(y_cols, 16, a["odd_w_out"][0], a["norm_w"][1, 3:4], 1.0,
                           tuple(tx), x_tmp, col)

    def mixer2(l, tx, col):
        w = a["w_in_2"][l]
        r0 = R_L + l * L_N
        PJ = arena(0, 4 * Q_N).rearrange("p (c d) -> p c d", c=4)
        PJr = ARr[:, 0:4 * Q_N].rearrange("p (c d) -> p c d", c=4)
        QT = arena(4 * Q_N, 8704).rearrange("p (f s) -> p f s", s=S)
        QTr = ARr[:, 4 * Q_N:4 * Q_N + 8704].rearrange("p (f s) -> p f s", s=S)
        SKL = ARr[:, 4 * Q_N + 8704:4 * Q_N + 9216].rearrange("p (c s) -> p c s", s=P)
        FQ, FK, DQ, DK, SQ, SK, IQ, IK = 0, 3, 6, 8, 10, 13, 14, 16
        small[0] = SM0
        xm = x_cols
        settle()
        wr = sm(64 + 64 + 32 + 32 + 64 + 64)
        wo = 0
        wv = {}
        for name, src, n, f in (("fq", L_FQ, 64, 0.125), ("fk", L_FK, 64, 1.0), ("dq", L_DQ, 32, 32.0 ** -0.5),
                                ("dk", L_DK, 32, 1.0), ("sq", L_SQ, 64, 0.125), ("sk", L_SK, 64, 1.0)):
            wv[name] = wr[:, wo:wo + n]
            t_wv = ts(wv[name], rp(r0 + src, n), f, ALU.mult, None, None)
            wo += n
        lam_init = 0.8 - 0.6 * float(np.exp(-0.3 * l))
        ld, lj = sm(4), sm(32)

        def weights():
            t = t_wv
            for k, (x, y) in enumerate(((L_LQ1, L_LK1), (L_LQ2, L_LK2))):
                t = DV(lambda e, k=k, x=x, y=y: e.tensor_tensor_reduce(lj, rp(r0 + x, 32), rp(r0 + y, 32), 1.0, 0.0,
                                                                       ALU.mult, ALU.add, ld[:, k:k + 1]), t)
            yield
            t = act(ld[:, 0:2], ld[:, 0:2], ACT.Exp, t)
            yield
            t = tt(DV, ld[:, 2:3], ld[:, 1:2], ld[:, 0:1], ALU.subtract, t)
            ts(ld[:, 2:3], ld[:, 2:3], -lam_init, ALU.add, None, None, t)

        NS = sm(140).rearrange("p (c h) -> p c h", c=4)
        FG = sm(24)
        F3 = FG.rearrange("p (c h) -> p c h", c=4)
        IW = sm(16)
        I3 = IW.rearrange("p (c h) -> p c h", c=4)
        s1, s2, s3 = sm(24), sm(24), sm(24)
        CG = sm(24)
        m8 = sm(24)
        CR = Xf[:, 4096:7168].rearrange("p (h s) -> p h s", s=S)
        DTMP = Xf[:, 7168:7680].rearrange("p (k s) -> p k s", k=2)
        t_end, t_cg, t_cr = [], [], []
        sqb = Slots([scr[3], scr[4]])
        T4 = [SC[:, 2560 + i * 256:2560 + (i + 1) * 256] for i in range(4)]
        KDS, KDI = (x.rearrange("p (c d) -> p c d", c=4) for x in (scr[7], scr[8]))
        got = {}
        qt = {}

        def rope(off, nh, dh, c, *toks):
            kr = K_R64 if dh == 64 else K_R32
            hf = dh // 8
            cs, sn = (kc(kr + y * 4 * hf + c * hf, hf).unsqueeze(1).broadcast_to((P, nh, hf)) for y in range(2))
            v = PJ[:, c, off:off + nh * dh].rearrange("p (h d) -> p h d", d=dh)
            x1, x2 = v[:, :, 0:hf], v[:, :, hf:2 * hf]
            tv = [x[:, 0:nh * hf].rearrange("p (h d) -> p h d", d=hf) for x in T4]
            t0 = DV.now()
            tt(DV, tv[0], x1, cs, ALU.mult, t0, *toks)
            tt(DV, tv[1], x2, sn, ALU.mult)
            tt(DV, tv[2], x2, cs, ALU.mult)
            t = tt(DV, tv[3], x1, sn, ALU.mult)
            tt(DV, x1, tv[0], tv[1], ALU.subtract, t)
            return tt(DV, x2, tv[2], tv[3], ALU.add)

        def turns(blocks, tok):
            for f, src in blocks:
                b, fr = psum.take()
                for m in range(4):
                    t = PE(lambda e: e.transpose(banks[b][:, m * P:(m + 1) * P], src(m), IDN), *tok, *fr)
                yield
                if f >= IQ:
                    qt[f] = evac(QT[:, f, :], banks[b][:, :], t)
                else:
                    t = hi(QTr[:, f, :], banks[b][:, :], t)
                    yield
                    qt[f] = DV(lambda e: e.tensor_tensor(low[f], banks[b][:, :].rearrange("p (c s) -> p c s", s=P),
                                                         QTr[:, f, :].bitcast(F32).rearrange("p (c s) -> p c s", s=P),
                                                         ALU.subtract), t)
                psum.give(b, qt[f])

        at = lambda k: (lambda m: PJ[:, m, k:k + P])
        low = {f + k: PJr[:, :, c0 + k * P:c0 + (k + 1) * P] for f, c0, n in (
            (FQ, Q_FQ, 3), (FK, Q_FK, 3), (DQ, Q_DQ, 4), (SQ, Q_SQ, 3)) for k in range(n)}
        low[SK] = SKL

        def part(c0, off, nh, dh, o, ws, roped, blocks):
            tk = got[c0]
            ns = NS[:, :, o:o + nh]
            for c in range(4):
                n, fr = sqb.take()
                v = n[:, 0:nh * dh]
                t = act(v, PJ[:, c, off:off + nh * dh], ACT.Square, tk[c], *fr)
                yield
                t = DV(lambda e: e.tensor_reduce(NS[:, c, o:o + nh], v.rearrange("p (h d) -> p h d", d=dh), AX, ALU.add), t)
                sqb.give(n, t)
            t = ts(ns, ns, 1.0 / dh, ALU.mult, EPS, ALU.add, t)
            yield
            t = act(ns, ns, ACT.Sqrt, t)
            yield
            t = DV(lambda e: e.reciprocal(ns, ns), t)
            tp = []
            for c in range(4):
                v = PJ[:, c, off:off + nh * dh].rearrange("p (h d) -> p h d", d=dh)
                t1 = tt(DV, v, v, NS[:, c, o:o + nh].unsqueeze(2).broadcast_to((P, nh, dh)), ALU.mult, t)
                yield
                h = 0
                for name, k in ws:
                    vv = v[:, h:h + k, :]
                    t2 = tt(PL, vv, vv, wv[name].unsqueeze(1).broadcast_to((P, k, dh)), ALU.mult, t1, t_wv)
                    h += k
                tp.append(t2)
            yield
            if roped:
                for c in range(4):
                    tp[c] = rope(off, nh, dh, c, tp[c])
                    if o == 28:
                        for k in (0, 64):
                            tp[c] = DV(lambda e: e.tensor_copy(KDS[:, c, k:k + 64], PJ[:, c, Q_SK:Q_SK + 64]), tp[c])
                    yield
            yield from turns(blocks, tp)

        def gates():
            t = tt(DV, F3, PJ[:, :, Q_FF:Q_FF + 6], rp(r0 + L_FB, 6).unsqueeze(1).broadcast_to((P, 4, 6)), ALU.add,
                   *got[768])
            t = ts(FG, FG, -1.0, ALU.mult, None, None, t)
            yield from softplus(FG, s1, s2, s3, t)
            t_f = ts(FG, FG, -1.0, ALU.mult, None, None, sp_t[0])
            yield
            b, fr = psum.take()
            for i in range(4):
                for j in range(i + 1):
                    t = PE(lambda e: e.matmul(banks[b][:, i * 6:i * 6 + 6], TRI if j == i else ONE,
                                              F3[:, j, :], start=(j == 0), stop=(j == i)), t_f, *fr)
            yield
            t_cg.append(DV(lambda e: e.tensor_copy(CG, banks[b][:, 0:24]), t))
            psum.give(b, t_cg[0])
            while not t_end:
                yield
            for h in range(6):
                b, fr = psum.take()
                for i in range(4):
                    for j in range(i + 1):
                        t = PE(lambda e: e.matmul(
                            banks[b][:, i * P:(i + 1) * P], F3[:, j, h:h + 1].broadcast_to((P, P)),
                            TRI if j == i else ONE, start=(j == 0), stop=(j == i)), t_f, *fr)
                yield
                t_cr.append(AC(lambda e: e.mul(CR[:, h, :], banks[b][:, :], -1.0), t, *t_end))
                psum.give(b, t_cr[h])

        b3 = lambda x: x.rearrange("p (c s) -> p c s", s=P)
        sel = {1: QT[:, IQ:IQ + 2, 0:P], 2: PJ[:, 0:3, Q_IQ:Q_IQ + P], 3: PJ[:, 0:4, Q_IQ + P:Q_IQ + 2 * P]}
        t_sel = {}

        def index():
            tp = []
            for c in range(4):
                t = rope(Q_IQ, 5, 64, c, got[Q_IQ][c])
                for k in (0, 64):
                    t = DV(lambda e: e.tensor_copy(KDI[:, c, k:k + 64], PJ[:, c, Q_IK:Q_IK + 64]), t)
                tp.append(t)
            t_iw = ts(I3, PJ[:, :, Q_IW:Q_IW + 4], 0.5, ALU.mult, None, None, *got[Q_IQ])
            yield
            yield from turns(((IQ, at(Q_IQ)), (IQ + 1, at(Q_IQ + P)), (IK, lambda m: KDI[:, m, :])), tp)
            rb = Slots([0, 1, 2])
            yield
            for i in (1, 2, 3):
                W = (i + 1) * P
                acc = sel[i]
                ta = [t_iw]
                for h in range(4):
                    rr = 64 * (h % 2)
                    b, fr = psum.take()
                    t = PE(lambda e: e.matmul(
                        banks[b][:, 0:W], QT[rr:rr + 64, IQ + h // 2, i * P:(i + 1) * P], QT[rr:rr + 64, IK, 0:W],
                        start=True, stop=True), qt[IQ], qt[IQ + 1], qt[IK], *fr)
                    n, fn = rb.take()
                    t = act(scr[n][:, 0:W], banks[b][:, 0:W], ACT.Relu, t, *fn, scale=0.125)
                    psum.give(b, t)
                    yield
                    if h == 0:
                        t = ts(acc, b3(scr[n][:, 0:W]), I3[:, i, 0:1], ALU.mult, None, None, t, *ta)
                    else:
                        t = stt(acc, b3(scr[n][:, 0:W]), I3[:, i, h:h + 1], acc, ALU.mult, ALU.add, t, *ta)
                    ta = [t]
                    rb.give(n, t)
                t_sel[i] = tt(DV, acc, acc, b3(kc(K_CAUS + 512 - W, W)), ALU.add, *ta)
            works["k"] = beside(best())

        def best():
            for k in range(16):
                for i in (1, 2, 3):
                    mv = m8[:, (i - 1) * 8:i * 8]
                    t_sel[i] = DV(lambda e: e.max(mv, sel[i]), t_sel[i])
                    yield
                for i in (1, 2, 3):
                    mv = m8[:, (i - 1) * 8:i * 8]
                    t_sel[i] = DV(lambda e: e.match_replace(sel[i], mv, sel[i], LOW), t_sel[i])
                    yield
            for i in (1, 2, 3):
                t_sel[i] = ts(sel[i], sel[i], -2e38, ALU.is_gt, -BIG, ALU.mult, t_sel[i])

        works = {}
        wk = beside(weights())
        for c0, n in ((Q_IQ, 324), (Q_SQ, 512), (Q_DQ, 512), (Q_FQ, 384), (Q_FK, 384), (Q_FV, 390), (Q_DV, 256)):
            def use(m, b, t):
                t = AC(lambda e: e.copy(PJ[:, m, c0:c0 + n], banks[b][:, 0:n]), t)
                psum.give(b, t)
                got.setdefault(c0, []).append(t)
            gemm(xm, 8, w, c0, n, use, tuple(tx))
            pace[0] = PACE
            if c0 == Q_IQ:
                works["i"] = beside(index())
            elif c0 == Q_SQ:
                works["s"] = beside(part(c0, Q_SQ, 7, 64, 28, (("sq", 6), ("sk", 1)), True, [(SQ + k, at(Q_SQ + k * P))
                                    for k in range(3)] + [(SK, lambda m: KDS[:, m, :])]))
            elif c0 == Q_DQ:
                works["d"] = beside(part(c0, Q_DQ, 16, 32, 12, (("dq", 8), ("dk", 8)), True,
                                         [(DQ + k, at(Q_DQ + k * P)) for k in range(4)]))
            elif c0 == Q_FQ:
                works["fq"] = beside(part(c0, Q_FQ, 6, 64, 0, (("fq", 6),), False, [(FQ + k, at(Q_FQ + k * P))
                                                                                  for k in range(3)]))
            elif c0 == Q_FK:
                works["fk"] = beside(part(c0, Q_FK, 6, 64, 6, (("fk", 6),), False, [(FK + k, at(Q_FK + k * P))
                                                                                  for k in range(3)]))
            elif c0 == Q_FV:
                works["g"] = beside(gates())
        t_end.append(PE.now())
        finish(wk, *(works[k] for k in ("i", "s", "d", "fq", "fk")))
        pace[0] = 1
        fence()
        O = XTt[:, :].rearrange("p (m d) -> p m d", m=4)

        def chosen():
            finish(works["k"])

        def gated():
            finish(works["g"])
        u_f, u_d, u_s = [], [], []
        mk = Slots([0, 1])
        fmv = [WRt[:, 0:512], WRt[:, 512:1024]]
        dtmp = [DTMP[:, k, :].rearrange("p (h d) -> p h d", d=64) for k in range(2)]
        Q3 = lambda f, rr, n, i: (QTr[rr:rr + n, f, i * P:(i + 1) * P], low[f][rr:rr + n, i, :])
        K3 = lambda f, rr, n: (lambda W: (QTr[rr:rr + n, f, 0:W], low[f][rr:rr + n, 0:W // P, :]))
        for i in (3, 2, 1, 0):
            W = (i + 1) * P
            caus = kc(K_CAUS + 512 - W, W)

            def done_f(bank, r, t, tr, i=i):
                return scale_heads(O[:, i, 0:384].rearrange("p (h d) -> p h d", d=64), bank, r, 6, 0, t, tr)

            def done_s(bank, r, t, tr, i=i):
                return scale_heads(O[:, i, 640:1024].rearrange("p (h d) -> p h d", d=64), bank, r, 6, 0, t, tr)

            def done_d(bank, r, t, tr, i=i):
                r2 = r.rearrange("p (h m) -> p h m", m=2)
                x = dtmp[i % 2]
                ov = O[:, i, 384:640].rearrange("p (h d) -> p h d", d=64)
                bv = bank[:, :].rearrange("p (h m d) -> p h m d", m=2, d=64)
                t1 = ts(r2[:, :, 1], r2[:, :, 1], ld[:, 2:3], ALU.mult, None, None, tr)
                t2 = tt(DV, ov, bv[:, :, 0, :], r2[:, :, 0].unsqueeze(2).broadcast_to((P, 4, 64)), ALU.mult, t, tr)
                t1 = tt(DV, x, bv[:, :, 1, :], r2[:, :, 1].unsqueeze(2).broadcast_to((P, 4, 64)), ALU.mult, t1, t)
                return tt(DV, ov, ov, x, ALU.add, t1, t2)

            for h in range(6):
                rr = 64 * (h % 2)

                def mask(h=h, i=i, W=W, caus=caus):
                    n, fr = mk.take()
                    v = fmv[n][:, 0:W]
                    t = stt(v, CR[:, h, 0:W], CG[:, i * 6 + h:i * 6 + h + 1], caus, ALU.add, ALU.add, t_cr[h], t_cg[0], *fr)
                    return fmv[n][:, 0:W], (t,)

                def free(t, i=i, h=h):
                    mk.give((6 * i + h) % 2, t)
                u_f.append(dict(i=i, start=gated if i == 3 and h == 0 else None, q=Q3(FQ + h // 2, rr, 64, i), k=K3(FK + h // 2, rr, 64), mask=mask,
                                  free=free, times=None,
                                  values=lambda kb, h=h: PJ[:, kb, Q_FV + h * 64:Q_FV + h * 64 + 64], slot=h,
                                  done=done_f if h == 5 else None))
            for x in range(8):
                rr = 32 * (x % 4)
                u_d.append(dict(i=i, q=Q3(DQ + x // 4, rr, 32, i), k=K3(DK + x // 4, rr, 32), mask=caus,
                                  times=None, values=lambda kb, x=x: PJ[:, kb, Q_DV + (x // 2) * 64:Q_DV + (x // 2) * 64 + 64],
                                  slot=x, done=done_d if x == 7 else None))
            for h in range(6):
                rr = 64 * (h % 2)
                u_s.append(dict(i=i, start=chosen if i == 3 and h == 0 else None, q=Q3(SQ + h // 2, rr, 64, i), k=K3(SK, rr, 64),
                                  mask=(lambda i=i: (sel[i], (t_sel[i],))) if i else caus, times=None,
                                  values=lambda kb: PJ[:, kb, Q_SV:Q_SV + 64], slot=h,
                                  done=done_s if h == 5 else None))
        attention(u_d[:16] + u_f[:12] + u_s[:12] + u_d[16:] + u_f[12:] + u_s[12:], 2)
        fence()
        NO = sm(16)
        tprev = []
        for c in range(4):
            t = act(scr[0][:, 0:256], O[:, c, 384:640], ACT.Square, *tprev)
            t = DV(lambda e, c=c: e.tensor_reduce(NO[:, c * 4:c * 4 + 4], scr[0][:, 0:256].rearrange("p (h d) -> p h d", d=64),
                                                  AX, ALU.add), t)
            tprev = [t]
        t = inv_root(NO, NO, 1.0 / 64, t, factor=1.0 - lam_init)
        ready = []
        for c in range(4):
            v = O[:, c, 384:640].rearrange("p (h d) -> p h d", d=64)
            t1 = tt(DV, v, v, NO[:, c * 4:c * 4 + 4].unsqueeze(2).broadcast_to((P, 4, 64)), ALU.mult, t)
            ready.append([tt(PL, v, v, rp(r0 + L_SUB, 64).unsqueeze(1).broadcast_to((P, 4, 64)), ALU.mult, t1)])
        o_at, o_cols = halves(0, 8)
        tx = turn(lambda m, f: O[:, m, f * P:(f + 1) * P], 8, o_at, ready)
        return product_out(o_cols, 8, a["w_out_2"][l], None, None, tuple(tx), x_tmp, col)

    SM0 = small[0]
    steps = []
    nw = a["norm_w"]
    for l in range(2):
        fw = [[a[n][l, x] for n in ("ffn_w_gate", "ffn_w_up", "ffn_w_down")] for x in range(2)]
        steps.append(lambda t, c, l=l, fw=fw: ffn(*fw[0], nw[l, 1:2], 0.5, t, c))
        steps.append(even if l == 0 else odd)
        steps.append(lambda t, c, l=l, fw=fw: ffn(*fw[1], nw[l, 5:6], 0.5, t, c))
    for l in range(2):
        steps.append(lambda t, c, l=l: mixer2(l, t, c))
        gu = a["w_gate_up_2"][l]
        steps.append(lambda t, c, l=l, gu=gu: ffn(gu[:, 0:FF], gu[:, FF:2 * FF], a["w_down_2"][l], None, None, t, c))
    steps = steps[:upto]
    t = junction(None, None, None, x_tmp, 0)
    for n, step in enumerate(steps):
        t = step(t, n + 1 if n + 1 < len(steps) else None)
    for m in range(4):
        SP.quiet(lambda e: e.dma_start(out[0, m * P:(m + 1) * P, :], H[:, m, :]).then_inc(s_out, 16), *t[m])
    SP.wait((s_out, 64))


def constants():
    p = np.arange(P)
    c = np.zeros((P, K_N), np.float32)
    c[:, K_ID:K_ID + P] = np.eye(P)
    c[:, K_TRI:K_TRI + P] = p[:, None] <= p[None, :]
    c[:, K_ONE:K_ONE + P] = 1
    c[:, K_LOW:K_LOW + P] = p[None, :] < p[:, None]

    def level(b):
        i, j = p[:, None], p[None, :]
        return ((i // (2 * b) == j // (2 * b)) & ((i // b) % 2 == 1) & ((j // b) % 2 == 0)).astype(np.float32)
    ce = np.zeros((P, E_N), np.float32)
    ce[:, E_M1:E_M1 + P] = level(1)
    for n in range(1, 7):
        ce[:, E_LV + (n - 1) * P:E_LV + n * P] = level(2 ** n).T
    delta = p[:, None] - (np.arange(512)[None, :] - 384)
    c[:, K_CAUS:K_CAUS + 512] = np.where(delta >= 0, 0.0, -BIG)
    times = ((delta >= 0) & (delta <= 128)).astype(np.float32) + ((delta >= 0) & (delta % 4 == 0)) \
        + ((delta >= 0) & (delta % 16 == 0))
    ce[:, E_CM:E_CM + 512] = times
    for k0, dh in ((K_R64, 64), (K_R32, 32)):
        rot = dh // 4
        inv = (np.float32(1.0) / np.power(np.float32(500000.0), np.arange(0, rot, 2, dtype=np.float32) / np.float32(rot))
               ).astype(np.float32)
        ang = np.arange(S, dtype=np.float32)[:, None] * inv[None, :]
        for k, f in ((0, np.cos), (1, np.sin)):
            v = f(ang).astype(np.float32).reshape(4, P, rot // 2).transpose(1, 0, 2).reshape(P, -1)
            c[:, k0 + k * v.shape[1]:k0 + (k + 1) * v.shape[1]] = v
    return c, ce


WHOLE = ["x", "norm_w", "ffn_w_gate", "ffn_w_up", "ffn_w_down", "even_w_in", "even_w_out", "odd_w_in", "odd_w_out",
         "w_in_2", "w_out_2", "w_gate_up_2", "w_down_2"]


def pack(inputs):
    v = {k: np.asarray(x) for k, x in inputs.items()}
    arrays = {k: np.ascontiguousarray(v[k]) for k in WHOLE}
    cols = []
    for x in (v["norm_w"][0, 0], v["norm_w"][0, 2], v["norm_w"][0, 4], v["norm_w"][1, 0], v["norm_w"][1, 2],
              v["norm_w"][1, 4], v["attn_norm_2"][0], v["ffn_norm_2"][0], v["attn_norm_2"][1], v["ffn_norm_2"][1]):
        cols.append(x.reshape(8, P).T)
    for x, n in ((v["even_conv_w"][0], 12), (v["odd_conv_w"][0], 24)):
        cols.append(x.reshape(4, n, P).transpose(2, 1, 0).reshape(P, -1))
    cols.append(v["odd_conv_b"][0].reshape(24, P).T)
    cols.append(v["odd_out_norm_w"][0].reshape(16, P).T)
    cols.append(v["even_head_norm_w"][0][:, None])
    arrays["colp"] = np.ascontiguousarray(np.concatenate(cols, axis=1))
    rows = [v["even_a_log"][0], v["even_dt_bias"][0], v["odd_a_log"][0], v["odd_dt_bias"][0], v["odd_d_skip"][0]]
    for l in range(2):
        rows += [v[n + "_2"][l] for n in ("fox_fb", "fox_qn", "fox_kn", "diff_qn", "diff_kn", "diff_subln", "dsa_qn",
                                          "dsa_kn", "diff_lq1", "diff_lk1", "diff_lq2", "diff_lk2")]
    arrays["rowp"] = np.ascontiguousarray(np.concatenate(rows)[None, :])
    arrays["consts"], arrays["consts_e"] = constants()
    return arrays


def program(nc, arrays, upto=99):
    a = {k: nc.dram_tensor("in_" + k, list(x.shape), F32, kind="ExternalInput").ap() for k, x in arrays.items()}
    out = nc.dram_tensor("out_y", [1, S, D], F32, kind="ExternalOutput").ap()
    build(nc, a, out, upto)


def kernel(**inputs):
    import concourse.bacc as bacc
    from concourse.bass_utils import run_bass_kernel_spmd

    nc = bacc.Bacc("TRN2", target_bir_lowering=False, num_devices=1)
    arrays = pack(inputs)
    program(nc, arrays)
    r = run_bass_kernel_spmd(nc, [{"in_" + k: x for k, x in arrays.items()}], core_ids=[0])
    return r.results[0]["out_y"]
```
